# Optimizing a Trainium2 kernel written in Bass

```python
import jax, jax.numpy as jnp
from jax import lax
import numpy as np

D_MODEL = 1024
BATCH = 1
SEQ = 2048
DEPTH = 1

EPS = 1e-6
HEAD_DIM = 64
GLA_HEADS = 4
GLA_DK = 48
GLA_DV = 96
GLA_WIDTH = GLA_HEADS * GLA_DV
GLA_GATE_RANK = 16
GLA_GATE_TEMP = 16.0
GLA_CHUNK = 64
LRU_WIDTH = 256
LRU_BLOCKS = 8
LRU_BLOCK = LRU_WIDTH // LRU_BLOCKS
LRU_C = 8.0
LRU_CONV = 4
SWA_HEADS = 6
SWA_WIDTH = SWA_HEADS * HEAD_DIM
DILATED_PATTERNS = ((128, 1), (512, 4), (2048, 16))
SWA_BLOCK = 128
ROPE_THETA = 500000.0
ROPE_DIM = HEAD_DIM // 4
MIX_WIDTH = GLA_WIDTH + LRU_WIDTH + SWA_WIDTH
FFN_DIM = 2816
FFN_CONV = 3
IN_SPLITS = (GLA_HEADS * GLA_DK, GLA_HEADS * GLA_DK, GLA_WIDTH, GLA_WIDTH, GLA_GATE_RANK,
             LRU_WIDTH, LRU_WIDTH, SWA_WIDTH, SWA_WIDTH, SWA_WIDTH)
IN_COLS = sum(IN_SPLITS)

kernel_name = 'hymba_style_gla_rglru_dilated_swa_trunk'

def rms_norm(x, g):
    xf = x.astype(jnp.float32)
    y = xf * lax.rsqrt(jnp.mean(xf * xf, axis=-1, keepdims=True) + EPS)
    return (y * g).astype(x.dtype)

def causal_dwconv(x, w, b):
    K = w.shape[0]
    S = x.shape[1]
    xp = jnp.pad(x, ((0, 0), (K - 1, 0), (0, 0)))
    y = b + xp[:, K - 1:K - 1 + S] * w[K - 1]
    for k in range(K - 1):
        y = y + xp[:, k:k + S] * w[k]
    return y

def rope_tables(S):
    inv = ROPE_THETA ** (-jnp.arange(0, ROPE_DIM, 2, dtype=jnp.float32) / ROPE_DIM)
    ang = jnp.arange(S, dtype=jnp.float32)[:, None] * inv[None, :]
    return jnp.cos(ang), jnp.sin(ang)

def partial_rope(x, cos, sin):
    xr, xpass = x[..., :ROPE_DIM], x[..., ROPE_DIM:]
    x1, x2 = xr[..., :ROPE_DIM // 2], xr[..., ROPE_DIM // 2:]
    c = cos[None, :, None, :]
    s = sin[None, :, None, :]
    rot = jnp.concatenate([x1 * c - x2 * s, x2 * c + x1 * s], axis=-1).astype(x.dtype)
    return jnp.concatenate([rot, xpass], axis=-1)

def gla_chunked(q, k, v, g):
    B, S, H, dk = q.shape
    dv = v.shape[-1]
    C = GLA_CHUNK
    n = S // C

    def to_chunks(t):
        return t.astype(jnp.float32).reshape(B, n, C, H, t.shape[-1]).transpose(1, 0, 3, 2, 4)

    qc = to_chunks(q) * (dk ** -0.5)
    kc, vc, gc = to_chunks(k), to_chunks(v), to_chunks(g)
    causal = jnp.tril(jnp.ones((C, C), dtype=bool))

    def step(state, inp):
        qb, kb, vb, gb = inp
        b = jnp.cumsum(gb, axis=2)
        o_inter = jnp.einsum('bhik,bhkv->bhiv', qb * jnp.exp(b), state)
        diff = b[:, :, :, None, :] - b[:, :, None, :, :]
        decay = jnp.exp(jnp.where(causal[:, :, None], diff, -jnp.inf))
        scores = jnp.einsum('bhik,bhjk,bhijk->bhij', qb, kb, decay)
        o_intra = jnp.einsum('bhij,bhjv->bhiv', scores, vb)
        b_last = b[:, :, -1]
        k_dec = kb * jnp.exp(b_last[:, :, None, :] - b)
        state = jnp.exp(b_last)[..., None] * state + jnp.einsum('bhjk,bhjv->bhkv', k_dec, vb)
        return state, o_inter + o_intra

    state0 = jnp.zeros((B, H, dk, dv), jnp.float32)
    _, out = lax.scan(step, state0, (qc, kc, vc, gc))
    return out.transpose(1, 0, 3, 2, 4).reshape(B, S, H, dv)

def rg_lru(x, w_a, b_a, w_x, b_x, lam):
    B, S, W = x.shape
    xf = x.astype(jnp.float32)
    xb = xf.reshape(B, S, LRU_BLOCKS, LRU_BLOCK)
    r = jax.nn.sigmoid(jnp.einsum('bsni,nij->bsnj', xb, w_a).reshape(B, S, W) + b_a)
    i = jax.nn.sigmoid(jnp.einsum('bsni,nij->bsnj', xb, w_x).reshape(B, S, W) + b_x)
    log_a = -LRU_C * r * jax.nn.softplus(-lam)
    a = jnp.exp(log_a)
    u = jnp.sqrt(-jnp.expm1(2.0 * log_a)) * (i * xf)

    def combine(c1, c2):
        a1, b1 = c1
        a2, b2 = c2
        return a1 * a2, a2 * b1 + b2

    _, h = lax.associative_scan(combine, (a, u), axis=1)
    return h.astype(x.dtype)

def banded_causal_attention(q, k, v, span):
    N, L, H, hd = q.shape
    nb = -(-L // SWA_BLOCK)
    Lp = nb * SWA_BLOCK
    pad = ((0, 0), (0, Lp - L), (0, 0), (0, 0))
    q, k, v = (jnp.pad(t, pad) for t in (q, k, v))
    qb = q.reshape(N, nb, SWA_BLOCK, H, hd)

    def with_prev(t):
        tb = t.reshape(N, nb, SWA_BLOCK, H, hd)
        prev = jnp.pad(tb, ((0, 0), (1, 0), (0, 0), (0, 0), (0, 0)))[:, :-1]
        return jnp.concatenate([prev, tb], axis=2)

    kb, vb = with_prev(k), with_prev(v)
    s = jnp.einsum('nbqhd,nbkhd->nbhqk', qb, kb).astype(jnp.float32) * (hd ** -0.5)
    qi = jnp.arange(SWA_BLOCK)[:, None]
    kj = jnp.arange(2 * SWA_BLOCK)[None, :]
    dist = qi + SWA_BLOCK - kj
    blk = jnp.arange(nb)[:, None, None]
    valid = (dist >= 0) & (dist <= span) & (blk * SWA_BLOCK + kj - SWA_BLOCK >= 0)
    s = jnp.where(valid[None, :, None], s, -jnp.inf)
    m = jnp.max(s, axis=-1, keepdims=True)
    p = jnp.exp(s - m)
    denom = jnp.sum(p, axis=-1, keepdims=True)
    o = jnp.einsum('nbhqk,nbkhd->nbqhd', p / denom, vb.astype(jnp.float32))
    lse = (m + jnp.log(denom))[..., 0].transpose(0, 1, 3, 2)
    return o.reshape(N, Lp, H, hd)[:, :L], lse.reshape(N, Lp, H)[:, :L]

def dilated_attention(q, k, v):
    B, S, H, hd = q.shape
    outs, lses = [], []
    for window, dil in DILATED_PATTERNS:
        L = S // dil

        def to_sub(t):
            return t.reshape(B, L, dil, H, hd).transpose(0, 2, 1, 3, 4).reshape(B * dil, L, H, hd)

        o, lse = banded_causal_attention(to_sub(q), to_sub(k), to_sub(v), window // dil)
        outs.append(o.reshape(B, dil, L, H, hd).transpose(0, 2, 1, 3, 4).reshape(B, S, H, hd))
        lses.append(lse.reshape(B, dil, L, H).transpose(0, 2, 1, 3).reshape(B, S, H))
    w = jax.nn.softmax(jnp.stack(lses, axis=0), axis=0)
    return jnp.einsum('pbsh,pbshd->bshd', w, jnp.stack(outs, axis=0))

def _normal(k, shape, scale):
    return jax.random.normal(k, shape, jnp.float32) * scale

def _gain(k, shape):
    return 1.0 + 0.1 * jax.random.normal(k, shape, jnp.float32)

def setup_inputs(seed: int = 0) -> dict:
    key = jax.random.key(seed)
    ks = jax.random.split(key, 22)
    a0 = jax.random.uniform(ks[12], (DEPTH, LRU_WIDTH), jnp.float32, minval=0.9, maxval=0.999)
    a_base = a0 ** (1.0 / LRU_C)
    lru_lambda = jnp.log(a_base) - jnp.log1p(-a_base)
    return {
        'x': jax.random.normal(ks[0], (BATCH, SEQ, D_MODEL), jnp.float32),
        'norm_mix': _gain(ks[1], (DEPTH, D_MODEL)),
        'w_in': _normal(ks[2], (DEPTH, D_MODEL, IN_COLS), D_MODEL ** -0.5),
        'gla_w_gate': _normal(ks[3], (DEPTH, GLA_GATE_RANK, GLA_HEADS * GLA_DK), GLA_GATE_RANK ** -0.5),
        'gla_b_gate': _normal(ks[4], (DEPTH, GLA_HEADS * GLA_DK), 0.1),
        'gla_norm': _gain(ks[5], (DEPTH, GLA_DV)),
        'lru_conv_w': _normal(ks[6], (DEPTH, LRU_CONV, LRU_WIDTH), LRU_CONV ** -0.5),
        'lru_conv_b': _normal(ks[7], (DEPTH, LRU_WIDTH), 0.02),
        'lru_w_a': _normal(ks[8], (DEPTH, LRU_BLOCKS, LRU_BLOCK, LRU_BLOCK), LRU_BLOCK ** -0.5),
        'lru_b_a': _normal(ks[9], (DEPTH, LRU_WIDTH), 0.1),
        'lru_w_x': _normal(ks[10], (DEPTH, LRU_BLOCKS, LRU_BLOCK, LRU_BLOCK), LRU_BLOCK ** -0.5),
        'lru_b_x': _normal(ks[11], (DEPTH, LRU_WIDTH), 0.1),
        'lru_lambda': lru_lambda,
        'lru_norm': _gain(ks[13], (DEPTH, LRU_WIDTH)),
        'swa_norm': _gain(ks[14], (DEPTH, SWA_WIDTH)),
        'w_out': _normal(ks[15], (DEPTH, MIX_WIDTH, D_MODEL), MIX_WIDTH ** -0.5),
        'norm_ffn': _gain(ks[16], (DEPTH, D_MODEL)),
        'ffn_w_up': _normal(ks[17], (DEPTH, D_MODEL, 2 * FFN_DIM), D_MODEL ** -0.5),
        'ffn_conv_w': _normal(ks[18], (DEPTH, FFN_CONV, 2 * FFN_DIM), FFN_CONV ** -0.5),
        'ffn_conv_b': _normal(ks[19], (DEPTH, 2 * FFN_DIM), 0.02),
        'ffn_w_down': _normal(ks[20], (DEPTH, FFN_DIM, D_MODEL), FFN_DIM ** -0.5),
        'norm_final': _gain(ks[21], (D_MODEL,)),
    }

def reference(x, norm_mix, w_in, gla_w_gate, gla_b_gate, gla_norm, lru_conv_w, lru_conv_b,
              lru_w_a, lru_b_a, lru_w_x, lru_b_x, lru_lambda, lru_norm, swa_norm, w_out,
              norm_ffn, ffn_w_up, ffn_conv_w, ffn_conv_b, ffn_w_down, norm_final):
    B, S, _ = x.shape
    cos, sin = rope_tables(S)
    split_points = np.cumsum(IN_SPLITS)[:-1].tolist()
    for l in range(DEPTH):
        h = rms_norm(x, norm_mix[l])
        proj = h @ w_in[l]
        a_q, a_k, a_v, a_r, a_glr, b_gate, b_in, c_q, c_k, c_v = jnp.split(proj, split_points, axis=-1)

        g = jax.nn.log_sigmoid((a_glr @ gla_w_gate[l] + gla_b_gate[l]).astype(jnp.float32)) / GLA_GATE_TEMP
        o_a = gla_chunked(a_q.reshape(B, S, GLA_HEADS, GLA_DK), a_k.reshape(B, S, GLA_HEADS, GLA_DK),
                          a_v.reshape(B, S, GLA_HEADS, GLA_DV), g.reshape(B, S, GLA_HEADS, GLA_DK))
        o_a = rms_norm(o_a.astype(x.dtype), gla_norm[l]).reshape(B, S, GLA_WIDTH) * jax.nn.silu(a_r)

        u = causal_dwconv(b_in, lru_conv_w[l], lru_conv_b[l])
        h_rec = rg_lru(u, lru_w_a[l], lru_b_a[l], lru_w_x[l], lru_b_x[l], lru_lambda[l])
        o_b = rms_norm(h_rec * jax.nn.gelu(b_gate), lru_norm[l])

        q = partial_rope(c_q.reshape(B, S, SWA_HEADS, HEAD_DIM), cos, sin)
        k = partial_rope(c_k.reshape(B, S, SWA_HEADS, HEAD_DIM), cos, sin)
        o_c = dilated_attention(q, k, c_v.reshape(B, S, SWA_HEADS, HEAD_DIM))
        o_c = rms_norm(o_c.astype(x.dtype).reshape(B, S, SWA_WIDTH), swa_norm[l])

        x = x + jnp.concatenate([o_a, o_b, o_c], axis=-1) @ w_out[l]

        h = rms_norm(x, norm_ffn[l])
        up = causal_dwconv(h @ ffn_w_up[l], ffn_conv_w[l], ffn_conv_b[l])
        u_val, u_gate = jnp.split(up, 2, axis=-1)
        x = x + (jax.nn.gelu(u_gate) * u_val) @ ffn_w_down[l]
    return rms_norm(x, norm_final)


_drawn_inputs = setup_inputs


def setup_inputs(seed=0):
    import zlib

    import numpy as np

    out = dict(_drawn_inputs(seed))
    spreads = {}
    factors = {'gla_b_gate': 4.209, 'lru_b_a': 5.98, 'lru_b_x': 4.622, 'ffn_conv_b': 4.633}
    for name, (base, spread) in spreads.items():
        noise = np.random.default_rng([zlib.crc32(name.encode()), seed]).standard_normal(out[name].shape)
        drawn = base * np.exp(spread * noise) if base else spread * noise
        out[name] = __import__('jax').numpy.asarray(drawn.astype(out[name].dtype))
    for name, factor in factors.items():
        out[name] = (out[name] * factor).astype(out[name].dtype)
    return out
```

```python
from contextlib import ExitStack

import numpy as np

import concourse.bass as bass
from concourse import mybir

F32 = mybir.dt.float32
F32R = mybir.dt.float32r
BF16 = mybir.dt.bfloat16
ALU = mybir.AluOpType
ACT = mybir.ActivationFunctionType
AX = mybir.AxisListType

P = 128
D = 1024
KT = D // P
S = 2048
NB = 512
BLOCKS = S // NB
EPS = 1e-6

T_AQ, T_AK, T_AV, T_AR, T_BG, T_BI, T_CQ, T_CK, T_CV = 0, 2, 4, 7, 10, 12, 14, 17, 20
TILES = 23
GLR_ROW = 112


def free_semaphores(nc, used):
    nc.clear_and_free_semaphores(used)
    nc.all_engine_barrier()


def product(pe, out, w_hi, w_lo, x_hi, x_lo):
    n = len(w_hi)
    for k in range(n):
        pe.matmul(out, w_hi[k], x_hi[k], start=(k == 0), stop=False)
        pe.matmul(out, w_hi[k], x_lo[k], start=False, stop=False)
        last = pe.matmul(out, w_lo[k], x_hi[k], start=False, stop=(k == n - 1))
    return last


def input_projection(nc, x_t, norm_gain, w_tiles, proj_t):
    with ExitStack() as ctx:
        used = []
        ctx.callback(free_semaphores, nc, used)

        def sb(name, shape, dt=F32):
            return ctx.enter_context(nc.sbuf_tensor("ip_" + name, shape, dt))

        def sem(name):
            used.append(nc.alloc_semaphore("ip_" + name))
            return used[-1]

        x_in = sb("x_in", [P, 2, KT, NB])
        squares = sb("squares", [P, 2, NB])
        h_hi = sb("h_hi", [P, KT, S], F32R)
        h_lo = sb("h_lo", [P, KT, S], F32R)
        w_raw = sb("w_raw", [P, KT, P])
        w_hi = sb("w_hi", [P, 2, KT, P], F32R)
        w_lo = sb("w_lo", [P, 2, KT, P], F32R)
        staged = sb("staged", [P, 2, S])
        rstd = sb("rstd", [P, NB])
        h_raw = sb("h_raw", [P, 2, NB])
        gain = sb("gain", [P, KT])
        ones = sb("ones", [P, P])
        eps = sb("eps", [P, 1])
        banks = [ctx.enter_context(nc.psum_tensor(f"ip_bank{i}", [P, NB], F32)) for i in range(8)]

        gain_in = sem("gain_in")
        x_loaded = [sem(f"x_loaded{i}") for i in range(2)]
        x_used = sem("x_used")
        consts_ready = sem("consts_ready")
        square_ready = sem("square_ready")
        square_used = sem("square_used")
        sum_done = sem("sum_done")
        std_ready = sem("std_ready")
        rstd_ready = sem("rstd_ready")
        h_raw_ready = sem("h_raw_ready")
        h_hi_ready = sem("h_hi_ready")
        h_ready = sem("h_ready")
        w_loaded = sem("w_loaded")
        w_hi_ready = sem("w_hi_ready")
        w_ready = sem("w_ready")
        w_free = sem("w_free")
        product_done = sem("product_done")
        bank_free = sem("bank_free")
        stored = [sem(f"stored{i}") for i in range(2)]

        block = ctx.enter_context(nc.Block())

        @block.sync
        def _(sp):
            for p in range(2):
                sp.sem_inc(stored[p], 16)
            sp.dma_start(gain[:, :], norm_gain).then_inc(gain_in, 16)

            def load_weights(t):
                sp.wait_ge(w_ready, t)
                sp.dma_start(w_raw[:, :, :], w_tiles[t]).then_inc(w_loaded, 16)

            for b in range(BLOCKS):
                if b >= 2:
                    sp.wait_ge(x_used, KT * (b - 1))
                sp.dma_start(x_in[:, b % 2, :, :], x_t[:, :, b * NB:(b + 1) * NB]).then_inc(x_loaded[b % 2], 16)
                if b == 0:
                    sp.dma_start(w_raw[:, :, :], w_tiles[0]).then_inc(w_loaded, 16)

            def store(t, p):
                sp.wait_ge(bank_free, 8 + BLOCKS * (t + 1))
                sp.dma_start(proj_t[t], staged[:, p, :]).then_inc(stored[p], 16)

            load_weights(1)
            store(0, 0)
            with sp.Fori(0, (TILES - 1) // 2 - 1) as i:
                for j in range(2):
                    load_weights(2 * i + (2 + j))
                    store(2 * i + (1 + j), (1 + j) % 2)
            load_weights(TILES - 1)
            store(TILES - 2, (TILES - 2) % 2)
            store(TILES - 1, (TILES - 1) % 2)
            sp.wait_ge(stored[0], 16 + 16 * ((TILES + 1) // 2))
            sp.wait_ge(stored[1], 16 + 16 * (TILES // 2))

        @block.scalar
        def _(act):
            act.sem_inc(bank_free, 8)

            def square(b):
                act.wait_ge(x_loaded[b % 2], 16 * (b // 2 + 1))
                for k in range(KT):
                    n = KT * b + k
                    if n >= 2:
                        act.wait_ge(square_used, n - 1)
                    act.activation(squares[:, n % 2, :], x_in[:, b % 2, k, :], ACT.Square).then_inc(square_ready, 1)

            square(0)
            act.wait_ge(consts_ready, 2)
            for b in range(BLOCKS):
                if b + 1 < BLOCKS:
                    square(b + 1)
                act.wait_ge(sum_done, b + 1)
                if b:
                    act.wait_ge(h_ready, b)
                act.activation(rstd[:, :], banks[4 + b][:, :], ACT.Sqrt, bias=eps[:, :], scale=1.0 / D).then_inc(std_ready, 1)
                for k in range(KT):
                    n = KT * b + k
                    act.wait_ge(h_raw_ready, n + 1)
                    act.activation(h_hi[:, k, b * NB:(b + 1) * NB], h_raw[:, n % 2, :], ACT.Copy).then_inc(h_hi_ready, 1)

            def drain(t, p, use):
                act.wait_ge(stored[p], 16 * (use + 1))
                for b in range(BLOCKS):
                    act.wait_ge(product_done, BLOCKS * t + (b + 1))
                    act.activation(staged[:, p, b * NB:(b + 1) * NB], banks[4 * p + b][:, :], ACT.Copy).then_inc(bank_free, 1)

            drain(0, 0, 0)
            with act.Fori(0, (TILES - 1) // 2) as i:
                drain(2 * i + 1, 1, i)
                drain(2 * i + 2, 0, i + 1)

        @block.vector
        def _(dve):
            dve.memset(ones[:, :], 1.0).then_inc(consts_ready, 1)
            dve.memset(eps[:, :], EPS).then_inc(consts_ready, 1)

            def split_weights(t, p):
                dve.wait_ge(w_loaded, 16 * (t + 1))
                dve.wait_ge(w_free, t + 1)
                dve.tensor_copy(w_hi[:, p, :, :], w_raw[:, :, :]).then_inc(w_hi_ready, 1)
                dve.wait_ge(w_hi_ready, t + 1)
                dve.tensor_tensor(w_lo[:, p, :, :], w_raw[:, :, :], w_hi[:, p, :, :].bitcast(F32),
                                  ALU.subtract).then_inc(w_ready, 1)

            split_weights(0, 0)
            dve.wait_ge(gain_in, 16)
            for b in range(BLOCKS):
                dve.wait_ge(std_ready, b + 1)
                dve.reciprocal(rstd[:, :], rstd[:, :]).then_inc(rstd_ready, 1)
                dve.wait_ge(rstd_ready, b + 1)

                def normalise(k):
                    n = KT * b + k
                    if n >= 2:
                        dve.wait_ge(x_used, n - 1)
                    dve.scalar_tensor_tensor(out=h_raw[:, n % 2, :], in0=x_in[:, b % 2, k, :], scalar=gain[:, k:k + 1],
                                             in1=rstd[:, :], op0=ALU.mult, op1=ALU.mult).then_inc(h_raw_ready, 1)

                def low_part(k):
                    n = KT * b + k
                    dve.wait_ge(h_hi_ready, n + 1)
                    cols = slice(b * NB, (b + 1) * NB)
                    low = dve.tensor_tensor(h_lo[:, k, cols], h_raw[:, n % 2, :], h_hi[:, k, cols].bitcast(F32), ALU.subtract)
                    low.then_inc(x_used, 1)
                    if k == KT - 1:
                        dve.wait_ge(x_used, KT * (b + 1))
                        dve.sem_inc(h_ready, 1)

                normalise(0)
                for k in range(1, KT):
                    normalise(k)
                    low_part(k - 1)
                low_part(KT - 1)
                if b == 1:
                    split_weights(1, 1)
            with dve.Fori(0, (TILES - 1) // 2 - 1) as i:
                split_weights(2 * i + 2, 0)
                split_weights(2 * i + 3, 1)
            split_weights(TILES - 1, 0)

        @block.tensor
        def _(pe):
            pe.sem_inc(w_free, 2)
            pe.wait_ge(consts_ready, 2)

            def sum_squares(b):
                for k in range(KT):
                    n = KT * b + k
                    pe.wait_ge(square_ready, n + 1)
                    pe.matmul(banks[4 + b][:, :], ones[:, :], squares[:, n % 2, :], start=(k == 0),
                              stop=(k == KT - 1)).then_inc(square_used, 1)
                pe.wait_ge(square_used, KT * (b + 1))
                pe.sem_inc(sum_done, 1)

            def project(t, p, b):
                cols = slice(b * NB, (b + 1) * NB)
                pe.wait_ge(bank_free, BLOCKS * t + (b + 1))
                product(pe, banks[4 * p + b][:, :],
                        [w_hi[:, p, k, :] for k in range(KT)], [w_lo[:, p, k, :] for k in range(KT)],
                        [h_hi[:, k, cols] for k in range(KT)], [h_lo[:, k, cols] for k in range(KT)]
                        ).then_inc(product_done, 1)

            def tile(t, p):
                pe.wait_ge(w_ready, t + 1)
                for b in range(BLOCKS):
                    project(t, p, b)
                pe.wait_ge(product_done, BLOCKS * (t + 1))
                pe.sem_inc(w_free, 1)

            sum_squares(0)
            sum_squares(1)
            pe.wait_ge(w_ready, 1)
            for b in range(BLOCKS):
                pe.wait_ge(h_ready, b + 1)
                project(0, 0, b)
                if b + 2 < BLOCKS:
                    sum_squares(b + 2)
            pe.wait_ge(product_done, BLOCKS)
            pe.sem_inc(w_free, 1)
            pe.wait_ge(std_ready, BLOCKS)
            with pe.Fori(0, (TILES - 1) // 2) as i:
                tile(2 * i + 1, 1)
                tile(2 * i + 2, 0)
HEADS = 6
HD = 64
GROUPS = HEADS // 2
DILATIONS = (1, 4, 16)
SPAN = 128
PAIRED = 32
SINGLE = 16
OW = HD + 1
ROW = HEADS * (OW + 1)
NEG = HEADS * OW


def attention_blocks():
    for pat, dil in enumerate(DILATIONS):
        for r in range(dil):
            for b in range(S // dil // SPAN):
                yield pat, r, b


def dilated_attention(nc, proj_t, rope, rotate, masks, ident, ident_bf, head_scales, o_scratch):
    with ExitStack() as ctx:
        used = []
        ctx.callback(free_semaphores, nc, used)

        def sb(name, shape, dt=F32):
            return ctx.enter_context(nc.sbuf_tensor("at_" + name, shape, dt))

        def sem(name):
            used.append(nc.alloc_semaphore("at_" + name))
            return used[-1]

        qkv = sb("qkv", [P, 3, GROUPS, S])
        cos_sin = sb("cos_sin", [P, 2, S])
        rot_w = sb("rot_w", [P, P])
        mask = sb("mask", [P, PAIRED, 2 * SPAN], BF16)
        idf = sb("idf", [P, P])
        head_scale = sb("head_scale", [P, 2])
        idb = sb("idb", [P, P], BF16)
        rope_c = sb("rope_c", [P, 2, NB])
        rope_s = sb("rope_s", [P, 2, NB])
        q_s = sb("q_s", [P, 2, GROUPS, 2, SPAN])
        k_s = sb("k_s", [P, 2, GROUPS, 2 * SPAN])
        v_s = sb("v_s", [P, 2, GROUPS, SPAN])
        v_tok = sb("v_tok", [P, 2, HEADS, OW])
        probs = sb("probs", [P, GROUPS, 4 * SPAN])
        probs_t = sb("probs_t", [P, GROUPS, 4 * SPAN])
        o_sb = sb("o_sb", [P, 2, ROW])

        def bank(name):
            return ctx.enter_context(nc.psum_tensor("at_" + name, [P, NB], F32))

        s_bank = [bank(f"s{i}") for i in range(GROUPS)]
        t_bank = [bank(f"t{i}") for i in range(2)]
        o_bank = [bank(f"o{i}") for i in range(2)]
        v_bank = bank("v")

        consts_in = sem("consts_in")
        q_in, k_in, v_in = sem("q_in"), sem("k_in"), sem("v_in")
        rotated = sem("rotated")
        times_cos = sem("times_cos")
        times_sin = sem("times_sin")
        roped = sem("roped")
        staged = sem("staged")
        scores_ready = sem("scores_ready")
        max_ready = sem("max_ready")
        probs_ready = sem("probs_ready")
        pt_done = sem("pt_done")
        pt_even = sem("pt_even")
        pt_odd = sem("pt_odd")
        vt_done = sem("vt_done")
        v_ready = sem("v_ready")
        o_done = sem("o_done")
        o_ready = sem("o_ready")
        stored = [sem(f"stored{i}") for i in range(2)]

        block = ctx.enter_context(nc.Block())
        blocks = list(attention_blocks())

        @block.sync
        def _(sp):
            sp.dma_start(rot_w[:, :], rotate).then_inc(consts_in, 16)
            sp.dma_start(head_scale[:, :], head_scales).then_inc(consts_in, 16)
            for a, (t, loaded) in enumerate([(T_CQ, q_in), (T_CK, k_in), (T_CV, v_in)]):
                sp.dma_start(qkv[:, a, :, :], proj_t[t:t + GROUPS].rearrange("g p s -> p g s")).then_inc(loaded, 16)
                if a == 0:
                    sp.dma_start(cos_sin[:, :, :], rope).then_inc(consts_in, 16)
            sp.dma_start(idf[:, :], ident).then_inc(consts_in, 16)
            sp.dma_start(idb[:, :], ident_bf).then_inc(consts_in, 16)
            sp.dma_start(mask[:, :, :], masks).then_inc(consts_in, 16)
            for j, (pat, r, b) in enumerate(blocks):
                dil = DILATIONS[pat]
                first = dil * SPAN * b + r
                rows = o_scratch[pat, first:first + dil * (SPAN - 1) + 1:dil, :]
                sp.wait_ge(o_ready, j + 1)
                sp.dma_start(rows, o_sb[:, j % 2, :]).then_inc(stored[j % 2], 16)
            for p in range(2):
                sp.wait_ge(stored[p], 16 * len(blocks) // 2)

        @block.gpsimd
        def _(pool):
            pool.wait_ge(consts_in, 16 * 6)
            pool.wait_ge(k_in, 16)
            pool.wait_ge(q_in, 16)
            with pool.Fori(0, BLOCKS) as i:
                for m in range(2 * GROUPS):
                    pool.wait_ge(roped, 2 * GROUPS * i + (m + 1))
                    at = bass.ds(i * NB, NB)
                    pool.tensor_tensor(rope_c[:, m % 2, :], qkv[:, m // GROUPS, m % GROUPS, at], cos_sin[:, 0, at],
                                       ALU.mult).then_inc(times_cos, 1)
            pool.wait_ge(roped, 2 + 2 * GROUPS * BLOCKS)
            pool.wait_ge(v_in, 16)
            for j, (pat, r, b) in enumerate(blocks):
                dil = DILATIONS[pat]
                first = dil * SPAN * b + r

                def tokens(a, start):
                    return qkv[:, a, :, start:start + dil * (SPAN - 1) + 1:dil]

                if j >= 2:
                    pool.wait_ge(scores_ready, GROUPS * (j - 1))
                    pool.wait_ge(vt_done, j - 1)
                for hh in range(2):
                    pool.tensor_scalar(q_s[:, j % 2, :, hh, :], tokens(0, first), head_scale[:, hh:hh + 1], None,
                                       ALU.mult).then_inc(staged, 1)
                if pat < 2:
                    prev = first - dil * SPAN if b else first
                    pool.tensor_copy(k_s[:, j % 2, :, 0:SPAN], tokens(1, prev)).then_inc(staged, 1)
                    pool.tensor_copy(k_s[:, j % 2, :, SPAN:2 * SPAN], tokens(1, first)).then_inc(staged, 1)
                else:
                    pool.tensor_copy(k_s[:, j % 2, :, 0:SPAN], tokens(1, first)).then_inc(staged, 1)
                pool.tensor_copy(v_s[:, j % 2, :, :], tokens(2, first)).then_inc(staged, 1)

        def staged_after(j, wide):
            return 5 * j + 5 if wide else 4 * j + (4 + PAIRED)

        @block.scalar
        def _(act):
            def neg_at(slot, hh, g):
                return o_sb[:, slot, NEG + 2 * g + hh:NEG + 2 * g + hh + 1]

            def exps(j, slot, wide, g, fresh):
                width = (2 if wide else 1) * SPAN
                act.wait_ge(max_ready, GROUPS * j + (g + 1))
                if not fresh:
                    act.wait_ge(pt_done, GROUPS * j + (g - 2))
                for hh in range(2):
                    ins = act.activation(probs[:, g, hh * width:(hh + 1) * width], s_bank[g][:, hh * width:(hh + 1) * width],
                                         ACT.Exp, bias=neg_at(slot, hh, g))
                ins.then_inc(probs_ready, 1)

            def turned_odd(j, slot, wide, fresh):
                n = (4 if wide else 2) * SPAN
                act.wait_ge(pt_done, GROUPS * j + 2)
                if not fresh:
                    act.wait_ge(o_done, j)
                act.activation(probs_t[:, 1, 0:n], t_bank[(slot + 1) % 2][:, 0:n], ACT.Copy).then_inc(pt_odd, 1)

            def body(j, slot, wide, last_fresh=False):
                exps(j, slot, wide, 0, False)
                exps(j, slot, wide, 1, False)
                turned_odd(j - 1, 1 - slot, wide, last_fresh)
                exps(j, slot, wide, 2, False)

            for g in range(GROUPS):
                exps(0, 0, True, g, True)
            body(1, 1, True, True)
            with act.Fori(0, PAIRED // 2 - 1) as i:
                body(2 * i + 2, 0, True)
                body(2 * i + 3, 1, True)
            turned_odd(PAIRED - 1, 1, True, False)
            for g in range(GROUPS):
                exps(PAIRED, 0, False, g, False)
            body(PAIRED + 1, 1, False)
            with act.Fori(0, SINGLE // 2 - 1) as i:
                body(2 * i + (PAIRED + 2), 0, False)
                body(2 * i + (PAIRED + 3), 1, False)
            turned_odd(PAIRED + SINGLE - 1, 1, False, False)

        @block.vector
        def _(dve):
            dve.sem_inc(roped, 2)
            dve.sem_inc(times_sin, 2)
            for slot in range(2):
                dve.memset(v_tok[:, slot, :, :], 1.0).then_inc(v_ready, 1)
            with dve.Fori(0, BLOCKS) as i:
                for m in range(2 * GROUPS):
                    n = 2 * GROUPS * i + m
                    at = bass.ds(i * NB, NB)
                    dve.wait_ge(rotated, n + 1)
                    dve.wait_ge(roped, n + 1)
                    dve.tensor_tensor(rope_s[:, m % 2, :], s_bank[m % 2][:, :], cos_sin[:, 1, at], ALU.mult).then_inc(times_sin, 1)
                    dve.wait_ge(times_sin, n + 3)
                    dve.wait_ge(times_cos, n + 1)
                    dve.tensor_tensor(qkv[:, m // GROUPS, m % GROUPS, at], rope_c[:, m % 2, :], rope_s[:, m % 2, :],
                                      ALU.add).then_inc(roped, 1)

            def maxima(j, slot, wide, g, fresh):
                width = (2 if wide else 1) * SPAN
                dve.wait_ge(scores_ready, GROUPS * j + (g + 1))
                dve.tensor_reduce(o_sb[:, slot, NEG + 2 * g:NEG + 2 * g + 2],
                                  s_bank[g][:, 0:2 * width].rearrange("p (h k) -> p h k", h=2), AX.X, ALU.max,
                                  negate=True).then_inc(max_ready, 1)

            def turned_even(j, slot, wide, g, fresh):
                n = (4 if wide else 2) * SPAN
                dve.wait_ge(pt_done, GROUPS * j + (g + 1))
                if not fresh:
                    dve.wait_ge(o_done, j)
                dve.tensor_copy(probs_t[:, g, 0:n], t_bank[(slot + g) % 2][:, 0:n]).then_inc(pt_even, 1)

            def take_sums(j, slot):
                dve.wait_ge(o_done, j + 1)
                dve.tensor_copy(o_sb[:, slot, 0:NEG], o_bank[slot][:, 0:NEG]).then_inc(o_ready, 1)

            def take_v(j, slot):
                dve.wait_ge(vt_done, j + 1)
                dve.tensor_copy(v_tok[:, slot, :, 0:HD], v_bank[:, 0:HEADS * HD].rearrange("p (h d) -> p h d", h=HEADS)
                                ).then_inc(v_ready, 1)

            def start(j, slot, wide, fresh, uses):
                for g in range(GROUPS):
                    if g == 0 and uses:
                        dve.wait_ge(stored[slot], uses)
                    maxima(j, slot, wide, g, True)
                take_v(j, slot)

            def body(j, slot, wide, uses, last_fresh=False):
                if uses is not None:
                    dve.wait_ge(stored[slot], uses)
                maxima(j, slot, wide, 0, True)
                turned_even(j - 1, 1 - slot, wide, 0, last_fresh)
                maxima(j, slot, wide, 1, True)
                maxima(j, slot, wide, 2, True)
                turned_even(j - 1, 1 - slot, wide, 2, last_fresh)
                take_sums(j - 1, 1 - slot)
                take_v(j, slot)

            def finish(j, slot, wide):
                turned_even(j, slot, wide, 0, False)
                turned_even(j, slot, wide, 2, False)
                take_sums(j, slot)

            dve.wait_ge(v_ready, 2)
            start(0, 0, True, True, None)
            body(1, 1, True, None, True)
            with dve.Fori(0, PAIRED // 2 - 1) as i:
                body(2 * i + 2, 0, True, 16 * (i + 1))
                body(2 * i + 3, 1, True, 16 * (i + 1))
            finish(PAIRED - 1, 1, True)
            start(PAIRED, 0, False, False, 16 * (PAIRED // 2))
            body(PAIRED + 1, 1, False, 16 * (PAIRED // 2))
            with dve.Fori(0, SINGLE // 2 - 1) as i:
                body(2 * i + (PAIRED + 2), 0, False, 16 * (i + (PAIRED // 2 + 1)))
                body(2 * i + (PAIRED + 3), 1, False, 16 * (i + (PAIRED // 2 + 1)))
            finish(PAIRED + SINGLE - 1, 1, False)

        @block.tensor
        def _(pe):
            pe.wait_ge(consts_in, 16 * 6)
            pe.wait_ge(q_in, 16)
            pe.wait_ge(k_in, 16)
            with pe.Fori(0, BLOCKS) as i:
                for m in range(2 * GROUPS):
                    pe.wait_ge(times_sin, 2 * GROUPS * i + (m + 1))
                    pe.matmul(s_bank[m % 2][:, :], rot_w[:, :], qkv[:, m // GROUPS, m % GROUPS, bass.ds(i * NB, NB)],
                              start=True, stop=True).then_inc(rotated, 1)
            pe.wait_ge(times_sin, 2 + 2 * GROUPS * BLOCKS)

            def turn_v(j, slot, wide):
                pe.wait_ge(staged, staged_after(j, wide))
                pe.wait_ge(v_ready, j + 2)
                for g in range(GROUPS):
                    ins = pe.transpose(v_bank[:, g * SPAN:(g + 1) * SPAN], v_s[:, slot, g, :], idf[:, :])
                ins.then_inc(vt_done, 1)

            def scores(j, slot, wide, g, fresh):
                width = (2 if wide else 1) * SPAN
                if not fresh:
                    pe.wait_ge(probs_ready, GROUPS * j + (g - 2))
                if wide:
                    at = mask[:, bass.ds(j, 1), :] if not isinstance(j, int) else mask[:, j:j + 1, :]
                else:
                    at = mask[:, 1:2, SPAN:2 * SPAN]
                for hh in range(2):
                    pe.matmul(s_bank[g][:, hh * width:(hh + 1) * width], idb[:, :], at.rearrange("p o k -> p (o k)"),
                              start=(hh == 0), stop=False, skip_group_check=True)
                for hh in range(2):
                    ins = pe.matmul(s_bank[g][:, hh * width:(hh + 1) * width], q_s[:, slot, g, hh, :],
                                    k_s[:, slot, g, 0:width], start=False, stop=(hh == 1), skip_group_check=True)
                ins.then_inc(scores_ready, 1)

            def turn_probs(j, slot, wide, g, fresh):
                pe.wait_ge(probs_ready, GROUPS * j + (g + 1))
                if g == 2:
                    pe.wait_ge(pt_even, 2 * j + 1)
                elif not fresh:
                    pe.wait_ge(pt_odd, j) if g == 0 else pe.wait_ge(pt_even, 2 * j)
                for c in range(4 if wide else 2):
                    ins = pe.transpose(t_bank[(slot + g) % 2][:, c * SPAN:(c + 1) * SPAN],
                                       probs[:, g, c * SPAN:(c + 1) * SPAN], idf[:, :])
                ins.then_inc(pt_done, 1)

            def sums(j, slot, wide, g):
                if g == 1:
                    pe.wait_ge(pt_odd, j + 1)
                else:
                    pe.wait_ge(pt_even, 2 * j + (1 if g == 0 else 2))
                if g == 0:
                    pe.wait_ge(v_ready, j + 3)
                for hh in range(2):
                    h = 2 * g + hh
                    out = o_bank[slot][:, h * OW:(h + 1) * OW]
                    if wide:
                        pe.matmul(out, probs_t[:, g, 2 * hh * SPAN:(2 * hh + 1) * SPAN], v_tok[:, 1 - slot, h, :], start=True, stop=False)
                        ins = pe.matmul(out, probs_t[:, g, (2 * hh + 1) * SPAN:(2 * hh + 2) * SPAN], v_tok[:, slot, h, :], start=False, stop=True)
                    else:
                        ins = pe.matmul(out, probs_t[:, g, hh * SPAN:(hh + 1) * SPAN], v_tok[:, slot, h, :], start=True, stop=True)
                if g == GROUPS - 1:
                    ins.then_inc(o_done, 1)

            def body(j, slot, wide, last_fresh=False):
                turn_v(j, slot, wide)
                for g in range(GROUPS):
                    scores(j, slot, wide, g, False)
                    turn_probs(j - 1, 1 - slot, wide, g, last_fresh)
                    if g:
                        sums(j - 1, 1 - slot, wide, g - 1)
                sums(j - 1, 1 - slot, wide, GROUPS - 1)

            def start(j, slot, wide, fresh):
                turn_v(j, slot, wide)
                for g in range(GROUPS):
                    scores(j, slot, wide, g, fresh)

            def finish(j, slot, wide):
                for g in range(GROUPS):
                    turn_probs(j, slot, wide, g, False)
                    if g:
                        sums(j, slot, wide, g - 1)
                sums(j, slot, wide, GROUPS - 1)

            start(0, 0, True, True)
            body(1, 1, True, True)
            with pe.Fori(0, PAIRED // 2 - 1) as i:
                body(2 * i + 2, 0, True)
                body(2 * i + 3, 1, True)
            finish(PAIRED - 1, 1, True)
            start(PAIRED, 0, False, False)
            body(PAIRED + 1, 1, False)
            with pe.Fori(0, SINGLE // 2 - 1) as i:
                body(2 * i + (PAIRED + 2), 0, False)
                body(2 * i + (PAIRED + 3), 1, False)
            finish(PAIRED + SINGLE - 1, 1, False)
GH = 4
DK = 48
DV = 96
GP = GH // 2
CH = 128
CHUNKS = NB // CH
RANK = 16
TEMP = 16.0
LIMIT = 80.0 * TEMP
AW = GH * DV


def gated_linear_attention(nc, proj_t, gate_w, gate_b, chunk_starts, causal, ident, norm_gain, mix_t):
    with ExitStack() as ctx:
        used = []
        ctx.callback(free_semaphores, nc, used)

        def sb(name, shape, dt=F32):
            return ctx.enter_context(nc.sbuf_tensor("gl_" + name, shape, dt))

        def sem(name):
            used.append(nc.alloc_semaphore("gl_" + name))
            return used[-1]

        q_in = sb("q_in", [P, 2, GP, NB])
        k_in = sb("k_in", [P, 2, GP, NB])
        v_in = sb("v_in", [P, 2, 3, NB])
        low_rank = sb("low_rank", [RANK, 2, NB])
        w_gate = sb("w_gate", [RANK, GP, P])
        b_gate = sb("b_gate", [P, GP])
        starts = sb("starts", [P, NB])
        keep = sb("keep", [P, 2, CH], mybir.dt.uint32)
        idf = sb("idf", [P, P])
        gain = sb("gain", [P, 3])
        eps = sb("eps", [P, 1])
        z = sb("z", [P, GP, NB])
        z_abs = sb("z_abs", [P, GP, NB])
        log_g = sb("log_g", [P, GP, NB])
        cum = sb("cum", [P, GP, NB])
        to_mid = sb("to_mid", [P, GP, NB])
        to_end = sb("to_end", [P, GP, NB])
        to_border = sb("to_border", [P, GP, NB])
        e_mid = sb("e_mid", [P, GP, NB])
        e_mid_inv = sb("e_mid_inv", [P, GP, NB])
        e_cum = sb("e_cum", [P, GP, NB])
        q_mid = sb("q_mid", [P, GP, NB])
        k_mid = sb("k_mid", [P, GP, NB])
        q_start = sb("q_start", [P, GP, NB])
        k_end = sb("k_end", [P, GP, NB])
        qk_border = sb("qk_border", [P, GP, NB])
        v_tok = sb("v_tok", [P, 2, AW])
        k_tok = sb("k_tok", [P, 2, GP, P])
        scores = sb("scores", [P, 2, GH, CH])
        state = sb("state", [P, 2, GP, DV])
        o_all = sb("o_all", [P, S // CH, AW])
        square = sb("square", [P, AW * 4])
        ss = sb("ss", [P, S // CH * GH])
        rstd = sb("rstd", [P, S // CH * GH])
        o_n = sb("o_n", [P, CHUNKS, AW])
        gate_r = sb("gate_r", [P, 3, S])

        def bank(name):
            return ctx.enter_context(nc.psum_tensor("gl_bank_" + name, [P, NB], F32))

        z_bank, v_bank, k_bank, st_bank = bank("z"), bank("v"), bank("k"), bank("st")
        s_bank = [bank(f"s{i}") for i in range(2)]
        o_bank = [bank(f"o{i}") for i in range(2)]

        consts_in = sem("consts_in")
        zeroed = sem("zeroed")
        loaded = [sem(f"loaded{i}") for i in range(2)]
        r_loaded = sem("r_loaded")
        z_ready = sem("z_ready")
        z_copied = sem("z_copied")
        z_abs_ready = sem("z_abs_ready")
        act_step = sem("act_step")
        dve_step = sem("dve_step")
        exps_ready = sem("exps_ready")
        factors_ready = sem("factors_ready")
        turned = sem("turned")
        tok_ready = sem("tok_ready")
        scores_done = sem("scores_done")
        scores_ready = sem("scores_ready")
        update_done = sem("update_done")
        state_ready = sem("state_ready")
        o_done = sem("o_done")
        o_ready = sem("o_ready")
        silu_ready = sem("silu_ready")
        gated_ready = sem("gated_ready")
        ss_ready = sem("ss_ready")
        rms_ready = sem("rms_ready")
        rstd_ready = sem("rstd_ready")
        o_n_ready = sem("o_n_ready")
        o_turned = sem("o_turned")
        out_ready = sem("out_ready")
        stored = sem("stored")

        block = ctx.enter_context(nc.Block())
        PRE = 8
        LOADS = 4

        def col(chunk, lo=0, hi=CH):
            return slice(chunk * CH + lo, chunk * CH + hi)

        @block.sync
        def _(sp):
            for dst, src in ((w_gate[:, :, :], gate_w), (b_gate[:, :], gate_b), (starts[:, :], chunk_starts),
                             (keep[:, :, :], causal), (idf[:, :], ident), (gain[:, :], norm_gain)):
                sp.dma_start(dst, src).then_inc(consts_in, 16)

            def load(n, p):
                at = bass.ds(n * NB, NB)
                sp.dma_start(q_in[:, p, :, :], proj_t[T_AQ:T_AQ + 2, :, at].rearrange("g p s -> p g s")).then_inc(loaded[p], 16)
                sp.dma_start(low_rank[:, p, :], proj_t[T_AQ, GLR_ROW:GLR_ROW + RANK, at]).then_inc(loaded[p], 16)
                sp.dma_start(k_in[:, p, :, :], proj_t[T_AK:T_AK + 2, :, at].rearrange("g p s -> p g s")).then_inc(loaded[p], 16)
                sp.dma_start(v_in[:, p, :, :], proj_t[T_AV:T_AV + 3, :, at].rearrange("g p s -> p g s")).then_inc(loaded[p], 16)

            load(0, 0)
            load(1, 1)
            sp.dma_start(gate_r[:, :, :], proj_t[T_AR:T_AR + 3].rearrange("g p s -> p g s")).then_inc(r_loaded, 16)
            for n in range(2, BLOCKS):
                sp.wait_ge(factors_ready, n - 1)
                sp.wait_ge(turned, CHUNKS * (n - 1))
                load(n, n % 2)
            for n in range(BLOCKS):
                sp.wait_ge(out_ready, 3 * (n + 1))
                sp.dma_start(mix_t[0:3, :, n * NB:(n + 1) * NB].rearrange("g p s -> p g s"), gate_r[:, :, n * NB:(n + 1) * NB]
                             ).then_inc(stored, 16)
            sp.wait_ge(stored, 16 * BLOCKS)

        @block.tensor
        def _(pe):
            pe.wait_ge(consts_in, 16 * 6)

            def gate(n, p):
                pe.wait_ge(loaded[p], 16 * LOADS * (n // 2 + 1))
                for m in range(GP):
                    u = GP * n + m
                    if u:
                        pe.wait_ge(z_copied, u)
                    pe.matmul(z_bank[:, :], w_gate[:, m, :], low_rank[:, p, :], start=True, stop=True).then_inc(z_ready, 1)

            def turn(c, chunk, p):
                if c:
                    pe.wait_ge(tok_ready, c)
                for g in range(3):
                    pe.transpose(v_bank[:, g * P:(g + 1) * P], v_in[:, p, g, col(chunk)], idf[:, :])
                for m in range(GP):
                    ins = pe.transpose(k_bank[:, m * P:(m + 1) * P], k_end[:, m, col(chunk)], idf[:, :])
                ins.then_inc(turned, 1)

            def inner(c, chunk):
                if c:
                    pe.wait_ge(scores_ready, c)
                for h in range(GH):
                    m, b = h // 2, h % 2
                    rows = slice(64 * b, 64 * b + DK)
                    at = m * CH
                    pe.matmul(s_bank[b][0:64, at:at + 64], k_mid[rows, m, col(chunk, 0, 64)], q_mid[rows, m, col(chunk, 0, 64)],
                              start=True, stop=True)
                    pe.matmul(s_bank[b][64:128, at + 64:at + 128], k_mid[rows, m, col(chunk, 64)], q_mid[rows, m, col(chunk, 64)],
                              start=True, stop=True)
                    ins = pe.matmul(s_bank[b][0:64, at + 64:at + 128], qk_border[rows, m, col(chunk, 0, 64)],
                                    qk_border[rows, m, col(chunk, 64)], start=True, stop=True)
                ins.then_inc(scores_done, 1)

            def update(c):
                pe.wait_ge(tok_ready, c + 1)
                if c:
                    pe.wait_ge(state_ready, c)
                for h in range(GH):
                    m, b = h // 2, h % 2
                    ins = pe.matmul(st_bank[64 * b:64 * b + 64, m * DV:(m + 1) * DV], k_tok[:, c % 2, m, 64 * b:64 * b + 64],
                                    v_tok[:, c % 2, h * DV:(h + 1) * DV], start=True, stop=True)
                ins.then_inc(update_done, 1)

            def output(c, chunk):
                pe.wait_ge(scores_ready, c + 1)
                if c:
                    pe.wait_ge(o_ready, c)
                    pe.wait_ge(state_ready, c)
                for m in range(GP):
                    for b in range(2):
                        h = 2 * m + b
                        out = o_bank[b][:, m * DV:(m + 1) * DV]
                        pe.matmul(out, scores[:, c % 2, h, :], v_tok[:, c % 2, h * DV:(h + 1) * DV], start=True, stop=False)
                        ins = pe.matmul(out, q_start[64 * b:64 * b + DK, m, col(chunk)], state[64 * b:64 * b + DK, c % 2, m, :],
                                        start=False, stop=True)
                ins.then_inc(o_done, 1)

            pe.wait_ge(zeroed, 3)
            gate(0, 0)
            for n in range(BLOCKS):
                pe.wait_ge(factors_ready, n + 1)
                for chunk in range(CHUNKS):
                    c = CHUNKS * n + chunk
                    turn(c, chunk, n % 2)
                    inner(c, chunk)
                    if chunk == 0 and n + 1 < BLOCKS:
                        gate(n + 1, (n + 1) % 2)
                    update(c)
                    output(c, chunk)

            for n in range(BLOCKS):
                for t in range(CHUNKS):
                    pe.wait_ge(o_n_ready, CHUNKS * n + t + 1)
                    for g in range(3):
                        if t == 0 and n:
                            pe.wait_ge(out_ready, 3 * (n - 1) + g + 1)
                        ins = pe.transpose([v_bank, k_bank, st_bank][g][:, t * CH:(t + 1) * CH], o_n[:, t, g * P:(g + 1) * P], idf[:, :])
                    ins.then_inc(o_turned, 1)

        @block.scalar
        def _(act):
            act.wait_ge(consts_in, 16 * 6)

            def gate(n):
                for m in range(GP):
                    u = GP * n + m
                    act.wait_ge(z_ready, u + 1)
                    if n:
                        act.wait_ge(dve_step, PRE * (n - 1) + 1)
                    act.activation(z[:, m, :], z_bank[:, :], ACT.Identity, bias=b_gate[:, m:m + 1]).then_inc(z_copied, 1)
                act.wait_ge(z_copied, GP * (n + 1))
                act.activation(z_abs[:, :, :], z[:, :, :], ACT.Abs).then_inc(z_abs_ready, 1)
                act.wait_ge(z_abs_ready, n + 1)
                act.activation(z_abs[:, :, :], z_abs[:, :, :], ACT.Exp, scale=-1.0).then_inc(act_step, 1)
                act.wait_ge(act_step, 2 * n + 1)
                act.activation(z_abs[:, :, :], z_abs[:, :, :], ACT.Ln, bias=1.0).then_inc(act_step, 1)

            def exps(n):
                if n:
                    act.wait_ge(state_ready, CHUNKS * n)
                    act.wait_ge(factors_ready, n)
                act.wait_ge(dve_step, PRE * n + 3)
                act.activation(e_cum[:, :, :], cum[:, :, :], ACT.Exp, scale=1.0 / TEMP).then_inc(exps_ready, 1)
                act.wait_ge(dve_step, PRE * n + 5)
                act.activation(e_mid[:, :, :], to_mid[:, :, :], ACT.Exp, scale=1.0 / TEMP).then_inc(exps_ready, 1)
                act.activation(e_mid_inv[:, :, :], to_mid[:, :, :], ACT.Exp, scale=-1.0 / TEMP).then_inc(exps_ready, 1)
                act.wait_ge(dve_step, PRE * n + 8)
                act.activation(to_end[:, :, :], to_end[:, :, :], ACT.Exp, scale=1.0 / TEMP).then_inc(exps_ready, 1)
                act.activation(to_border[:, :, :], to_border[:, :, :], ACT.Exp, scale=1.0 / TEMP).then_inc(exps_ready, 1)

            def tokens(c):
                act.wait_ge(turned, c + 1)
                if c >= 2:
                    act.wait_ge(o_done, c - 1)
                act.activation(v_tok[:, c % 2, :], v_bank[:, 0:AW], ACT.Copy)
                act.activation(k_tok[:, c % 2, :, :], k_bank[:, 0:GP * P].rearrange("p (m k) -> p m k", m=GP), ACT.Copy
                               ).then_inc(tok_ready, 1)

            def output(c):
                act.wait_ge(o_done, c + 1)
                for b in range(2):
                    ins = act.activation(o_all[:, c, :].rearrange("p (m b v) -> p m b v", m=GP, b=2)[:, :, b, :],
                                         o_bank[b][:, 0:GP * DV].rearrange("p (m v) -> p m v", m=GP), ACT.Copy)
                ins.then_inc(o_ready, 1)

            gate(0)
            exps(0)
            for n in range(BLOCKS):
                for chunk in range(CHUNKS):
                    c = CHUNKS * n + chunk
                    tokens(c)
                    if chunk == 0 and n + 1 < BLOCKS:
                        gate(n + 1)
                    output(c)
                if n + 1 < BLOCKS:
                    exps(n + 1)
            act.wait_ge(r_loaded, 16)
            for g in range(3):
                act.activation(gate_r[:, g, :], gate_r[:, g, :], ACT.Silu).then_inc(silu_ready, 1)
            act.wait_ge(ss_ready, S // CH // 4)
            act.activation(rstd[:, :], ss[:, :], ACT.Sqrt, bias=eps[:, :], scale=1.0 / DV).then_inc(rms_ready, 1)

        @block.vector
        def _(dve):
            dve.memset(scores[:, :, :, :], 0.0).then_inc(zeroed, 1)
            dve.memset(state[:, 0, :, :], 0.0).then_inc(zeroed, 1)
            dve.memset(eps[:, :], EPS).then_inc(zeroed, 1)
            dve.wait_ge(zeroed, 3)
            dve.wait_ge(consts_in, 16 * 6)

            def halves(x):
                return x[:, :, :].rearrange("p m (c j) -> p (m c) j", j=64)

            def chunked(x):
                return x[:, :, :].rearrange("p m (c j) -> p (m c) j", j=CH)

            def decays(n):
                dve.wait_ge(act_step, 2 * n + 2)
                if n:
                    dve.wait_ge(exps_ready, 5 * n)
                    dve.wait_ge(dve_step, PRE * n)
                dve.scalar_tensor_tensor(out=log_g[:, :, :], in0=z[:, :, :], scalar=0.0, in1=z_abs[:, :, :], op0=ALU.min,
                                         op1=ALU.subtract).then_inc(dve_step, 1)
                dve.wait_ge(dve_step, PRE * n + 1)
                for m in range(GP):
                    dve.tensor_tensor_scan(cum[:, m, :], starts[:, :], log_g[:, m, :], 0.0, ALU.mult, ALU.add).then_inc(dve_step, 1)
                dve.wait_ge(dve_step, PRE * n + 3)
                mid = halves(cum)[:, :, 31:32].to_broadcast([P, GP * NB // 64, 64])
                dve.tensor_tensor(halves(to_mid), halves(cum), mid, ALU.subtract).then_inc(dve_step, 1)
                dve.wait_ge(dve_step, PRE * n + 4)
                dve.tensor_scalar(to_mid[:, :, :], to_mid[:, :, :], LIMIT, -LIMIT, ALU.min, ALU.max).then_inc(dve_step, 1)
                if n:
                    dve.wait_ge(factors_ready, n)
                end = chunked(cum)[:, :, CH - 1:CH].to_broadcast([P, GP * CHUNKS, CH])
                dve.tensor_tensor(chunked(to_end), end, chunked(cum), ALU.subtract).then_inc(dve_step, 1)
                border = chunked(cum)[:, :, 63:64].to_broadcast([P, GP * CHUNKS, 64])
                dve.tensor_tensor(chunked(to_border)[:, :, 0:64], border, chunked(cum)[:, :, 0:64], ALU.subtract).then_inc(dve_step, 1)
                dve.tensor_tensor(chunked(to_border)[:, :, 64:CH], chunked(cum)[:, :, 64:CH], border, ALU.subtract).then_inc(dve_step, 1)

            def factors(n, p):
                if n:
                    dve.wait_ge(o_done, CHUNKS * n)
                dve.wait_ge(loaded[p], 16 * LOADS * (n // 2 + 1))
                q, k = q_in[:, p, :, :], k_in[:, p, :, :]
                scale = DK ** -0.5

                def scaled(out, x, e):
                    return dve.scalar_tensor_tensor(out=out, in0=x, scalar=scale, in1=e, op0=ALU.mult, op1=ALU.mult)

                dve.wait_ge(exps_ready, 5 * n + 1)
                scaled(q_start[:, :, :], q, e_cum[:, :, :])
                dve.wait_ge(exps_ready, 5 * n + 2)
                scaled(q_mid[:, :, :], q, e_mid[:, :, :])
                dve.wait_ge(exps_ready, 5 * n + 3)
                dve.tensor_tensor(k_mid[:, :, :], k, e_mid_inv[:, :, :], ALU.mult)
                dve.wait_ge(exps_ready, 5 * n + 4)
                dve.tensor_tensor(k_end[:, :, :], k, to_end[:, :, :], ALU.mult)
                dve.wait_ge(exps_ready, 5 * n + 5)
                kc = k.rearrange("p m (c j) -> p (m c) j", j=CH)
                qc = q.rearrange("p m (c j) -> p (m c) j", j=CH)
                dve.tensor_tensor(chunked(qk_border)[:, :, 0:64], kc[:, :, 0:64], chunked(to_border)[:, :, 0:64], ALU.mult)
                scaled(chunked(qk_border)[:, :, 64:CH], qc[:, :, 64:CH], chunked(to_border)[:, :, 64:CH]).then_inc(factors_ready, 1)

            def mask(c):
                dve.wait_ge(scores_done, c + 1)
                if c >= 2:
                    dve.wait_ge(o_done, c - 1)
                for b in range(2):
                    sc = scores[:, c % 2, :, :].rearrange("p (m b) i -> p m b i", b=2)[:, :, b, :]
                    ps = s_bank[b][:, 0:GP * CH].rearrange("p (m i) -> p m i", m=GP)
                    dve.copy_predicated(sc[0:64], keep[0:64, :, :], ps[0:64])
                    ins = dve.copy_predicated(sc[64:128, :, 64:CH], keep[64:128, :, 64:CH], ps[64:128, :, 64:CH])
                ins.then_inc(scores_ready, 1)

            def advance(c, chunk):
                dve.wait_ge(update_done, c + 1)
                if c:
                    dve.wait_ge(state_ready, c)
                    dve.wait_ge(o_done, c)
                for m in range(GP):
                    ins = dve.scalar_tensor_tensor(out=state[:, (c + 1) % 2, m, :], in0=state[:, c % 2, m, :],
                                                   scalar=e_cum[:, m, (chunk + 1) * CH - 1:(chunk + 1) * CH],
                                                   in1=st_bank[:, m * DV:(m + 1) * DV], op0=ALU.mult, op1=ALU.add)
                ins.then_inc(state_ready, 1)

            decays(0)
            factors(0, 0)
            for n in range(BLOCKS):
                for chunk in range(CHUNKS):
                    c = CHUNKS * n + chunk
                    mask(c)
                    advance(c, chunk)
                    if chunk == CHUNKS - 2 and n + 1 < BLOCKS:
                        decays(n + 1)
                if n + 1 < BLOCKS:
                    factors(n + 1, (n + 1) % 2)
            dve.wait_ge(silu_ready, 3)
            for g in range(3):
                dve.tensor_scalar(gate_r[:, g, :], gate_r[:, g, :], gain[:, g:g + 1], None, ALU.mult).then_inc(gated_ready, 1)
            for t in range(S // CH // 4):
                dve.wait_ge(o_ready, 4 * (t + 1))
                if t:
                    dve.wait_ge(ss_ready, t)
                o4 = o_all[:, 4 * t:4 * t + 4, :].rearrange("p c v -> p (c v)")
                dve.tensor_tensor(square[:, :], o4, o4, ALU.mult).then_inc(dve_step, 1)
                dve.wait_ge(dve_step, PRE * BLOCKS + t + 1)
                dve.tensor_reduce(ss[:, 4 * GH * t:4 * GH * (t + 1)], square[:, :].rearrange("p (h v) -> p h v", v=DV), AX.X,
                                  ALU.add).then_inc(ss_ready, 1)
            dve.wait_ge(rms_ready, 1)
            dve.reciprocal(rstd[:, :], rstd[:, :]).then_inc(rstd_ready, 1)
            dve.wait_ge(rstd_ready, 1)
            dve.wait_ge(gated_ready, 3)
            for n in range(BLOCKS):
                for t in range(CHUNKS):
                    c = CHUNKS * n + t
                    if n:
                        dve.wait_ge(o_turned, CHUNKS * (n - 1) + t + 1)
                    dve.tensor_tensor(o_n[:, t, :].rearrange("p (h v) -> p h v", v=DV), o_all[:, c, :].rearrange("p (h v) -> p h v", v=DV),
                                      rstd[:, GH * c:GH * (c + 1)].unsqueeze(2).to_broadcast([P, GH, DV]), ALU.mult).then_inc(o_n_ready, 1)
                dve.wait_ge(o_turned, CHUNKS * (n + 1))
                for g in range(3):
                    at = gate_r[:, g, n * NB:(n + 1) * NB]
                    dve.tensor_tensor(at, [v_bank, k_bank, st_bank][g][:, :], at, ALU.mult).then_inc(out_ready, 1)


LW = 256
LT = LW // P
LTAPS = 4
C_TAP, C_BIAS, C_BA, C_BX, C_LAM, C_NORM = 0, 4, 5, 6, 7, 8


def recurrent_branch(nc, proj_t, consts, gate_w, mix_t):
    with ExitStack() as ctx:
        used = []
        ctx.callback(free_semaphores, nc, used)

        def sb(name, shape, dt=F32):
            return ctx.enter_context(nc.sbuf_tensor("lr_" + name, shape, dt))

        def sem(name):
            used.append(nc.alloc_semaphore("lr_" + name))
            return used[-1]

        x_in = sb("x_in", [P, LT, LTAPS - 1 + S])
        gate = sb("gate", [P, LT, S])
        xc = sb("xc", [P, LT, S])
        r = sb("r", [P, LT, S])
        i_x = sb("i_x", [P, LT, S])
        root = sb("root", [P, LT, S])
        a2 = sb("a2", [P, LT, S])
        rstd = sb("rstd", [P, S])
        c = sb("c", [P, LT, C_NORM + 1])
        w = sb("w", [P, LT, 2, P])
        sp8 = sb("sp8", [P, LT, 4])
        ones = sb("ones", [P, P])
        eps = sb("eps", [P, 1])
        banks = [ctx.enter_context(nc.psum_tensor(f"lr_bank{i}", [P, NB], F32)) for i in range(8)]

        consts_in = sem("consts_in")
        x_loaded = sem("x_loaded")
        gate_loaded = sem("gate_loaded")
        zeroed = sem("zeroed")
        small = sem("small")
        small_act = sem("small_act")
        conv_step = sem("conv_step")
        gates_done = sem("gates_done")
        gates_ready = sem("gates_ready")
        tanh_ready = sem("tanh_ready")
        a_ready = sem("a_ready")
        a2_ready = sem("a2_ready")
        power_ready = sem("power_ready")
        root_ready = sem("root_ready")
        ix_ready = sem("ix_ready")
        u_ready = sem("u_ready")
        h_ready = sem("h_ready")
        gelu_ready = sem("gelu_ready")
        hg_ready = sem("hg_ready")
        sq_ready = sem("sq_ready")
        sums_done = sem("sums_done")
        std_ready = sem("std_ready")
        rstd_ready = sem("rstd_ready")
        out_ready = sem("out_ready")
        stored = sem("stored")

        block = ctx.enter_context(nc.Block())

        @block.sync
        def _(sp):
            sp.dma_start(c[:, :, :], consts).then_inc(consts_in, 16)
            sp.dma_start(w[:, :, :, :], gate_w).then_inc(consts_in, 16)
            sp.dma_start(x_in[:, :, LTAPS - 1:], proj_t[T_BI:T_BI + LT].rearrange("g p s -> p g s")).then_inc(x_loaded, 16)
            sp.dma_start(gate[:, :, :], proj_t[T_BG:T_BG + LT].rearrange("g p s -> p g s")).then_inc(gate_loaded, 16)
            for m in range(LT):
                sp.wait_ge(out_ready, m + 1)
                sp.dma_start(mix_t[3 + m], i_x[:, m, :]).then_inc(stored, 16)
            sp.wait_ge(stored, 16 * LT)

        @block.vector
        def _(dve):
            dve.memset(x_in[:, :, 0:LTAPS - 1], 0.0).then_inc(zeroed, 1)
            dve.memset(ones[:, :], 1.0).then_inc(zeroed, 1)
            dve.memset(eps[:, :], EPS).then_inc(zeroed, 1)
            dve.wait_ge(zeroed, 3)
            dve.wait_ge(consts_in, 32)
            dve.wait_ge(x_loaded, 16)
            for m in range(LT):
                dve.tensor_scalar(xc[:, m, :], x_in[:, m, LTAPS - 1:], c[:, m, LTAPS - 1:LTAPS], c[:, m, C_BIAS:C_BIAS + 1],
                                  ALU.mult, ALU.add).then_inc(conv_step, 1)
            for t in range(LTAPS - 1):
                for m in range(LT):
                    dve.wait_ge(conv_step, LT * t + m + 1)
                    dve.scalar_tensor_tensor(out=xc[:, m, :], in0=x_in[:, m, t:t + S], scalar=c[:, m, t:t + 1], in1=xc[:, m, :],
                                             op0=ALU.mult, op1=ALU.add).then_inc(conv_step, 1)
            dve.wait_ge(small_act, 3)
            dve.tensor_scalar(sp8[:, :, 2:3], c[:, :, C_LAM:C_LAM + 1], -1.0, 0.0, ALU.mult, ALU.max).then_inc(small, 1)
            dve.wait_ge(small, 1)
            dve.tensor_tensor(sp8[:, :, 1:2], sp8[:, :, 1:2], sp8[:, :, 2:3], ALU.add).then_inc(small, 1)
            dve.wait_ge(small, 2)
            dve.tensor_scalar(sp8[:, :, 2:3], sp8[:, :, 1:2], 8.0, None, ALU.mult).then_inc(small, 1)
            dve.tensor_scalar(sp8[:, :, 3:4], sp8[:, :, 1:2], -8.0, None, ALU.mult).then_inc(small, 1)
            for m in range(LT):
                dve.wait_ge(a2_ready, m + 1)
                dve.wait_ge(tanh_ready, m + 1)
                dve.scalar_tensor_tensor(out=root[:, m, :], in0=a2[:, m, :], scalar=1.0, in1=root[:, m, :], op0=ALU.add,
                                         op1=ALU.mult).then_inc(power_ready, 1)
            for m in range(LT):
                dve.wait_ge(root_ready, m + 1)
                dve.wait_ge(ix_ready, m + 1)
                dve.tensor_tensor(root[:, m, :], root[:, m, :], i_x[:, m, :], ALU.mult).then_inc(u_ready, 1)
                dve.wait_ge(u_ready, m + 1)
                dve.tensor_tensor_scan(xc[:, m, :], r[:, m, :], root[:, m, :], 0.0, ALU.mult, ALU.add).then_inc(h_ready, 1)
                dve.wait_ge(h_ready, m + 1)
                dve.wait_ge(gelu_ready, m + 1)
                dve.tensor_tensor(xc[:, m, :], xc[:, m, :], gate[:, m, :], ALU.mult).then_inc(hg_ready, 1)
            for b in range(BLOCKS):
                at = slice(b * NB, (b + 1) * NB)
                dve.wait_ge(std_ready, b + 1)
                dve.reciprocal(rstd[:, at], rstd[:, at]).then_inc(rstd_ready, 1)
                dve.wait_ge(rstd_ready, b + 1)
                for m in range(LT):
                    ins = dve.scalar_tensor_tensor(out=i_x[:, m, at], in0=xc[:, m, at], scalar=c[:, m, C_NORM:C_NORM + 1], in1=rstd[:, at],
                                                   op0=ALU.mult, op1=ALU.mult)
            ins.then_inc(out_ready, LT)

        @block.gpsimd
        def _(pool):
            for m in range(LT):
                pool.wait_ge(gates_ready, 2 * BLOCKS * (m + 1))
                pool.tensor_tensor(i_x[:, m, :], i_x[:, m, :], xc[:, m, :], ALU.mult).then_inc(ix_ready, 1)

        @block.scalar
        def _(act):
            act.wait_ge(consts_in, 32)
            act.activation(sp8[:, :, 0:1], c[:, :, C_LAM:C_LAM + 1], ACT.Abs).then_inc(small_act, 1)
            act.wait_ge(small_act, 1)
            act.activation(sp8[:, :, 0:1], sp8[:, :, 0:1], ACT.Exp, scale=-1.0).then_inc(small_act, 1)
            act.wait_ge(small_act, 2)
            act.activation(sp8[:, :, 1:2], sp8[:, :, 0:1], ACT.Ln, bias=1.0).then_inc(small_act, 1)
            for m in range(LT):
                for s, (out, bias) in enumerate(((r, C_BA), (i_x, C_BX))):
                    for b in range(BLOCKS):
                        n = (LT * m + s) * BLOCKS + b
                        act.wait_ge(gates_done, n + 1)
                        act.activation(out[:, m, b * NB:(b + 1) * NB], banks[n % 8][:, :], ACT.Sigmoid,
                                       bias=c[:, m, bias:bias + 1]).then_inc(gates_ready, 1)
            act.wait_ge(small, 4)
            act.wait_ge(gates_ready, 4 * BLOCKS)
            for m in range(LT):
                act.activation(root[:, m, :], r[:, m, :], ACT.Tanh, scale=sp8[:, m, 2:3]).then_inc(tanh_ready, 1)
                act.wait_ge(tanh_ready, m + 1)
                act.activation(r[:, m, :], r[:, m, :], ACT.Exp, scale=sp8[:, m, 3:4]).then_inc(a_ready, 1)
                act.wait_ge(a_ready, m + 1)
                act.activation(a2[:, m, :], r[:, m, :], ACT.Square).then_inc(a2_ready, 1)
            for m in range(LT):
                act.wait_ge(power_ready, m + 1)
                act.activation(root[:, m, :], root[:, m, :], ACT.Sqrt).then_inc(root_ready, 1)
            act.wait_ge(gate_loaded, 16)
            for m in range(LT):
                act.activation(gate[:, m, :], gate[:, m, :], ACT.Gelu_apprx_tanh).then_inc(gelu_ready, 1)
            act.wait_ge(power_ready, LT)
            for m in range(LT):
                act.wait_ge(hg_ready, m + 1)
                act.activation(a2[:, m, :], xc[:, m, :], ACT.Square).then_inc(sq_ready, 1)
            for b in range(BLOCKS):
                act.wait_ge(sums_done, b + 1)
                act.activation(rstd[:, b * NB:(b + 1) * NB], banks[b][:, :], ACT.Sqrt, bias=eps[:, :], scale=1.0 / LW).then_inc(std_ready, 1)

        @block.tensor
        def _(pe):
            pe.wait_ge(consts_in, 32)
            for m in range(LT):
                pe.wait_ge(conv_step, LT * (LTAPS - 1) + m + 1)
                for s in range(2):
                    for b in range(BLOCKS):
                        n = (LT * m + s) * BLOCKS + b
                        if n >= 8:
                            pe.wait_ge(gates_ready, n - 7)
                        pe.matmul(banks[n % 8][:, :], w[:, m, s, :], xc[:, m, b * NB:(b + 1) * NB], start=True, stop=True
                                  ).then_inc(gates_done, 1)
            pe.wait_ge(gates_ready, 4 * BLOCKS)
            pe.wait_ge(sq_ready, LT)
            for b in range(BLOCKS):
                for m in range(LT):
                    ins = pe.matmul(banks[b][:, :], ones[:, :], a2[:, m, b * NB:(b + 1) * NB], start=(m == 0), stop=(m == LT - 1))
                ins.then_inc(sums_done, 1)


def combine_patterns(nc, o_scratch, ident, norm_gain, mix_t):
    TILES_T = S // P
    PATS = len(DILATIONS)
    CW = HEADS * HD
    with ExitStack() as ctx:
        used = []
        ctx.callback(free_semaphores, nc, used)

        def sb(name, shape, dt=F32):
            return ctx.enter_context(nc.sbuf_tensor("cb_" + name, shape, dt))

        def sem(name):
            used.append(nc.alloc_semaphore("cb_" + name))
            return used[-1]

        rows = sb("rows", [P, 2, PATS, ROW])
        low = sb("low", [P, 2, HEADS])
        weight = sb("weight", [P, 2, PATS, HEADS])
        total = sb("total", [P, 2, HEADS, OW])
        o_all = sb("o_all", [P, TILES_T, CW])
        junk = sb("junk", [P, CW])
        ss = sb("ss", [P, TILES_T])
        rstd = sb("rstd", [P, TILES_T])
        o_n = sb("o_n", [P, 4, CW])
        out = sb("out", [P, 2, GROUPS, NB])
        idf = sb("idf", [P, P])
        gain = sb("gain", [P, GROUPS])
        eps = sb("eps", [P, 1])
        banks = [ctx.enter_context(nc.psum_tensor(f"cb_bank{i}", [P, NB], F32)) for i in range(2 * GROUPS)]

        consts_in = sem("consts_in")
        eps_ready = sem("eps_ready")
        loaded = [sem(f"loaded{i}") for i in range(2)]
        step = sem("step")
        low_ready = sem("low_ready")
        weight_ready = sem("weight_ready")
        rms_ready = sem("rms_ready")
        rstd_ready = sem("rstd_ready")
        o_n_ready = sem("o_n_ready")
        turned = sem("turned")
        out_ready = sem("out_ready")
        stored = [sem(f"stored{i}") for i in range(2)]
        STEPS = 12

        block = ctx.enter_context(nc.Block())

        @block.sync
        def _(sp):
            sp.dma_start(idf[:, :], ident).then_inc(consts_in, 16)
            sp.dma_start(gain[:, :], norm_gain).then_inc(consts_in, 16)
            for t in range(TILES_T):
                if t >= 2:
                    sp.wait_ge(step, STEPS * (t - 1))
                sp.dma_start(rows[:, t % 2, :, :], o_scratch[:, t * P:(t + 1) * P, :].rearrange("a p r -> p a r")
                             ).then_inc(loaded[t % 2], 16)
            for b in range(BLOCKS):
                sp.wait_ge(out_ready, GROUPS * (b + 1))
                sp.dma_start(mix_t[5:8, :, b * NB:(b + 1) * NB].rearrange("g p s -> p g s"), out[:, b % 2, :, :]).then_inc(stored[b % 2], 16)
            for p in range(2):
                sp.wait_ge(stored[p], 16 * BLOCKS // 2)

        @block.scalar
        def _(act):
            with act.Fori(0, TILES_T // 2) as i:
                for p in range(2):
                    act.wait_ge(low_ready, 2 * i + (p + 1))
                    act.activation(weight[:, p, :, :], weight[:, p, :, :], ACT.Exp).then_inc(weight_ready, 1)
            act.wait_ge(step, STEPS * TILES_T)
            act.wait_ge(eps_ready, 1)
            act.activation(rstd[:, :], ss[:, :], ACT.Sqrt, bias=eps[:, :], scale=1.0 / CW).then_inc(rms_ready, 1)
            act.wait_ge(consts_in, 32)
            for b in range(BLOCKS):
                if b >= 2:
                    act.wait_ge(stored[b % 2], 16 * (b // 2))
                act.wait_ge(turned, 4 * (b + 1))
                for g in range(GROUPS):
                    act.activation(out[:, b % 2, g, :], banks[GROUPS * (b % 2) + g][:, :], ACT.Copy, scale=gain[:, g:g + 1]
                                   ).then_inc(out_ready, 1)

        @block.vector
        def _(dve):
            dve.memset(eps[:, :], EPS).then_inc(eps_ready, 1)

            def combine(t, p, use):
                def done(ins, count):
                    ins.then_inc(step, 1)
                    dve.wait_ge(step, STEPS * t + count)

                dve.wait_ge(loaded[p], 16 * (use + 1))
                neg = [rows[:, p, a, NEG:NEG + HEADS] for a in range(PATS)]
                done(dve.tensor_tensor(low[:, p, :], neg[0], neg[1], ALU.min), 1)
                done(dve.tensor_tensor(low[:, p, :], low[:, p, :], neg[2], ALU.min), 2)
                done(dve.tensor_tensor(weight[:, p, :, :], low[:, p, :].unsqueeze(1).to_broadcast([P, PATS, HEADS]),
                                       rows[:, p, :, NEG:NEG + HEADS], ALU.subtract), 3)
                dve.sem_inc(low_ready, 1)
                dve.wait_ge(weight_ready, t + 1)
                sums = [rows[:, p, a, 0:NEG].rearrange("p (h d) -> p h d", d=OW) for a in range(PATS)]
                for a in range(PATS):
                    ins = dve.tensor_tensor(sums[a], sums[a], weight[:, p, a, :].unsqueeze(2).to_broadcast([P, HEADS, OW]), ALU.mult)
                    ins.then_inc(step, 1)
                dve.wait_ge(step, STEPS * t + 5)
                done(dve.tensor_tensor(total[:, p, :, :], sums[0], sums[1], ALU.add), 7)
                done(dve.tensor_tensor(total[:, p, :, :], total[:, p, :, :], sums[2], ALU.add), 8)
                done(dve.reciprocal(low[:, p, :].unsqueeze(2), total[:, p, :, HD:OW]), 9)
                o = o_all[:, bass.ds(t, 1), :].rearrange("p o (h d) -> p (o h) d", d=HD)
                done(dve.tensor_tensor(o, total[:, p, :, 0:HD], low[:, p, :].unsqueeze(2).to_broadcast([P, HEADS, HD]), ALU.mult), 10)
                flat = o_all[:, bass.ds(t, 1), :].rearrange("p o d -> p (o d)")
                done(dve.tensor_tensor(junk[:, :], flat, flat, ALU.mult), 11)
                done(dve.tensor_reduce(ss[:, bass.ds(t, 1)], junk[:, :], AX.X, ALU.add), 12)

            with dve.Fori(0, TILES_T // 2) as i:
                combine(2 * i, 0, i)
                combine(2 * i + 1, 1, i)
            dve.wait_ge(rms_ready, 1)
            dve.reciprocal(rstd[:, :], rstd[:, :]).then_inc(rstd_ready, 1)
            dve.wait_ge(rstd_ready, 1)
            for t in range(TILES_T):
                if t >= 4:
                    dve.wait_ge(turned, t - 3)
                dve.tensor_scalar(o_n[:, t % 4, :], o_all[:, t, :], rstd[:, t:t + 1], None, ALU.mult).then_inc(o_n_ready, 1)

        @block.tensor
        def _(pe):
            pe.wait_ge(consts_in, 32)
            for t in range(TILES_T):
                b = t // 4
                pe.wait_ge(o_n_ready, t + 1)
                if b >= 2 and t % 4 == 0:
                    pe.wait_ge(out_ready, GROUPS * (b - 1))
                for g in range(GROUPS):
                    ins = pe.transpose(banks[GROUPS * (b % 2) + g][:, (t % 4) * P:(t % 4 + 1) * P], o_n[:, t % 4, g * P:(g + 1) * P], idf[:, :])
                ins.then_inc(turned, 1)


def shape_constants():

    def bf16_bits(v):
        return (np.ascontiguousarray(v).view(np.uint32) >> 16).astype(np.uint16)

    rot = HD // 4
    inv = (np.float32(500000.0) ** (-np.arange(0, rot, 2, dtype=np.float32) / np.float32(rot))).astype(np.float32)
    angle = np.arange(S, dtype=np.float32)[None, :] * inv[:, None]
    rope = np.zeros((P, 2, S), np.float32)
    rope[:, 0] = 1.0
    rotate = np.zeros((P, P), np.float32)
    for head in range(2):
        lo = slice(head * HD, head * HD + rot // 2)
        hi = slice(head * HD + rot // 2, head * HD + rot)
        rope[lo, 0] = rope[hi, 0] = np.cos(angle)
        rope[lo, 1] = rope[hi, 1] = np.sin(angle)
        for d in range(rot // 2):
            rotate[hi.start + d, lo.start + d] = -1.0
            rotate[lo.start + d, hi.start + d] = 1.0
    q = np.arange(SPAN)[:, None]
    k = np.arange(SPAN)[None, :]
    masks = np.zeros((P, PAIRED, 2 * SPAN), np.float32)
    for j, (pat, r, b) in enumerate(attention_blocks()):
        if j < PAIRED:
            masks[:, j, :SPAN] = np.where((k >= q) & (b > 0), 0.0, -1e30)
            masks[:, j, SPAN:] = np.where(k <= q, 0.0, -1e30)
    ident = np.eye(P, dtype=np.float32)
    head_scales = np.zeros((P, 2), np.float32)
    for head in range(2):
        head_scales[head * HD:(head + 1) * HD, head] = HD ** -0.5
    return {"head_scales": head_scales, "rope": rope, "rotate": rotate, "masks": bf16_bits(masks), "ident": ident,
            "ident_bf": bf16_bits(ident)}
FFN = 2816
PAIRS = FFN // P
OUT_SLABS = KT // 2
HALF = S // 2
HB = HALF // NB
TAPS = 3


def ffn_half(nc, half, mix_t, x_t, slabs, w_down, conv, gains, halo, out_t):
    tok = half * HALF
    with ExitStack() as ctx:
        used = []
        ctx.callback(free_semaphores, nc, used)

        def sb(name, shape, dt=F32):
            return ctx.enter_context(nc.sbuf_tensor(f"f{half}_{name}", shape, dt))

        def sem(name):
            used.append(nc.alloc_semaphore(f"f{half}_{name}"))
            return used[-1]

        h_hi = sb("h_hi", [P, KT, HALF], F32R)
        h_lo = sb("h_lo", [P, KT, HALF], F32R)
        x2 = sb("x2", [P, KT, HALF])
        up_raw = sb("up_raw", [P, KT, 2 * P])
        up_hi = sb("up_hi", [P, 2, KT, 2 * P], F32R)
        up_lo = sb("up_lo", [P, 2, KT, 2 * P], F32R)
        dn_raw = sb("dn_raw", [P, D])
        dn_hi = sb("dn_hi", [P, 2, D], F32R)
        dn_lo = sb("dn_lo", [P, 2, D], F32R)
        u = sb("u", [P, 2, TAPS - 1 + HALF])
        y = sb("y", [P, 2, HALF])
        a_raw = sb("a_raw", [P, HALF])
        a_hi = sb("a_hi", [P, 2, HALF], F32R)
        a_lo = sb("a_lo", [P, 2, HALF], F32R)
        conv_all = sb("conv_all", [P, PAIRS, 2, TAPS + 1])
        conv_now = sb("conv_now", [P, 2, 2, TAPS + 1])
        rstd = sb("rstd", [P, NB])
        ring = sb("ring", [P, 2, NB])
        squares = sb("squares", [P, 2, NB])
        gain = sb("gain", [P, 2, KT])
        ones = sb("ones", [P, P])
        eps = sb("eps", [P, 1])
        banks = [ctx.enter_context(nc.psum_tensor(f"f{half}_bank{i}", [P, NB], F32)) for i in range(8)]

        consts_in = sem("consts_in")
        consts_ready = sem("consts_ready")
        mix_loaded = [sem(f"mix_loaded{i}") for i in range(2)]
        mix_hi_ready = sem("mix_hi_ready")
        mix_ready = sem("mix_ready")
        x_loaded = sem("x_loaded")
        up_loaded = sem("up_loaded")
        up_hi_ready = sem("up_hi_ready")
        up_ready = sem("up_ready")
        up_free = sem("up_free")
        up_done = sem("up_done")
        res_added = sem("res_added")
        dn_loaded = sem("dn_loaded")
        dn_hi_ready = sem("dn_hi_ready")
        dn_ready = sem("dn_ready")
        dn_free = sem("dn_free")
        dn_done = sem("dn_done")
        dn_added = sem("dn_added")
        square_ready = sem("square_ready")
        square_used = sem("square_used")
        std_ready = sem("std_ready")
        rstd_ready = sem("rstd_ready")
        ring_ready = sem("ring_ready")
        ring_hi_ready = sem("ring_hi_ready")
        h_ready = sem("h_ready")
        u_ready = sem("u_ready")
        halo_in = sem("halo_in")
        halo_out = sem("halo_out")
        conv_w_ready = sem("conv_w_ready")
        conv_step = sem("conv_step")
        gelu_ready = sem("gelu_ready")
        a_raw_ready = sem("a_raw_ready")
        a_hi_ready = sem("a_hi_ready")
        a_ready = sem("a_ready")
        a_free = sem("a_free")
        y_ready = sem("y_ready")
        stored = [sem(f"stored{i}") for i in range(2)]

        block = ctx.enter_context(nc.Block())
        DOWN = KT * HB

        def blk(b):
            return slice(b * NB, (b + 1) * NB)

        @block.sync
        def _(sp):
            def load_slab(n):
                sp.wait_ge(up_ready, n)
                sp.dma_start(up_raw[:, :, :], slabs[n]).then_inc(up_loaded, 16)

            def load_down(e):
                sp.wait_ge(dn_ready, e)
                sp.dma_start(dn_raw[:, :], w_down[e]).then_inc(dn_loaded, 16)

            sp.dma_start(up_raw[:, :, :], slabs[0]).then_inc(up_loaded, 16)
            for k in range(KT):
                if k >= 2:
                    sp.wait_ge(mix_ready, k - 1)
                sp.dma_start(y[:, k % 2, :], mix_t[k, :, tok:tok + HALF]).then_inc(mix_loaded[k % 2], 16)
                if k == 3:
                    load_slab(1)
            sp.dma_start(x2[:, :, :], x_t[:, :, tok:tok + HALF]).then_inc(x_loaded, 16)
            sp.dma_start(gain[:, :, :], gains).then_inc(consts_in, 16)
            sp.dma_start(conv_all[:, :, :, :], conv).then_inc(consts_in, 16)
            sp.dma_start(dn_raw[:, :], w_down[0]).then_inc(dn_loaded, 16)
            for n in range(2, OUT_SLABS + 2):
                load_slab(n)
            load_down(1)
            load_slab(OUT_SLABS + 2)
            with sp.Fori(0, PAIRS // 2 - 2) as i:
                for j in range(2):
                    load_slab(2 * i + (j + OUT_SLABS + 3))
                    load_down(2 * i + (j + 2))
            load_slab(OUT_SLABS + PAIRS - 1)
            load_down(PAIRS - 2)
            load_down(PAIRS - 1)
            for b in range(HB):
                for k in range(KT):
                    n = KT * b + k
                    sp.wait_ge(y_ready, n + 1)
                    sp.dma_start(out_t[:, k, tok + b * NB:tok + (b + 1) * NB], ring[:, n % 2, :]).then_inc(stored[n % 2], 16)
            for p in range(2):
                sp.wait_ge(stored[p], 16 * HB * KT // 2)

        @block.gpsimd
        def _(pool):
            pool.sem_inc(halo_out, 1)
            pool.wait_ge(consts_in, 32)

            def halos(e, j):
                pool.wait_ge(conv_step, 4 * e + 4)
                pool.wait_ge(halo_out, e + 1)
                pool.tensor_copy(conv_now[:, j, :, :], conv_all[:, bass.ds(e, 1), :, :].rearrange("p o a t -> p (o a) t")).then_inc(conv_w_ready, 1)
                pool.tensor_copy(u[:, :, 0:TAPS - 1], halo[:, half, bass.ds(e, 1), :, :].rearrange("p o a t -> p (o a) t")).then_inc(halo_in, 1)
                if half == 0:
                    pool.wait_ge(u_ready, 4 * e + 8)
                    pool.tensor_copy(halo[:, 1, bass.ds(e, 1), :, :].rearrange("p o a t -> p (o a) t"), u[:, :, HALF:HALF + TAPS - 1]).then_inc(halo_out, 1)
                else:
                    pool.sem_inc(halo_out, 1)

            with pool.Fori(0, PAIRS // 2) as i:
                for j in range(2):
                    halos(2 * i + j, j)

        @block.scalar
        def _(act):
            act.sem_inc(u_ready, 4)

            def slab_high(n, p):
                act.wait_ge(up_loaded, 16 * (n + 1))
                act.wait_ge(up_free, n + 1)
                act.activation(up_hi[:, p, :, :], up_raw[:, :, :], ACT.Copy).then_inc(up_hi_ready, 1)

            def down_high(e, p):
                act.wait_ge(dn_loaded, 16 * (e + 1))
                act.wait_ge(dn_free, e + 1)
                act.activation(dn_hi[:, p, :], dn_raw[:, :], ACT.Copy).then_inc(dn_hi_ready, 1)

            def square(b, turn):
                for k in range(KT):
                    n = turn * KT * HB + KT * b + k
                    if n >= 2:
                        act.wait_ge(square_used, n - 1)
                    act.activation(squares[:, n % 2, :], x2[:, k, blk(b)], ACT.Square).then_inc(square_ready, 1)

            def spread(b, turn):
                n = turn * HB + b
                act.wait_ge(square_used, KT * (n + 1))
                if n > HB:
                    act.wait_ge(y_ready, KT * (n - HB))
                elif n:
                    act.wait_ge(ring_ready, KT * n)
                act.activation(rstd[:, :], banks[4 + b][:, :], ACT.Sqrt, bias=eps[:, :], scale=1.0 / D).then_inc(std_ready, 1)

            def to_conv(e, j):
                act.wait_ge(conv_step, 4 * e + 4)
                act.wait_ge(halo_out, e + 1)
                act.wait_ge(a_raw_ready, e + 1)
                act.wait_ge(conv_w_ready, e + 1)
                for a in range(2):
                    for b in range(HB):
                        act.wait_ge(up_done, 4 * OUT_SLABS + 4 * e + (2 * a + b + 1))
                        bank = banks[2 * a + b][:, :]
                        act.activation(u[:, a, TAPS - 1 + b * NB:TAPS - 1 + (b + 1) * NB], bank, ACT.Copy)
                        act.activation(y[:, a, blk(b)], bank, ACT.Identity, bias=conv_now[:, j, a, TAPS:TAPS + 1],
                                       scale=conv_now[:, j, a, TAPS - 1:TAPS]).then_inc(u_ready, 1)

            def gate(e, p):
                act.wait_ge(conv_step, 4 * e + 8)
                act.activation(y[:, 1, :], y[:, 1, :], ACT.Gelu_apprx_tanh).then_inc(gelu_ready, 1)
                act.wait_ge(a_free, e + 1)
                act.wait_ge(a_raw_ready, e + 2)
                act.activation(a_hi[:, p, :], a_raw[:, :], ACT.Copy).then_inc(a_hi_ready, 1)

            slab_high(0, 0)
            for k in range(KT):
                act.wait_ge(mix_loaded[k % 2], 16 * (k // 2 + 1))
                act.activation(h_hi[:, k, :], y[:, k % 2, :], ACT.Copy).then_inc(mix_hi_ready, 1)
            for n in range(1, OUT_SLABS + 2):
                slab_high(n, n % 2)
            act.wait_ge(res_added, 4 + 4 * OUT_SLABS)
            act.wait_ge(consts_ready, 2)
            square(0, 0)
            for b in range(HB):
                if b + 1 < HB:
                    square(b + 1, 0)
                spread(b, 0)
                for k in range(KT):
                    n = KT * b + k
                    act.wait_ge(ring_ready, n + 1)
                    act.activation(h_hi[:, k, blk(b)], ring[:, n % 2, :], ACT.Copy).then_inc(ring_hi_ready, 1)
            down_high(0, 0)
            to_conv(0, 0)
            slab_high(OUT_SLABS + 2, 0)
            gate(0, 0)
            down_high(1, 1)

            def body(e, j):
                to_conv(e + 1, 1 - j)
                slab_high(e + (OUT_SLABS + 3), 1 - j)
                gate(e + 1, 1 - j)
                down_high(e + 2, j)

            with act.Fori(0, PAIRS // 2 - 2) as i:
                body(2 * i, 0)
                body(2 * i + 1, 1)
            body(PAIRS - 4, 0)
            to_conv(PAIRS - 2, 0)
            gate(PAIRS - 2, 0)
            down_high(PAIRS - 1, 1)
            to_conv(PAIRS - 1, 1)
            gate(PAIRS - 1, 1)
            act.wait_ge(dn_added, 4 + DOWN * PAIRS)
            square(0, 1)
            for b in range(HB):
                if b + 1 < HB:
                    square(b + 1, 1)
                spread(b, 1)

        @block.vector
        def _(dve):
            dve.sem_inc(res_added, 4)
            dve.sem_inc(dn_added, 4)
            dve.sem_inc(conv_step, 4)
            dve.sem_inc(a_raw_ready, 1)
            dve.sem_inc(a_ready, 1)
            dve.memset(ones[:, :], 1.0).then_inc(consts_ready, 1)
            dve.memset(eps[:, :], EPS).then_inc(consts_ready, 1)

            def slab_low(n, p):
                dve.wait_ge(up_hi_ready, n + 1)
                dve.tensor_tensor(up_lo[:, p, :, :], up_raw[:, :, :], up_hi[:, p, :, :].bitcast(F32),
                                  ALU.subtract).then_inc(up_ready, 1)

            def down_low(e, p):
                dve.wait_ge(dn_hi_ready, e + 1)
                dve.tensor_tensor(dn_lo[:, p, :], dn_raw[:, :], dn_hi[:, p, :].bitcast(F32), ALU.subtract).then_inc(dn_ready, 1)

            def add_residual(n):
                for a in range(2):
                    for b in range(HB):
                        dve.wait_ge(up_done, 4 * n + (2 * a + b + 1))
                        at = x2[:, 2 * n + a, blk(b)]
                        dve.tensor_tensor(at, banks[2 * a + b][:, :], at, ALU.add).then_inc(res_added, 1)

            def normalise(b, turn, which):
                n0 = turn * HB * KT + KT * b
                dve.wait_ge(std_ready, turn * HB + b + 1)
                dve.reciprocal(rstd[:, :], rstd[:, :]).then_inc(rstd_ready, 1)
                dve.wait_ge(rstd_ready, turn * HB + b + 1)

                def scaled(k):
                    n = n0 + k
                    if turn == 0 and n >= 2:
                        dve.wait_ge(h_ready, n - 1)
                    if turn == 1:
                        m = KT * b + k
                        if m >= 2:
                            dve.wait_ge(stored[m % 2], 16 * (m // 2))
                        else:
                            dve.wait_ge(h_ready, HB * KT)
                    ins = dve.scalar_tensor_tensor(out=ring[:, n % 2, :], in0=x2[:, k, blk(b)], scalar=gain[:, which, k:k + 1],
                                                   in1=rstd[:, :], op0=ALU.mult, op1=ALU.mult)
                    ins.then_inc(ring_ready if turn == 0 else y_ready, 1)

                def low(k):
                    n = n0 + k
                    dve.wait_ge(ring_hi_ready, n + 1)
                    dve.tensor_tensor(h_lo[:, k, blk(b)], ring[:, n % 2, :], h_hi[:, k, blk(b)].bitcast(F32),
                                      ALU.subtract).then_inc(h_ready, 1)

                scaled(0)
                for k in range(1, KT):
                    scaled(k)
                    if turn == 0:
                        low(k - 1)
                if turn == 0:
                    low(KT - 1)

            def convolve(e, j):
                dve.wait_ge(u_ready, 4 * e + 8)
                dve.wait_ge(halo_in, e + 1)
                for s, (tap, a) in enumerate([(1, 1), (1, 0), (0, 1), (0, 0)]):
                    if tap == 0:
                        dve.wait_ge(conv_step, 4 * e + (4 + s - 1))
                    dve.scalar_tensor_tensor(out=y[:, a, :], in0=u[:, a, tap:tap + HALF], scalar=conv_now[:, j, a, tap:tap + 1],
                                             in1=y[:, a, :], op0=ALU.mult, op1=ALU.add).then_inc(conv_step, 1)

            def gated(e):
                dve.wait_ge(gelu_ready, e + 1)
                dve.wait_ge(conv_step, 4 * e + 8)
                dve.wait_ge(a_ready, e + 1)
                dve.tensor_tensor(a_raw[:, :], y[:, 0, :], y[:, 1, :], ALU.mult).then_inc(a_raw_ready, 1)

            def act_low(e, p):
                dve.wait_ge(a_hi_ready, e + 1)
                dve.tensor_tensor(a_lo[:, p, :], a_raw[:, :], a_hi[:, p, :].bitcast(F32), ALU.subtract).then_inc(a_ready, 1)

            def add_down(e):
                dve.wait_ge(dn_added, DOWN * e + 4)
                for m in range(DOWN):
                    dve.wait_ge(dn_done, DOWN * e + (m + 1))
                    at = x2[:, m // HB, blk(m % HB)]
                    dve.tensor_tensor(at, banks[4 + m % 4][:, :], at, ALU.add).then_inc(dn_added, 1)

            slab_low(0, 0)
            for k in range(KT):
                dve.wait_ge(mix_hi_ready, k + 1)
                dve.tensor_tensor(h_lo[:, k, :], y[:, k % 2, :], h_hi[:, k, :].bitcast(F32), ALU.subtract).then_inc(mix_ready, 1)
            slab_low(1, 1)
            dve.wait_ge(x_loaded, 16)
            for n in range(OUT_SLABS):
                add_residual(n)
                slab_low(n + 2, n % 2)
            dve.wait_ge(consts_in, 32)
            dve.wait_ge(res_added, 4 + 4 * OUT_SLABS)
            normalise(0, 0, 0)
            normalise(1, 0, 0)
            down_low(0, 0)
            convolve(0, 0)
            slab_low(OUT_SLABS + 2, 0)
            gated(0)
            act_low(0, 0)
            down_low(1, 1)

            def body(e, j):
                add_down(e)
                convolve(e + 1, 1 - j)
                slab_low(e + (OUT_SLABS + 3), 1 - j)
                gated(e + 1)
                act_low(e + 1, 1 - j)
                down_low(e + 2, j)

            with dve.Fori(0, PAIRS // 2 - 2) as i:
                body(2 * i, 0)
                body(2 * i + 1, 1)
            body(PAIRS - 4, 0)
            add_down(PAIRS - 3)
            convolve(PAIRS - 2, 0)
            gated(PAIRS - 2)
            act_low(PAIRS - 2, 0)
            down_low(PAIRS - 1, 1)
            add_down(PAIRS - 2)
            convolve(PAIRS - 1, 1)
            gated(PAIRS - 1)
            act_low(PAIRS - 1, 1)
            add_down(PAIRS - 1)
            dve.wait_ge(dn_added, 4 + DOWN * PAIRS)
            normalise(0, 1, 1)
            normalise(1, 1, 1)

        @block.tensor
        def _(pe):
            pe.sem_inc(up_free, 2)
            pe.sem_inc(dn_free, 2)
            pe.sem_inc(a_free, 2)
            pe.wait_ge(consts_ready, 2)

            def slab(n, p, bank_free, bank_at):
                pe.wait_ge(up_ready, n + 1)
                for a in range(2):
                    for b in range(HB):
                        pe.wait_ge(bank_free, bank_at + (2 * a + b + 1))
                        product(pe, banks[2 * a + b][:, :],
                                [up_hi[:, p, k, a * P:(a + 1) * P] for k in range(KT)],
                                [up_lo[:, p, k, a * P:(a + 1) * P] for k in range(KT)],
                                [h_hi[:, k, blk(b)] for k in range(KT)],
                                [h_lo[:, k, blk(b)] for k in range(KT)]).then_inc(up_done, 1)
                pe.wait_ge(up_done, 4 * (n + 1))
                pe.sem_inc(up_free, 1)

            def sum_squares(b, turn):
                for k in range(KT):
                    n = turn * KT * HB + KT * b + k
                    pe.wait_ge(square_ready, n + 1)
                    pe.matmul(banks[4 + b][:, :], ones[:, :], squares[:, n % 2, :], start=(k == 0),
                              stop=(k == KT - 1)).then_inc(square_used, 1)

            def down(e, p):
                pe.wait_ge(dn_ready, e + 1)
                pe.wait_ge(a_ready, e + 2)
                for m in range(DOWN):
                    pe.wait_ge(dn_added, DOWN * e + (m + 1))
                    oc = slice((m // HB) * P, (m // HB + 1) * P)
                    b = m % HB
                    product(pe, banks[4 + m % 4][:, :], [dn_hi[:, p, oc]], [dn_lo[:, p, oc]],
                            [a_hi[:, p, blk(b)]], [a_lo[:, p, blk(b)]]).then_inc(dn_done, 1)
                pe.wait_ge(dn_done, DOWN * (e + 1))
                pe.sem_inc(dn_free, 1)
                pe.sem_inc(a_free, 1)

            pe.wait_ge(mix_ready, KT)
            with pe.Fori(0, OUT_SLABS // 2) as i:
                for j in range(2):
                    slab(2 * i + j, j, res_added, 8 * i + 4 * j)
            sum_squares(0, 0)
            sum_squares(1, 0)
            pe.wait_ge(res_added, 4 + 4 * OUT_SLABS)
            pe.wait_ge(h_ready, KT * HB)

            def up(e, p):
                slab(e + OUT_SLABS, p, u_ready, 4 * e)

            up(0, 0)

            def body(e, j):
                up(e + 1, 1 - j)
                down(e, j)

            with pe.Fori(0, PAIRS // 2 - 1) as i:
                body(2 * i, 0)
                body(2 * i + 1, 1)
            body(PAIRS - 2, 0)
            down(PAIRS - 1, 1)
            pe.wait_ge(dn_added, 4 + DOWN * PAIRS)
            sum_squares(0, 1)
            sum_squares(1, 1)


def mixer_constants():
    starts = np.ones((P, NB), np.float32)
    starts[:, ::CH] = 0.0
    j = np.arange(P)[:, None]
    i = np.arange(CH)[None, :]
    return {"starts": starts, "causal": np.ascontiguousarray(np.broadcast_to((i >= j)[:, None, :], (P, 2, CH))).astype(np.uint32)}


def program(nc, t, out_t):
    proj_t = nc.dram_tensor("proj_t", [TILES, P, S], F32, kind="Internal").ap()
    o_scratch = nc.dram_tensor("o_scratch", [len(DILATIONS), S, ROW], F32, kind="Internal").ap()
    mix_t = nc.dram_tensor("mix_t", [KT, P, S], F32, kind="Internal").ap()
    input_projection(nc, t["x_t"], t["norm_mix"], t["w_in"], proj_t)
    dilated_attention(nc, proj_t, t["rope"], t["rotate"], t["masks"].bitcast(BF16), t["ident"], t["ident_bf"].bitcast(BF16), t["head_scales"], o_scratch)
    gated_linear_attention(nc, proj_t, t["gla_w_gate"], t["gla_b_gate"], t["starts"], t["causal"], t["ident"], t["gla_norm"], mix_t)
    recurrent_branch(nc, proj_t, t["lru"], t["lru_w"], mix_t)
    combine_patterns(nc, o_scratch, t["ident"], t["swa_norm"], mix_t)
    with ExitStack() as ctx:
        halo = ctx.enter_context(nc.sbuf_tensor("halo", [P, 2, PAIRS, 2, TAPS - 1], F32))
        zeroed = ctx.enter_context(nc.semaphore("halo_zeroed"))
        with nc.Block() as block:
            @block.vector
            def _(dve):
                dve.memset(halo[:, 0], 0.0).then_inc(zeroed, 1)
                dve.wait_ge(zeroed, 1)
        for half in range(2):
            ffn_half(nc, half, mix_t, t["x_t"], t["slabs"], t["w_down"], t["conv"], t["gains"], halo, out_t)


def pad_heads(w):
    out = np.zeros(w.shape[:-1] + (GP * P,), np.float32)
    for h in range(GH):
        out[..., h * 64:h * 64 + DK] = w[..., h * DK:(h + 1) * DK]
    return out


def kernel(**inputs):
    import concourse.bacc as bacc
    from concourse.bass_utils import run_bass_kernel_spmd as run

    a = {k: np.asarray(v) for k, v in inputs.items()}
    flat = np.ascontiguousarray

    def per_channel(v):
        return flat(v.reshape(-1, P).T)

    arrays = {"x_t": flat(a["x"][0].T.reshape(KT, P, S).transpose(1, 0, 2)), "norm_mix": per_channel(a["norm_mix"][0])}
    sizes = (GH * DK, GH * DK, AW, AW, RANK, LW, LW, HEADS * HD, HEADS * HD, HEADS * HD)
    aq, ak, av, ar, glr, bg, bi, cq, ck, cv = np.split(a["w_in"][0], np.cumsum(sizes)[:-1], axis=1)
    aq = pad_heads(aq)
    aq[:, GLR_ROW:GLR_ROW + RANK] = glr
    w = np.concatenate([aq, pad_heads(ak), av, ar, bg, bi, cq, ck, cv], axis=1)
    arrays["w_in"] = flat(w.reshape(KT, P, TILES, P).transpose(2, 1, 0, 3))
    arrays["gla_w_gate"] = flat(pad_heads(a["gla_w_gate"][0]).reshape(RANK, GP, P))
    arrays["gla_b_gate"] = per_channel(pad_heads(a["gla_b_gate"][0]))
    arrays["gla_norm"] = per_channel(np.tile(a["gla_norm"][0], GH))
    per = [a["lru_conv_w"][0][t] for t in range(LTAPS)] + [a[n][0] for n in ("lru_conv_b", "lru_b_a", "lru_b_x", "lru_lambda", "lru_norm")]
    arrays["lru"] = flat(np.stack(per).reshape(C_NORM + 1, LT, P).transpose(2, 1, 0))
    lru_w = np.zeros((P, LT, 2, P), np.float32)
    bs = a["lru_w_a"].shape[-1]
    for s, name in enumerate(("lru_w_a", "lru_w_x")):
        for n in range(LW // bs):
            at = n * bs % P
            lru_w[at:at + bs, n * bs // P, s, at:at + bs] = a[name][0, n]
    arrays["lru_w"] = lru_w
    arrays["swa_norm"] = per_channel(a["swa_norm"][0])
    w_out_slabs = a["w_out"][0].reshape(KT, P, OUT_SLABS, 2 * P).transpose(2, 1, 0, 3)
    w_up_slabs = a["ffn_w_up"][0].reshape(KT, P, 2, PAIRS, P).transpose(3, 1, 0, 2, 4).reshape(PAIRS, P, KT, 2 * P)
    arrays["slabs"] = np.concatenate([w_out_slabs, w_up_slabs])
    arrays["w_down"] = flat(a["ffn_w_down"][0].reshape(PAIRS, P, D))
    conv = np.concatenate([a["ffn_conv_w"][0], a["ffn_conv_b"]])
    arrays["conv"] = flat(conv.reshape(TAPS + 1, 2, PAIRS, P).transpose(3, 2, 1, 0))
    arrays["gains"] = flat(np.stack([per_channel(a["norm_ffn"][0]), per_channel(a["norm_final"])], axis=1))
    arrays.update(shape_constants())
    arrays.update(mixer_constants())

    nc = bacc.Bacc("TRN2", target_bir_lowering=False, num_devices=1)
    tensors = {k: nc.dram_tensor("in_" + k, v.shape, mybir.dt.from_np(v.dtype), kind="ExternalInput").ap() for k, v in arrays.items()}
    out_t = nc.dram_tensor("out_t", [P, KT, S], F32, kind="ExternalOutput").ap()
    program(nc, tensors, out_t)
    r = run(nc, [{"in_" + k: v for k, v in arrays.items()}], core_ids=[0])
    return flat(r.results[0]["out_t"].transpose(2, 1, 0).reshape(1, S, D))
```

```python
from contextlib import ExitStack

import numpy as np

import concourse.bass as bass
from concourse import mybir

F32 = mybir.dt.float32
F32R = mybir.dt.float32r
BF16 = mybir.dt.bfloat16
ALU = mybir.AluOpType
ACT = mybir.ActivationFunctionType
AX = mybir.AxisListType

P = 128
D = 1024
KT = D // P
S = 2048
NB = 512
BLOCKS = S // NB
EPS = 1e-6

T_AQ, T_AK, T_AV, T_AR, T_BG, T_BI, T_CQ, T_CK, T_CV = 0, 2, 4, 7, 10, 12, 14, 17, 20
TILES = 23
GLR_ROW = 112


def free_semaphores(nc, used):
    nc.clear_and_free_semaphores(used)
    nc.all_engine_barrier()


def product(pe, out, w_hi, w_lo, x_hi, x_lo, x_ready=None):
    n = len(w_hi)
    for k in range(n):
        if x_ready is not None:
            pe.wait_ge(x_ready, k + 1)
        pe.matmul(out, w_hi[k], x_hi[k], start=(k == 0), stop=False)
        pe.matmul(out, w_hi[k], x_lo[k], start=False, stop=False)
        last = pe.matmul(out, w_lo[k], x_hi[k], start=False, stop=(k == n - 1))
    return last


def input_projection(nc, x_t, norm_gain, w_tiles, proj_t):
    with ExitStack() as ctx:
        used = []
        ctx.callback(free_semaphores, nc, used)

        def sb(name, shape, dt=F32):
            return ctx.enter_context(nc.sbuf_tensor("ip_" + name, shape, dt))

        def sem(name):
            used.append(nc.alloc_semaphore("ip_" + name))
            return used[-1]

        x_in = sb("x_in", [P, 2, KT, NB])
        squares = sb("squares", [P, 3, NB])
        total = sb("total", [P, 2, 2, NB])
        x_hi = sb("x_hi", [P, KT, S], F32R)
        x_lo = sb("x_lo", [P, KT, S], F32R)
        w_raw = sb("w_raw", [P, KT, P])
        w_hi = sb("w_hi", [P, 2, KT, P], F32R)
        w_lo = sb("w_lo", [P, 2, KT, P], F32R)
        staged = sb("staged", [P, 2, NB])
        rstd = sb("rstd", [P, S])
        gain = sb("gain", [P, KT])
        ones = sb("ones", [P, P])
        eps = sb("eps", [P, 1])
        banks = [ctx.enter_context(nc.psum_tensor(f"ip_bank{i}", [P, NB], F32)) for i in range(8)]

        gain_in = sem("gain_in")
        x_loaded = [sem(f"x_loaded{i}") for i in range(2)]
        consts_ready = sem("consts_ready")
        hi_ready = sem("hi_ready")
        x_ready = sem("x_ready")
        square_ready = sem("square_ready")
        added = [sem("added_even"), sem("added_odd")]
        x_first_loaded = sem("x_first_loaded")
        sum_done = sem("sum_done")
        std_ready = sem("std_ready")
        rstd_ready = sem("rstd_ready")
        w_loaded = sem("w_loaded")
        w_scaled = sem("w_scaled")
        w_hi_ready = sem("w_hi_ready")
        w_ready = sem("w_ready")
        product_done = sem("product_done")
        bank_free = sem("bank_free")
        stored = [sem(f"stored{i}") for i in range(2)]

        block = ctx.enter_context(nc.Block())
        SUM_BANK = (7, 7, 0, 1)
        FIRST = 2 * BLOCKS
        TURNS = (TILES - 3) // 2

        def blk(b):
            return slice(b * NB, (b + 1) * NB)

        def add_squares(engine, b, odd):
            for k in range(KT // 2):
                n = KT // 2 * b + k
                engine.wait_ge(square_ready, 2 * n + odd + 1)
                at = squares[:, (2 * n + odd) % 3, :]
                if k:
                    engine.wait_ge(added[odd], n)
                    ins = engine.tensor_tensor(total[:, b % 2, odd, :], total[:, b % 2, odd, :], at, ALU.add)
                else:
                    if b >= 2:
                        engine.wait_ge(sum_done, b - 1)
                    ins = engine.tensor_copy(total[:, b % 2, odd, :], at)
                ins.then_inc(added[odd], 1)

        @block.sync
        def _(sp):
            for p in range(2):
                sp.sem_inc(stored[p], 16)

            def load_weights(t):
                if not isinstance(t, int) or t > 0:
                    sp.wait_ge(w_ready, t)
                sp.dma_start(w_raw[:, :, :], w_tiles[t]).then_inc(w_loaded, 16)

            def load_x(b):
                if b >= 2:
                    sp.wait_ge(x_ready, KT * (b - 1))
                    sp.wait_ge(square_ready, KT * (b - 1))
                if b == 0:
                    sp.dma_start(x_in[:, 0, 0:KT // 2, :], x_t[:, 0:KT // 2, blk(0)]).then_inc(x_first_loaded, 16)
                    sp.dma_start(x_in[:, 0, KT // 2:, :], x_t[:, KT // 2:, blk(0)]).then_inc(x_loaded[0], 16)
                else:
                    sp.dma_start(x_in[:, b % 2, :, :], x_t[:, :, blk(b)]).then_inc(x_loaded[b % 2], 16)

            def store_first(n):
                sp.wait_ge(bank_free, 8 + n + 1)
                sp.dma_start(proj_t[n % 2][:, blk(n // 2)], staged[:, n % 2, :]).then_inc(stored[n % 2], 16)

            def store_tile(t):
                for b in range(BLOCKS):
                    sp.wait_ge(bank_free, BLOCKS * t + (8 + b + 1))
                    sp.dma_start(proj_t[t][:, blk(b)], staged[:, b % 2, :]).then_inc(stored[b % 2], 16)

            load_weights(0)
            sp.dma_start(gain[:, :], norm_gain).then_inc(gain_in, 16)
            load_x(0)
            load_x(1)
            load_weights(1)
            load_x(2)
            load_x(3)
            load_weights(2)
            for n in range(FIRST):
                if n == FIRST - 2:
                    load_weights(3)
                store_first(n)
            with sp.Fori(0, TURNS - 1) as i:
                for j in range(2):
                    load_weights(2 * i + (4 + j))
                    store_tile(2 * i + (2 + j))
            load_weights(TILES - 1)
            for t in range(TILES - 3, TILES):
                store_tile(t)
            for p in range(2):
                sp.wait_ge(stored[p], 16 + 16 * BLOCKS // 2 * TILES)

        @block.gpsimd
        def _(pool):
            pool.wait_ge(gain_in, 16)

            def scale_weights(t):
                pool.wait_ge(w_loaded, 16 * (t + 1))
                pool.tensor_tensor(w_raw[:, :, :], w_raw[:, :, :], gain[:, :].unsqueeze(2).to_broadcast([P, KT, P]),
                                   ALU.mult).then_inc(w_scaled, 1)

            scale_weights(0)
            scale_weights(1)
            add_squares(pool, 0, 0)
            add_squares(pool, 1, 0)
            add_squares(pool, 2, 0)
            scale_weights(2)
            add_squares(pool, 3, 0)
            with pool.Fori(0, TURNS) as i:
                for j in range(2):
                    scale_weights(2 * i + (3 + j))

        @block.scalar
        def _(act):
            def weights_high(t, p, multiplied):
                act.wait_ge(w_scaled, t + 1)
                if multiplied is not None:
                    act.wait_ge(product_done, multiplied)
                act.activation(w_hi[:, p, :, :], w_raw[:, :, :], ACT.Copy).then_inc(w_hi_ready, 1)

            def split(b):
                if b == 0:
                    act.wait_ge(x_first_loaded, 16)
                for k in range(KT):
                    if k == (KT // 2 if b == 0 else 0):
                        act.wait_ge(x_loaded[b % 2], 16 * (b // 2 + 1))
                    act.activation(x_hi[:, k, blk(b)], x_in[:, b % 2, k, :], ACT.Copy).then_inc(hi_ready, 1)
                if b == 0:
                    weights_high(1, 1, None)
                for k in range(KT):
                    n = KT * b + k
                    if n >= 3:
                        act.wait_ge(added[(n - 3) % 2], (n - 3) // 2 + 1)
                    act.activation(squares[:, n % 3, :], x_in[:, b % 2, k, :], ACT.Square).then_inc(square_ready, 1)

            def root(b):
                act.wait_ge(sum_done, b + 1)
                act.activation(rstd[:, blk(b)], banks[SUM_BANK[b]][:, :], ACT.Sqrt, bias=eps[:, :],
                               scale=1.0 / D).then_inc(std_ready, 1)

            weights_high(0, 0, None)
            split(0)
            split(1)
            act.wait_ge(consts_ready, 2)
            split(2)
            root(0)
            split(3)
            root(1)
            root(2)
            weights_high(2, 0, FIRST - 1)
            root(3)
            with act.Fori(0, TURNS) as i:
                weights_high(2 * i + 3, 1, 8 * i + 8)
                weights_high(2 * i + 4, 0, 8 * i + 12)

        @block.vector
        def _(dve):
            dve.sem_inc(bank_free, 8)
            dve.memset(ones[:, :], 1.0).then_inc(consts_ready, 1)
            dve.memset(eps[:, :], EPS).then_inc(consts_ready, 1)

            def weights_low(t, p):
                dve.wait_ge(w_hi_ready, t + 1)
                dve.tensor_tensor(w_lo[:, p, :, :], w_raw[:, :, :], w_hi[:, p, :, :].bitcast(F32),
                                  ALU.subtract).then_inc(w_ready, 1)

            def low(b):
                for k in range(KT):
                    dve.wait_ge(hi_ready, KT * b + k + 1)
                    dve.tensor_tensor(x_lo[:, k, blk(b)], x_in[:, b % 2, k, :], x_hi[:, k, blk(b)].bitcast(F32),
                                      ALU.subtract).then_inc(x_ready, 1)

            def invert(b):
                dve.wait_ge(std_ready, b + 1)
                dve.reciprocal(rstd[:, blk(b)], rstd[:, blk(b)]).then_inc(rstd_ready, 1)
                dve.wait_ge(rstd_ready, b + 1)

            def drain(n, bank, b, use):
                dve.wait_ge(product_done, n + 1)
                dve.wait_ge(stored[bank % 2], 16 * (use + 1))
                dve.tensor_tensor(staged[:, bank % 2, :], banks[bank][:, :], rstd[:, blk(b)], ALU.mult).then_inc(bank_free, 1)

            def drain_tile(t, p):
                for b in range(BLOCKS):
                    drain(BLOCKS * t + b, 4 * p + b, b, 2 * t + b // 2)

            weights_low(0, 0)
            low(0)
            weights_low(1, 1)
            add_squares(dve, 0, 1)
            low(1)
            add_squares(dve, 1, 1)
            for b in range(BLOCKS):
                if b + 2 < BLOCKS:
                    low(b + 2)
                    add_squares(dve, b + 2, 1)
                if b == 3:
                    weights_low(2, 0)
                invert(b)
                for n in range(2 * b, 2 * b + 2):
                    drain(n, n, b, n // 2)
            with dve.Fori(0, TURNS) as i:
                weights_low(2 * i + 3, 1)
                drain_tile(2 * i + 2, 0)
                weights_low(2 * i + 4, 0)
                drain_tile(2 * i + 3, 1)
            drain_tile(TILES - 1, 0)

        @block.tensor
        def _(pe):
            pe.wait_ge(consts_ready, 2)

            def project(n, bank, p, b):
                pe.wait_ge(bank_free, n + 1)
                product(pe, banks[bank][:, :],
                        [w_hi[:, p, k, :] for k in range(KT)], [w_lo[:, p, k, :] for k in range(KT)],
                        [x_hi[:, k, blk(b)] for k in range(KT)], [x_lo[:, k, blk(b)] for k in range(KT)],
                        x_ready if isinstance(n, int) and n == 0 else None).then_inc(product_done, 1)

            def sum_squares(b):
                for odd in range(2):
                    pe.wait_ge(added[odd], KT // 2 * (b + 1))
                if b >= 2:
                    pe.wait_ge(bank_free, 8 + b - 1)
                elif b:
                    pe.wait_ge(std_ready, 1)
                for odd in range(2):
                    ins = pe.matmul(banks[SUM_BANK[b]][:, :], ones[:, :], total[:, b % 2, odd, :], start=(odd == 0),
                                    stop=(odd == 1))
                ins.then_inc(sum_done, 1)

            def tile(t, p):
                pe.wait_ge(w_ready, t + 1)
                for b in range(BLOCKS):
                    project(BLOCKS * t + b, 4 * p + b, p, b)

            for n in range(FIRST):
                b, t = n // 2, n % 2
                if b == 0:
                    pe.wait_ge(w_ready, t + 1)
                elif t == 0:
                    pe.wait_ge(x_ready, KT * (b + 1))
                if n == FIRST - 1:
                    pe.wait_ge(std_ready, 2)
                project(n, n, t, b)
                if n in (3, 5, 6, 7):
                    sum_squares({3: 0, 5: 1, 6: 2, 7: 3}[n])
            pe.wait_ge(w_ready, 3)
            for b in range(BLOCKS):
                if b < 2:
                    pe.wait_ge(std_ready, 3 + b)
                project(FIRST + b, b, 0, b)
            with pe.Fori(0, TURNS) as i:
                tile(2 * i + 3, 1)
                tile(2 * i + 4, 0)


HEADS = 6
HD = 64
GROUPS = HEADS // 2
DILATIONS = (1, 4, 16)
SPAN = 128
PAIRED = 32
SINGLE = 16
OW = HD + 1
ROW = HEADS * (OW + 1)
NEG = HEADS * OW


def attention_blocks():
    for pat, dil in enumerate(DILATIONS):
        for r in range(dil):
            for b in range(S // dil // SPAN):
                yield pat, r, b


def dilated_attention(nc, proj_t, rope, rotate, masks, ident, ident_bf, head_scales, o_scratch):
    with ExitStack() as ctx:
        used = []
        ctx.callback(free_semaphores, nc, used)

        def sb(name, shape, dt=F32):
            return ctx.enter_context(nc.sbuf_tensor("at_" + name, shape, dt))

        def sem(name):
            used.append(nc.alloc_semaphore("at_" + name))
            return used[-1]

        qkv = sb("qkv", [P, 3, GROUPS, S])
        cos_sin = sb("cos_sin", [P, 2, S])
        rot_w = sb("rot_w", [P, P])
        mask = sb("mask", [P, PAIRED, 2 * SPAN], BF16)
        idf = sb("idf", [P, P])
        head_scale = sb("head_scale", [P, 2])
        idb = sb("idb", [P, P], BF16)
        rope_c = sb("rope_c", [P, 2, NB])
        rope_s = sb("rope_s", [P, 2, NB])
        q_s = sb("q_s", [P, 2, GROUPS, 2, SPAN])
        k_s = sb("k_s", [P, 2, GROUPS, 2 * SPAN])
        v_s = sb("v_s", [P, 2, GROUPS, SPAN])
        v_tok = sb("v_tok", [P, 2, HEADS, OW])
        probs = sb("probs", [P, GROUPS, 4 * SPAN])
        probs_t = sb("probs_t", [P, GROUPS, 4 * SPAN])
        o_sb = sb("o_sb", [P, 2, ROW])

        def bank(name):
            return ctx.enter_context(nc.psum_tensor("at_" + name, [P, NB], F32))

        s_bank = [bank(f"s{i}") for i in range(GROUPS)]
        t_bank = [bank(f"t{i}") for i in range(2)]
        o_bank = [bank(f"o{i}") for i in range(2)]
        v_bank = bank("v")

        consts_in = sem("consts_in")
        q_in, k_in, v_in = sem("q_in"), sem("k_in"), sem("v_in")
        rotated = sem("rotated")
        times_cos = sem("times_cos")
        times_sin = sem("times_sin")
        roped = sem("roped")
        staged = sem("staged")
        scores_ready = sem("scores_ready")
        max_ready = sem("max_ready")
        probs_ready = sem("probs_ready")
        pt_done = sem("pt_done")
        pt_even = sem("pt_even")
        pt_odd = sem("pt_odd")
        vt_done = sem("vt_done")
        v_ready = sem("v_ready")
        o_done = sem("o_done")
        o_ready = sem("o_ready")
        stored = [sem(f"stored{i}") for i in range(2)]

        block = ctx.enter_context(nc.Block())
        blocks = list(attention_blocks())

        @block.sync
        def _(sp):
            sp.dma_start(rot_w[:, :], rotate).then_inc(consts_in, 16)
            sp.dma_start(head_scale[:, :], head_scales).then_inc(consts_in, 16)
            for a, (t, loaded) in enumerate([(T_CQ, q_in), (T_CK, k_in), (T_CV, v_in)]):
                sp.dma_start(qkv[:, a, :, :], proj_t[t:t + GROUPS].rearrange("g p s -> p g s")).then_inc(loaded, 16)
                if a == 0:
                    sp.dma_start(cos_sin[:, :, :], rope).then_inc(consts_in, 16)
            sp.dma_start(idf[:, :], ident).then_inc(consts_in, 16)
            sp.dma_start(idb[:, :], ident_bf).then_inc(consts_in, 16)
            sp.dma_start(mask[:, :, :], masks).then_inc(consts_in, 16)
            for j, (pat, r, b) in enumerate(blocks):
                dil = DILATIONS[pat]
                first = dil * SPAN * b + r
                rows = o_scratch[pat, first:first + dil * (SPAN - 1) + 1:dil, :]
                sp.wait_ge(o_ready, j + 1)
                sp.dma_start(rows, o_sb[:, j % 2, :]).then_inc(stored[j % 2], 16)
            for p in range(2):
                sp.wait_ge(stored[p], 16 * len(blocks) // 2)

        @block.gpsimd
        def _(pool):
            pool.wait_ge(consts_in, 16 * 6)
            pool.wait_ge(k_in, 16)
            pool.wait_ge(q_in, 16)
            with pool.Fori(0, BLOCKS) as i:
                for m in range(2 * GROUPS):
                    pool.wait_ge(roped, 2 * GROUPS * i + (m + 1))
                    at = bass.ds(i * NB, NB)
                    pool.tensor_tensor(rope_c[:, m % 2, :], qkv[:, m // GROUPS, m % GROUPS, at], cos_sin[:, 0, at],
                                       ALU.mult).then_inc(times_cos, 1)
            pool.wait_ge(roped, 2 + 2 * GROUPS * BLOCKS)
            pool.wait_ge(v_in, 16)
            for j, (pat, r, b) in enumerate(blocks):
                dil = DILATIONS[pat]
                first = dil * SPAN * b + r

                def tokens(a, start):
                    return qkv[:, a, :, start:start + dil * (SPAN - 1) + 1:dil]

                if j >= 2:
                    pool.wait_ge(scores_ready, GROUPS * (j - 1))
                    pool.wait_ge(vt_done, j - 1)
                for hh in range(2):
                    pool.tensor_scalar(q_s[:, j % 2, :, hh, :], tokens(0, first), head_scale[:, hh:hh + 1], None,
                                       ALU.mult).then_inc(staged, 1)
                if pat < 2:
                    prev = first - dil * SPAN if b else first
                    pool.tensor_copy(k_s[:, j % 2, :, 0:SPAN], tokens(1, prev)).then_inc(staged, 1)
                    pool.tensor_copy(k_s[:, j % 2, :, SPAN:2 * SPAN], tokens(1, first)).then_inc(staged, 1)
                else:
                    pool.tensor_copy(k_s[:, j % 2, :, 0:SPAN], tokens(1, first)).then_inc(staged, 1)
                pool.tensor_copy(v_s[:, j % 2, :, :], tokens(2, first)).then_inc(staged, 1)

        def staged_after(j, wide):
            return 5 * j + 5 if wide else 4 * j + (4 + PAIRED)

        @block.scalar
        def _(act):
            def neg_at(slot, hh, g):
                return o_sb[:, slot, NEG + 2 * g + hh:NEG + 2 * g + hh + 1]

            def exps(j, slot, wide, g, fresh):
                width = (2 if wide else 1) * SPAN
                act.wait_ge(max_ready, GROUPS * j + (g + 1))
                if not fresh:
                    act.wait_ge(pt_done, GROUPS * j + (g - 2))
                for hh in range(2):
                    ins = act.activation(probs[:, g, hh * width:(hh + 1) * width], s_bank[g][:, hh * width:(hh + 1) * width],
                                         ACT.Exp, bias=neg_at(slot, hh, g))
                ins.then_inc(probs_ready, 1)

            def turned_odd(j, slot, wide, fresh):
                n = (4 if wide else 2) * SPAN
                act.wait_ge(pt_done, GROUPS * j + 2)
                if not fresh:
                    act.wait_ge(o_done, j)
                act.activation(probs_t[:, 1, 0:n], t_bank[(slot + 1) % 2][:, 0:n], ACT.Copy).then_inc(pt_odd, 1)

            def body(j, slot, wide, last_fresh=False):
                exps(j, slot, wide, 0, False)
                exps(j, slot, wide, 1, False)
                turned_odd(j - 1, 1 - slot, wide, last_fresh)
                exps(j, slot, wide, 2, False)

            for g in range(GROUPS):
                exps(0, 0, True, g, True)
            body(1, 1, True, True)
            with act.Fori(0, PAIRED // 2 - 1) as i:
                body(2 * i + 2, 0, True)
                body(2 * i + 3, 1, True)
            turned_odd(PAIRED - 1, 1, True, False)
            for g in range(GROUPS):
                exps(PAIRED, 0, False, g, False)
            body(PAIRED + 1, 1, False)
            with act.Fori(0, SINGLE // 2 - 1) as i:
                body(2 * i + (PAIRED + 2), 0, False)
                body(2 * i + (PAIRED + 3), 1, False)
            turned_odd(PAIRED + SINGLE - 1, 1, False, False)

        @block.vector
        def _(dve):
            dve.sem_inc(roped, 2)
            dve.sem_inc(times_sin, 2)
            for slot in range(2):
                dve.memset(v_tok[:, slot, :, :], 1.0).then_inc(v_ready, 1)
            with dve.Fori(0, BLOCKS) as i:
                for m in range(2 * GROUPS):
                    n = 2 * GROUPS * i + m
                    at = bass.ds(i * NB, NB)
                    dve.wait_ge(rotated, n + 1)
                    dve.wait_ge(roped, n + 1)
                    dve.tensor_tensor(rope_s[:, m % 2, :], s_bank[m % 2][:, :], cos_sin[:, 1, at], ALU.mult).then_inc(times_sin, 1)
                    dve.wait_ge(times_sin, n + 3)
                    dve.wait_ge(times_cos, n + 1)
                    dve.tensor_tensor(qkv[:, m // GROUPS, m % GROUPS, at], rope_c[:, m % 2, :], rope_s[:, m % 2, :],
                                      ALU.add).then_inc(roped, 1)

            def maxima(j, slot, wide, g, fresh):
                width = (2 if wide else 1) * SPAN
                dve.wait_ge(scores_ready, GROUPS * j + (g + 1))
                dve.tensor_reduce(o_sb[:, slot, NEG + 2 * g:NEG + 2 * g + 2],
                                  s_bank[g][:, 0:2 * width].rearrange("p (h k) -> p h k", h=2), AX.X, ALU.max,
                                  negate=True).then_inc(max_ready, 1)

            def turned_even(j, slot, wide, g, fresh):
                n = (4 if wide else 2) * SPAN
                dve.wait_ge(pt_done, GROUPS * j + (g + 1))
                if not fresh:
                    dve.wait_ge(o_done, j)
                dve.tensor_copy(probs_t[:, g, 0:n], t_bank[(slot + g) % 2][:, 0:n]).then_inc(pt_even, 1)

            def take_sums(j, slot):
                dve.wait_ge(o_done, j + 1)
                dve.tensor_copy(o_sb[:, slot, 0:NEG], o_bank[slot][:, 0:NEG]).then_inc(o_ready, 1)

            def take_v(j, slot):
                dve.wait_ge(vt_done, j + 1)
                dve.tensor_copy(v_tok[:, slot, :, 0:HD], v_bank[:, 0:HEADS * HD].rearrange("p (h d) -> p h d", h=HEADS)
                                ).then_inc(v_ready, 1)

            def start(j, slot, wide, fresh, uses):
                for g in range(GROUPS):
                    if g == 0 and uses:
                        dve.wait_ge(stored[slot], uses)
                    maxima(j, slot, wide, g, True)
                take_v(j, slot)

            def body(j, slot, wide, uses, last_fresh=False):
                if uses is not None:
                    dve.wait_ge(stored[slot], uses)
                maxima(j, slot, wide, 0, True)
                turned_even(j - 1, 1 - slot, wide, 0, last_fresh)
                maxima(j, slot, wide, 1, True)
                maxima(j, slot, wide, 2, True)
                turned_even(j - 1, 1 - slot, wide, 2, last_fresh)
                take_sums(j - 1, 1 - slot)
                take_v(j, slot)

            def finish(j, slot, wide):
                turned_even(j, slot, wide, 0, False)
                turned_even(j, slot, wide, 2, False)
                take_sums(j, slot)

            dve.wait_ge(v_ready, 2)
            start(0, 0, True, True, None)
            body(1, 1, True, None, True)
            with dve.Fori(0, PAIRED // 2 - 1) as i:
                body(2 * i + 2, 0, True, 16 * (i + 1))
                body(2 * i + 3, 1, True, 16 * (i + 1))
            finish(PAIRED - 1, 1, True)
            start(PAIRED, 0, False, False, 16 * (PAIRED // 2))
            body(PAIRED + 1, 1, False, 16 * (PAIRED // 2))
            with dve.Fori(0, SINGLE // 2 - 1) as i:
                body(2 * i + (PAIRED + 2), 0, False, 16 * (i + (PAIRED // 2 + 1)))
                body(2 * i + (PAIRED + 3), 1, False, 16 * (i + (PAIRED // 2 + 1)))
            finish(PAIRED + SINGLE - 1, 1, False)

        @block.tensor
        def _(pe):
            pe.wait_ge(consts_in, 16 * 6)
            pe.wait_ge(q_in, 16)
            pe.wait_ge(k_in, 16)
            with pe.Fori(0, BLOCKS) as i:
                for m in range(2 * GROUPS):
                    pe.wait_ge(times_sin, 2 * GROUPS * i + (m + 1))
                    pe.matmul(s_bank[m % 2][:, :], rot_w[:, :], qkv[:, m // GROUPS, m % GROUPS, bass.ds(i * NB, NB)],
                              start=True, stop=True).then_inc(rotated, 1)
            pe.wait_ge(times_sin, 2 + 2 * GROUPS * BLOCKS)

            def turn_v(j, slot, wide):
                pe.wait_ge(staged, staged_after(j, wide))
                pe.wait_ge(v_ready, j + 2)
                for g in range(GROUPS):
                    ins = pe.transpose(v_bank[:, g * SPAN:(g + 1) * SPAN], v_s[:, slot, g, :], idf[:, :])
                ins.then_inc(vt_done, 1)

            def scores(j, slot, wide, g, fresh):
                width = (2 if wide else 1) * SPAN
                if not fresh:
                    pe.wait_ge(probs_ready, GROUPS * j + (g - 2))
                if wide:
                    at = mask[:, bass.ds(j, 1), :] if not isinstance(j, int) else mask[:, j:j + 1, :]
                else:
                    at = mask[:, 1:2, SPAN:2 * SPAN]
                for hh in range(2):
                    pe.matmul(s_bank[g][:, hh * width:(hh + 1) * width], idb[:, :], at.rearrange("p o k -> p (o k)"),
                              start=(hh == 0), stop=False, skip_group_check=True)
                for hh in range(2):
                    ins = pe.matmul(s_bank[g][:, hh * width:(hh + 1) * width], q_s[:, slot, g, hh, :],
                                    k_s[:, slot, g, 0:width], start=False, stop=(hh == 1), skip_group_check=True)
                ins.then_inc(scores_ready, 1)

            def turn_probs(j, slot, wide, g, fresh):
                pe.wait_ge(probs_ready, GROUPS * j + (g + 1))
                if g == 2:
                    pe.wait_ge(pt_even, 2 * j + 1)
                elif not fresh:
                    pe.wait_ge(pt_odd, j) if g == 0 else pe.wait_ge(pt_even, 2 * j)
                for c in range(4 if wide else 2):
                    ins = pe.transpose(t_bank[(slot + g) % 2][:, c * SPAN:(c + 1) * SPAN],
                                       probs[:, g, c * SPAN:(c + 1) * SPAN], idf[:, :])
                ins.then_inc(pt_done, 1)

            def sums(j, slot, wide, g):
                if g == 1:
                    pe.wait_ge(pt_odd, j + 1)
                else:
                    pe.wait_ge(pt_even, 2 * j + (1 if g == 0 else 2))
                if g == 0:
                    pe.wait_ge(v_ready, j + 3)
                for hh in range(2):
                    h = 2 * g + hh
                    out = o_bank[slot][:, h * OW:(h + 1) * OW]
                    if wide:
                        pe.matmul(out, probs_t[:, g, 2 * hh * SPAN:(2 * hh + 1) * SPAN], v_tok[:, 1 - slot, h, :], start=True, stop=False)
                        ins = pe.matmul(out, probs_t[:, g, (2 * hh + 1) * SPAN:(2 * hh + 2) * SPAN], v_tok[:, slot, h, :], start=False, stop=True)
                    else:
                        ins = pe.matmul(out, probs_t[:, g, hh * SPAN:(hh + 1) * SPAN], v_tok[:, slot, h, :], start=True, stop=True)
                if g == GROUPS - 1:
                    ins.then_inc(o_done, 1)

            def body(j, slot, wide, last_fresh=False):
                turn_v(j, slot, wide)
                for g in range(GROUPS):
                    scores(j, slot, wide, g, False)
                    turn_probs(j - 1, 1 - slot, wide, g, last_fresh)
                    if g:
                        sums(j - 1, 1 - slot, wide, g - 1)
                sums(j - 1, 1 - slot, wide, GROUPS - 1)

            def start(j, slot, wide, fresh):
                turn_v(j, slot, wide)
                for g in range(GROUPS):
                    scores(j, slot, wide, g, fresh)

            def finish(j, slot, wide):
                for g in range(GROUPS):
                    turn_probs(j, slot, wide, g, False)
                    if g:
                        sums(j, slot, wide, g - 1)
                sums(j, slot, wide, GROUPS - 1)

            start(0, 0, True, True)
            body(1, 1, True, True)
            with pe.Fori(0, PAIRED // 2 - 1) as i:
                body(2 * i + 2, 0, True)
                body(2 * i + 3, 1, True)
            finish(PAIRED - 1, 1, True)
            start(PAIRED, 0, False, False)
            body(PAIRED + 1, 1, False)
            with pe.Fori(0, SINGLE // 2 - 1) as i:
                body(2 * i + (PAIRED + 2), 0, False)
                body(2 * i + (PAIRED + 3), 1, False)
            finish(PAIRED + SINGLE - 1, 1, False)
GH = 4
DK = 48
DV = 96
GP = GH // 2
CH = 128
CHUNKS = NB // CH
RANK = 16
TEMP = 16.0
LIMIT = 80.0 * TEMP
AW = GH * DV


def gated_linear_attention(nc, proj_t, gate_w, gate_b, chunk_starts, causal, ident, norm_gain, mix_t):
    with ExitStack() as ctx:
        used = []
        ctx.callback(free_semaphores, nc, used)

        def sb(name, shape, dt=F32):
            return ctx.enter_context(nc.sbuf_tensor("gl_" + name, shape, dt))

        def sem(name):
            used.append(nc.alloc_semaphore("gl_" + name))
            return used[-1]

        q_in = sb("q_in", [P, 2, GP, NB])
        k_in = sb("k_in", [P, 2, GP, NB])
        v_in = sb("v_in", [P, 2, 3, NB])
        low_rank = sb("low_rank", [RANK, 2, NB])
        w_gate = sb("w_gate", [RANK, GP, P])
        b_gate = sb("b_gate", [P, GP])
        starts = sb("starts", [P, NB])
        keep = sb("keep", [P, 2, CH], mybir.dt.uint32)
        idf = sb("idf", [P, P])
        gain = sb("gain", [P, 3])
        eps = sb("eps", [P, 1])
        z = sb("z", [P, GP, NB])
        z_abs = sb("z_abs", [P, GP, NB])
        log_g = sb("log_g", [P, GP, NB])
        cum = sb("cum", [P, GP, NB])
        to_mid = sb("to_mid", [P, GP, NB])
        to_end = sb("to_end", [P, GP, NB])
        to_border = sb("to_border", [P, GP, NB])
        e_mid = sb("e_mid", [P, GP, NB])
        e_mid_inv = sb("e_mid_inv", [P, GP, NB])
        e_cum = sb("e_cum", [P, GP, NB])
        q_mid = sb("q_mid", [P, GP, NB])
        k_mid = sb("k_mid", [P, GP, NB])
        q_start = sb("q_start", [P, GP, NB])
        k_end = sb("k_end", [P, GP, NB])
        qk_border = sb("qk_border", [P, GP, NB])
        v_tok = sb("v_tok", [P, 2, AW])
        k_tok = sb("k_tok", [P, 2, GP, P])
        scores = sb("scores", [P, 2, GH, CH])
        state = sb("state", [P, 2, GP, DV])
        o_all = sb("o_all", [P, S // CH, AW])
        square = sb("square", [P, AW * 4])
        ss = sb("ss", [P, S // CH * GH])
        rstd = sb("rstd", [P, S // CH * GH])
        o_n = sb("o_n", [P, CHUNKS, AW])
        gate_r = sb("gate_r", [P, 3, S])

        def bank(name):
            return ctx.enter_context(nc.psum_tensor("gl_bank_" + name, [P, NB], F32))

        z_bank, v_bank, k_bank, st_bank = bank("z"), bank("v"), bank("k"), bank("st")
        s_bank = [bank(f"s{i}") for i in range(2)]
        o_bank = [bank(f"o{i}") for i in range(2)]

        consts_in = sem("consts_in")
        zeroed = sem("zeroed")
        loaded = [sem(f"loaded{i}") for i in range(2)]
        r_loaded = sem("r_loaded")
        z_ready = sem("z_ready")
        z_copied = sem("z_copied")
        z_abs_ready = sem("z_abs_ready")
        act_step = sem("act_step")
        dve_step = sem("dve_step")
        exps_ready = sem("exps_ready")
        factors_ready = sem("factors_ready")
        turned = sem("turned")
        tok_ready = sem("tok_ready")
        scores_done = sem("scores_done")
        scores_ready = sem("scores_ready")
        update_done = sem("update_done")
        state_ready = sem("state_ready")
        o_done = sem("o_done")
        o_ready = sem("o_ready")
        silu_ready = sem("silu_ready")
        gated_ready = sem("gated_ready")
        ss_ready = sem("ss_ready")
        rms_ready = sem("rms_ready")
        rstd_ready = sem("rstd_ready")
        o_n_ready = sem("o_n_ready")
        o_turned = sem("o_turned")
        out_ready = sem("out_ready")
        stored = sem("stored")

        block = ctx.enter_context(nc.Block())
        PRE = 8
        LOADS = 4

        def col(chunk, lo=0, hi=CH):
            return slice(chunk * CH + lo, chunk * CH + hi)

        @block.sync
        def _(sp):
            for dst, src in ((w_gate[:, :, :], gate_w), (b_gate[:, :], gate_b), (starts[:, :], chunk_starts),
                             (keep[:, :, :], causal), (idf[:, :], ident), (gain[:, :], norm_gain)):
                sp.dma_start(dst, src).then_inc(consts_in, 16)

            def load(n, p):
                at = bass.ds(n * NB, NB)
                sp.dma_start(q_in[:, p, :, :], proj_t[T_AQ:T_AQ + 2, :, at].rearrange("g p s -> p g s")).then_inc(loaded[p], 16)
                sp.dma_start(low_rank[:, p, :], proj_t[T_AQ, GLR_ROW:GLR_ROW + RANK, at]).then_inc(loaded[p], 16)
                sp.dma_start(k_in[:, p, :, :], proj_t[T_AK:T_AK + 2, :, at].rearrange("g p s -> p g s")).then_inc(loaded[p], 16)
                sp.dma_start(v_in[:, p, :, :], proj_t[T_AV:T_AV + 3, :, at].rearrange("g p s -> p g s")).then_inc(loaded[p], 16)

            load(0, 0)
            load(1, 1)
            sp.dma_start(gate_r[:, :, :], proj_t[T_AR:T_AR + 3].rearrange("g p s -> p g s")).then_inc(r_loaded, 16)
            for n in range(2, BLOCKS):
                sp.wait_ge(factors_ready, n - 1)
                sp.wait_ge(turned, CHUNKS * (n - 1))
                load(n, n % 2)
            for n in range(BLOCKS):
                sp.wait_ge(out_ready, 3 * (n + 1))
                sp.dma_start(mix_t[0:3, :, n * NB:(n + 1) * NB].rearrange("g p s -> p g s"), gate_r[:, :, n * NB:(n + 1) * NB]
                             ).then_inc(stored, 16)
            sp.wait_ge(stored, 16 * BLOCKS)

        @block.tensor
        def _(pe):
            pe.wait_ge(consts_in, 16 * 6)

            def gate(n, p):
                pe.wait_ge(loaded[p], 16 * LOADS * (n // 2 + 1))
                for m in range(GP):
                    u = GP * n + m
                    if u:
                        pe.wait_ge(z_copied, u)
                    pe.matmul(z_bank[:, :], w_gate[:, m, :], low_rank[:, p, :], start=True, stop=True).then_inc(z_ready, 1)

            def turn(c, chunk, p):
                if c:
                    pe.wait_ge(tok_ready, c)
                for g in range(3):
                    pe.transpose(v_bank[:, g * P:(g + 1) * P], v_in[:, p, g, col(chunk)], idf[:, :])
                for m in range(GP):
                    ins = pe.transpose(k_bank[:, m * P:(m + 1) * P], k_end[:, m, col(chunk)], idf[:, :])
                ins.then_inc(turned, 1)

            def inner(c, chunk):
                if c:
                    pe.wait_ge(scores_ready, c)
                for h in range(GH):
                    m, b = h // 2, h % 2
                    rows = slice(64 * b, 64 * b + DK)
                    at = m * CH
                    pe.matmul(s_bank[b][0:64, at:at + 64], k_mid[rows, m, col(chunk, 0, 64)], q_mid[rows, m, col(chunk, 0, 64)],
                              start=True, stop=True)
                    pe.matmul(s_bank[b][64:128, at + 64:at + 128], k_mid[rows, m, col(chunk, 64)], q_mid[rows, m, col(chunk, 64)],
                              start=True, stop=True)
                    ins = pe.matmul(s_bank[b][0:64, at + 64:at + 128], qk_border[rows, m, col(chunk, 0, 64)],
                                    qk_border[rows, m, col(chunk, 64)], start=True, stop=True)
                ins.then_inc(scores_done, 1)

            def update(c):
                pe.wait_ge(tok_ready, c + 1)
                if c:
                    pe.wait_ge(state_ready, c)
                for h in range(GH):
                    m, b = h // 2, h % 2
                    ins = pe.matmul(st_bank[64 * b:64 * b + 64, m * DV:(m + 1) * DV], k_tok[:, c % 2, m, 64 * b:64 * b + 64],
                                    v_tok[:, c % 2, h * DV:(h + 1) * DV], start=True, stop=True)
                ins.then_inc(update_done, 1)

            def output(c, chunk):
                pe.wait_ge(scores_ready, c + 1)
                if c:
                    pe.wait_ge(o_ready, c)
                    pe.wait_ge(state_ready, c)
                for m in range(GP):
                    for b in range(2):
                        h = 2 * m + b
                        out = o_bank[b][:, m * DV:(m + 1) * DV]
                        pe.matmul(out, scores[:, c % 2, h, :], v_tok[:, c % 2, h * DV:(h + 1) * DV], start=True, stop=False)
                        ins = pe.matmul(out, q_start[64 * b:64 * b + DK, m, col(chunk)], state[64 * b:64 * b + DK, c % 2, m, :],
                                        start=False, stop=True)
                ins.then_inc(o_done, 1)

            pe.wait_ge(zeroed, 3)
            gate(0, 0)
            for n in range(BLOCKS):
                pe.wait_ge(factors_ready, n + 1)
                for chunk in range(CHUNKS):
                    c = CHUNKS * n + chunk
                    turn(c, chunk, n % 2)
                    inner(c, chunk)
                    if chunk == 0 and n + 1 < BLOCKS:
                        gate(n + 1, (n + 1) % 2)
                    update(c)
                    output(c, chunk)

            for n in range(BLOCKS):
                for t in range(CHUNKS):
                    pe.wait_ge(o_n_ready, CHUNKS * n + t + 1)
                    for g in range(3):
                        if t == 0 and n:
                            pe.wait_ge(out_ready, 3 * (n - 1) + g + 1)
                        ins = pe.transpose([v_bank, k_bank, st_bank][g][:, t * CH:(t + 1) * CH], o_n[:, t, g * P:(g + 1) * P], idf[:, :])
                    ins.then_inc(o_turned, 1)

        @block.scalar
        def _(act):
            act.wait_ge(consts_in, 16 * 6)

            def gate(n):
                for m in range(GP):
                    u = GP * n + m
                    act.wait_ge(z_ready, u + 1)
                    if n:
                        act.wait_ge(dve_step, PRE * (n - 1) + 1)
                    act.activation(z[:, m, :], z_bank[:, :], ACT.Identity, bias=b_gate[:, m:m + 1]).then_inc(z_copied, 1)
                act.wait_ge(z_copied, GP * (n + 1))
                act.activation(z_abs[:, :, :], z[:, :, :], ACT.Abs).then_inc(z_abs_ready, 1)
                act.wait_ge(z_abs_ready, n + 1)
                act.activation(z_abs[:, :, :], z_abs[:, :, :], ACT.Exp, scale=-1.0).then_inc(act_step, 1)
                act.wait_ge(act_step, 2 * n + 1)
                act.activation(z_abs[:, :, :], z_abs[:, :, :], ACT.Ln, bias=1.0).then_inc(act_step, 1)

            def exps(n):
                if n:
                    act.wait_ge(state_ready, CHUNKS * n)
                    act.wait_ge(factors_ready, n)
                act.wait_ge(dve_step, PRE * n + 3)
                act.activation(e_cum[:, :, :], cum[:, :, :], ACT.Exp, scale=1.0 / TEMP).then_inc(exps_ready, 1)
                act.wait_ge(dve_step, PRE * n + 5)
                act.activation(e_mid[:, :, :], to_mid[:, :, :], ACT.Exp, scale=1.0 / TEMP).then_inc(exps_ready, 1)
                act.activation(e_mid_inv[:, :, :], to_mid[:, :, :], ACT.Exp, scale=-1.0 / TEMP).then_inc(exps_ready, 1)
                act.wait_ge(dve_step, PRE * n + 8)
                act.activation(to_end[:, :, :], to_end[:, :, :], ACT.Exp, scale=1.0 / TEMP).then_inc(exps_ready, 1)
                act.activation(to_border[:, :, :], to_border[:, :, :], ACT.Exp, scale=1.0 / TEMP).then_inc(exps_ready, 1)

            def tokens(c):
                act.wait_ge(turned, c + 1)
                if c >= 2:
                    act.wait_ge(o_done, c - 1)
                act.activation(v_tok[:, c % 2, :], v_bank[:, 0:AW], ACT.Copy)
                act.activation(k_tok[:, c % 2, :, :], k_bank[:, 0:GP * P].rearrange("p (m k) -> p m k", m=GP), ACT.Copy
                               ).then_inc(tok_ready, 1)

            def output(c):
                act.wait_ge(o_done, c + 1)
                for b in range(2):
                    ins = act.activation(o_all[:, c, :].rearrange("p (m b v) -> p m b v", m=GP, b=2)[:, :, b, :],
                                         o_bank[b][:, 0:GP * DV].rearrange("p (m v) -> p m v", m=GP), ACT.Copy)
                ins.then_inc(o_ready, 1)

            gate(0)
            exps(0)
            for n in range(BLOCKS):
                for chunk in range(CHUNKS):
                    c = CHUNKS * n + chunk
                    tokens(c)
                    if chunk == 0 and n + 1 < BLOCKS:
                        gate(n + 1)
                    output(c)
                if n + 1 < BLOCKS:
                    exps(n + 1)
            act.wait_ge(r_loaded, 16)
            for g in range(3):
                act.activation(gate_r[:, g, :], gate_r[:, g, :], ACT.Silu).then_inc(silu_ready, 1)
            act.wait_ge(ss_ready, S // CH // 4)
            act.activation(rstd[:, :], ss[:, :], ACT.Sqrt, bias=eps[:, :], scale=1.0 / DV).then_inc(rms_ready, 1)

        @block.vector
        def _(dve):
            dve.memset(scores[:, :, :, :], 0.0).then_inc(zeroed, 1)
            dve.memset(state[:, 0, :, :], 0.0).then_inc(zeroed, 1)
            dve.memset(eps[:, :], EPS).then_inc(zeroed, 1)
            dve.wait_ge(zeroed, 3)
            dve.wait_ge(consts_in, 16 * 6)

            def halves(x):
                return x[:, :, :].rearrange("p m (c j) -> p (m c) j", j=64)

            def chunked(x):
                return x[:, :, :].rearrange("p m (c j) -> p (m c) j", j=CH)

            def decays(n):
                dve.wait_ge(act_step, 2 * n + 2)
                if n:
                    dve.wait_ge(exps_ready, 5 * n)
                    dve.wait_ge(dve_step, PRE * n)
                dve.scalar_tensor_tensor(out=log_g[:, :, :], in0=z[:, :, :], scalar=0.0, in1=z_abs[:, :, :], op0=ALU.min,
                                         op1=ALU.subtract).then_inc(dve_step, 1)
                dve.wait_ge(dve_step, PRE * n + 1)
                for m in range(GP):
                    dve.tensor_tensor_scan(cum[:, m, :], starts[:, :], log_g[:, m, :], 0.0, ALU.mult, ALU.add).then_inc(dve_step, 1)
                dve.wait_ge(dve_step, PRE * n + 3)
                mid = halves(cum)[:, :, 31:32].to_broadcast([P, GP * NB // 64, 64])
                dve.tensor_tensor(halves(to_mid), halves(cum), mid, ALU.subtract).then_inc(dve_step, 1)
                dve.wait_ge(dve_step, PRE * n + 4)
                dve.tensor_scalar(to_mid[:, :, :], to_mid[:, :, :], LIMIT, -LIMIT, ALU.min, ALU.max).then_inc(dve_step, 1)
                if n:
                    dve.wait_ge(factors_ready, n)
                end = chunked(cum)[:, :, CH - 1:CH].to_broadcast([P, GP * CHUNKS, CH])
                dve.tensor_tensor(chunked(to_end), end, chunked(cum), ALU.subtract).then_inc(dve_step, 1)
                border = chunked(cum)[:, :, 63:64].to_broadcast([P, GP * CHUNKS, 64])
                dve.tensor_tensor(chunked(to_border)[:, :, 0:64], border, chunked(cum)[:, :, 0:64], ALU.subtract).then_inc(dve_step, 1)
                dve.tensor_tensor(chunked(to_border)[:, :, 64:CH], chunked(cum)[:, :, 64:CH], border, ALU.subtract).then_inc(dve_step, 1)

            def factors(n, p):
                if n:
                    dve.wait_ge(o_done, CHUNKS * n)
                dve.wait_ge(loaded[p], 16 * LOADS * (n // 2 + 1))
                q, k = q_in[:, p, :, :], k_in[:, p, :, :]
                scale = DK ** -0.5

                def scaled(out, x, e):
                    return dve.scalar_tensor_tensor(out=out, in0=x, scalar=scale, in1=e, op0=ALU.mult, op1=ALU.mult)

                dve.wait_ge(exps_ready, 5 * n + 1)
                scaled(q_start[:, :, :], q, e_cum[:, :, :])
                dve.wait_ge(exps_ready, 5 * n + 2)
                scaled(q_mid[:, :, :], q, e_mid[:, :, :])
                dve.wait_ge(exps_ready, 5 * n + 3)
                dve.tensor_tensor(k_mid[:, :, :], k, e_mid_inv[:, :, :], ALU.mult)
                dve.wait_ge(exps_ready, 5 * n + 4)
                dve.tensor_tensor(k_end[:, :, :], k, to_end[:, :, :], ALU.mult)
                dve.wait_ge(exps_ready, 5 * n + 5)
                kc = k.rearrange("p m (c j) -> p (m c) j", j=CH)
                qc = q.rearrange("p m (c j) -> p (m c) j", j=CH)
                dve.tensor_tensor(chunked(qk_border)[:, :, 0:64], kc[:, :, 0:64], chunked(to_border)[:, :, 0:64], ALU.mult)
                scaled(chunked(qk_border)[:, :, 64:CH], qc[:, :, 64:CH], chunked(to_border)[:, :, 64:CH]).then_inc(factors_ready, 1)

            def mask(c):
                dve.wait_ge(scores_done, c + 1)
                if c >= 2:
                    dve.wait_ge(o_done, c - 1)
                for b in range(2):
                    sc = scores[:, c % 2, :, :].rearrange("p (m b) i -> p m b i", b=2)[:, :, b, :]
                    ps = s_bank[b][:, 0:GP * CH].rearrange("p (m i) -> p m i", m=GP)
                    dve.copy_predicated(sc[0:64], keep[0:64, :, :], ps[0:64])
                    ins = dve.copy_predicated(sc[64:128, :, 64:CH], keep[64:128, :, 64:CH], ps[64:128, :, 64:CH])
                ins.then_inc(scores_ready, 1)

            def advance(c, chunk):
                dve.wait_ge(update_done, c + 1)
                if c:
                    dve.wait_ge(state_ready, c)
                    dve.wait_ge(o_done, c)
                for m in range(GP):
                    ins = dve.scalar_tensor_tensor(out=state[:, (c + 1) % 2, m, :], in0=state[:, c % 2, m, :],
                                                   scalar=e_cum[:, m, (chunk + 1) * CH - 1:(chunk + 1) * CH],
                                                   in1=st_bank[:, m * DV:(m + 1) * DV], op0=ALU.mult, op1=ALU.add)
                ins.then_inc(state_ready, 1)

            decays(0)
            factors(0, 0)
            for n in range(BLOCKS):
                for chunk in range(CHUNKS):
                    c = CHUNKS * n + chunk
                    mask(c)
                    advance(c, chunk)
                    if chunk == CHUNKS - 2 and n + 1 < BLOCKS:
                        decays(n + 1)
                if n + 1 < BLOCKS:
                    factors(n + 1, (n + 1) % 2)
            dve.wait_ge(silu_ready, 3)
            for g in range(3):
                dve.tensor_scalar(gate_r[:, g, :], gate_r[:, g, :], gain[:, g:g + 1], None, ALU.mult).then_inc(gated_ready, 1)
            for t in range(S // CH // 4):
                dve.wait_ge(o_ready, 4 * (t + 1))
                if t:
                    dve.wait_ge(ss_ready, t)
                o4 = o_all[:, 4 * t:4 * t + 4, :].rearrange("p c v -> p (c v)")
                dve.tensor_tensor(square[:, :], o4, o4, ALU.mult).then_inc(dve_step, 1)
                dve.wait_ge(dve_step, PRE * BLOCKS + t + 1)
                dve.tensor_reduce(ss[:, 4 * GH * t:4 * GH * (t + 1)], square[:, :].rearrange("p (h v) -> p h v", v=DV), AX.X,
                                  ALU.add).then_inc(ss_ready, 1)
            dve.wait_ge(rms_ready, 1)
            dve.reciprocal(rstd[:, :], rstd[:, :]).then_inc(rstd_ready, 1)
            dve.wait_ge(rstd_ready, 1)
            dve.wait_ge(gated_ready, 3)
            for n in range(BLOCKS):
                for t in range(CHUNKS):
                    c = CHUNKS * n + t
                    if n:
                        dve.wait_ge(o_turned, CHUNKS * (n - 1) + t + 1)
                    dve.tensor_tensor(o_n[:, t, :].rearrange("p (h v) -> p h v", v=DV), o_all[:, c, :].rearrange("p (h v) -> p h v", v=DV),
                                      rstd[:, GH * c:GH * (c + 1)].unsqueeze(2).to_broadcast([P, GH, DV]), ALU.mult).then_inc(o_n_ready, 1)
                dve.wait_ge(o_turned, CHUNKS * (n + 1))
                for g in range(3):
                    at = gate_r[:, g, n * NB:(n + 1) * NB]
                    dve.tensor_tensor(at, [v_bank, k_bank, st_bank][g][:, :], at, ALU.mult).then_inc(out_ready, 1)


LW = 256
LT = LW // P
LTAPS = 4
C_TAP, C_BIAS, C_BA, C_BX, C_LAM, C_NORM = 0, 4, 5, 6, 7, 8


def recurrent_branch(nc, proj_t, consts, gate_w, mix_t):
    with ExitStack() as ctx:
        used = []
        ctx.callback(free_semaphores, nc, used)

        def sb(name, shape, dt=F32):
            return ctx.enter_context(nc.sbuf_tensor("lr_" + name, shape, dt))

        def sem(name):
            used.append(nc.alloc_semaphore("lr_" + name))
            return used[-1]

        x_in = sb("x_in", [P, LT, LTAPS - 1 + S])
        gate = sb("gate", [P, LT, S])
        xc = sb("xc", [P, LT, S])
        r = sb("r", [P, LT, S])
        i_x = sb("i_x", [P, LT, S])
        root = sb("root", [P, LT, S])
        a2 = sb("a2", [P, LT, S])
        rstd = sb("rstd", [P, S])
        c = sb("c", [P, LT, C_NORM + 1])
        w = sb("w", [P, LT, 2, P])
        sp8 = sb("sp8", [P, LT, 4])
        ones = sb("ones", [P, P])
        eps = sb("eps", [P, 1])
        banks = [ctx.enter_context(nc.psum_tensor(f"lr_bank{i}", [P, NB], F32)) for i in range(8)]

        consts_in = sem("consts_in")
        x_loaded = sem("x_loaded")
        gate_loaded = sem("gate_loaded")
        zeroed = sem("zeroed")
        small = sem("small")
        small_act = sem("small_act")
        conv_step = sem("conv_step")
        gates_done = sem("gates_done")
        gates_ready = sem("gates_ready")
        tanh_ready = sem("tanh_ready")
        a_ready = sem("a_ready")
        a2_ready = sem("a2_ready")
        power_ready = sem("power_ready")
        root_ready = sem("root_ready")
        ix_ready = sem("ix_ready")
        u_ready = sem("u_ready")
        h_ready = sem("h_ready")
        gelu_ready = sem("gelu_ready")
        hg_ready = sem("hg_ready")
        sq_ready = sem("sq_ready")
        sums_done = sem("sums_done")
        std_ready = sem("std_ready")
        rstd_ready = sem("rstd_ready")
        out_ready = sem("out_ready")
        stored = sem("stored")

        block = ctx.enter_context(nc.Block())

        @block.sync
        def _(sp):
            sp.dma_start(c[:, :, :], consts).then_inc(consts_in, 16)
            sp.dma_start(w[:, :, :, :], gate_w).then_inc(consts_in, 16)
            sp.dma_start(x_in[:, :, LTAPS - 1:], proj_t[T_BI:T_BI + LT].rearrange("g p s -> p g s")).then_inc(x_loaded, 16)
            sp.dma_start(gate[:, :, :], proj_t[T_BG:T_BG + LT].rearrange("g p s -> p g s")).then_inc(gate_loaded, 16)
            for m in range(LT):
                sp.wait_ge(out_ready, m + 1)
                sp.dma_start(mix_t[3 + m], i_x[:, m, :]).then_inc(stored, 16)
            sp.wait_ge(stored, 16 * LT)

        @block.vector
        def _(dve):
            dve.memset(x_in[:, :, 0:LTAPS - 1], 0.0).then_inc(zeroed, 1)
            dve.memset(ones[:, :], 1.0).then_inc(zeroed, 1)
            dve.memset(eps[:, :], EPS).then_inc(zeroed, 1)
            dve.wait_ge(zeroed, 3)
            dve.wait_ge(consts_in, 32)
            dve.wait_ge(x_loaded, 16)
            for m in range(LT):
                dve.tensor_scalar(xc[:, m, :], x_in[:, m, LTAPS - 1:], c[:, m, LTAPS - 1:LTAPS], c[:, m, C_BIAS:C_BIAS + 1],
                                  ALU.mult, ALU.add).then_inc(conv_step, 1)
            for t in range(LTAPS - 1):
                for m in range(LT):
                    dve.wait_ge(conv_step, LT * t + m + 1)
                    dve.scalar_tensor_tensor(out=xc[:, m, :], in0=x_in[:, m, t:t + S], scalar=c[:, m, t:t + 1], in1=xc[:, m, :],
                                             op0=ALU.mult, op1=ALU.add).then_inc(conv_step, 1)
            dve.wait_ge(small_act, 3)
            dve.tensor_scalar(sp8[:, :, 2:3], c[:, :, C_LAM:C_LAM + 1], -1.0, 0.0, ALU.mult, ALU.max).then_inc(small, 1)
            dve.wait_ge(small, 1)
            dve.tensor_tensor(sp8[:, :, 1:2], sp8[:, :, 1:2], sp8[:, :, 2:3], ALU.add).then_inc(small, 1)
            dve.wait_ge(small, 2)
            dve.tensor_scalar(sp8[:, :, 2:3], sp8[:, :, 1:2], 8.0, None, ALU.mult).then_inc(small, 1)
            dve.tensor_scalar(sp8[:, :, 3:4], sp8[:, :, 1:2], -8.0, None, ALU.mult).then_inc(small, 1)
            for m in range(LT):
                dve.wait_ge(a2_ready, m + 1)
                dve.wait_ge(tanh_ready, m + 1)
                dve.scalar_tensor_tensor(out=root[:, m, :], in0=a2[:, m, :], scalar=1.0, in1=root[:, m, :], op0=ALU.add,
                                         op1=ALU.mult).then_inc(power_ready, 1)
            for m in range(LT):
                dve.wait_ge(root_ready, m + 1)
                dve.wait_ge(ix_ready, m + 1)
                dve.tensor_tensor(root[:, m, :], root[:, m, :], i_x[:, m, :], ALU.mult).then_inc(u_ready, 1)
                dve.wait_ge(u_ready, m + 1)
                dve.tensor_tensor_scan(xc[:, m, :], r[:, m, :], root[:, m, :], 0.0, ALU.mult, ALU.add).then_inc(h_ready, 1)
                dve.wait_ge(h_ready, m + 1)
                dve.wait_ge(gelu_ready, m + 1)
                dve.tensor_tensor(xc[:, m, :], xc[:, m, :], gate[:, m, :], ALU.mult).then_inc(hg_ready, 1)
            for b in range(BLOCKS):
                at = slice(b * NB, (b + 1) * NB)
                dve.wait_ge(std_ready, b + 1)
                dve.reciprocal(rstd[:, at], rstd[:, at]).then_inc(rstd_ready, 1)
                dve.wait_ge(rstd_ready, b + 1)
                for m in range(LT):
                    ins = dve.scalar_tensor_tensor(out=i_x[:, m, at], in0=xc[:, m, at], scalar=c[:, m, C_NORM:C_NORM + 1], in1=rstd[:, at],
                                                   op0=ALU.mult, op1=ALU.mult)
            ins.then_inc(out_ready, LT)

        @block.gpsimd
        def _(pool):
            for m in range(LT):
                pool.wait_ge(gates_ready, 2 * BLOCKS * (m + 1))
                pool.tensor_tensor(i_x[:, m, :], i_x[:, m, :], xc[:, m, :], ALU.mult).then_inc(ix_ready, 1)

        @block.scalar
        def _(act):
            act.wait_ge(consts_in, 32)
            act.activation(sp8[:, :, 0:1], c[:, :, C_LAM:C_LAM + 1], ACT.Abs).then_inc(small_act, 1)
            act.wait_ge(small_act, 1)
            act.activation(sp8[:, :, 0:1], sp8[:, :, 0:1], ACT.Exp, scale=-1.0).then_inc(small_act, 1)
            act.wait_ge(small_act, 2)
            act.activation(sp8[:, :, 1:2], sp8[:, :, 0:1], ACT.Ln, bias=1.0).then_inc(small_act, 1)
            for m in range(LT):
                for s, (out, bias) in enumerate(((r, C_BA), (i_x, C_BX))):
                    for b in range(BLOCKS):
                        n = (LT * m + s) * BLOCKS + b
                        act.wait_ge(gates_done, n + 1)
                        act.activation(out[:, m, b * NB:(b + 1) * NB], banks[n % 8][:, :], ACT.Sigmoid,
                                       bias=c[:, m, bias:bias + 1]).then_inc(gates_ready, 1)
            act.wait_ge(small, 4)
            act.wait_ge(gates_ready, 4 * BLOCKS)
            for m in range(LT):
                act.activation(root[:, m, :], r[:, m, :], ACT.Tanh, scale=sp8[:, m, 2:3]).then_inc(tanh_ready, 1)
                act.wait_ge(tanh_ready, m + 1)
                act.activation(r[:, m, :], r[:, m, :], ACT.Exp, scale=sp8[:, m, 3:4]).then_inc(a_ready, 1)
                act.wait_ge(a_ready, m + 1)
                act.activation(a2[:, m, :], r[:, m, :], ACT.Square).then_inc(a2_ready, 1)
            for m in range(LT):
                act.wait_ge(power_ready, m + 1)
                act.activation(root[:, m, :], root[:, m, :], ACT.Sqrt).then_inc(root_ready, 1)
            act.wait_ge(gate_loaded, 16)
            for m in range(LT):
                act.activation(gate[:, m, :], gate[:, m, :], ACT.Gelu_apprx_tanh).then_inc(gelu_ready, 1)
            act.wait_ge(power_ready, LT)
            for m in range(LT):
                act.wait_ge(hg_ready, m + 1)
                act.activation(a2[:, m, :], xc[:, m, :], ACT.Square).then_inc(sq_ready, 1)
            for b in range(BLOCKS):
                act.wait_ge(sums_done, b + 1)
                act.activation(rstd[:, b * NB:(b + 1) * NB], banks[b][:, :], ACT.Sqrt, bias=eps[:, :], scale=1.0 / LW).then_inc(std_ready, 1)

        @block.tensor
        def _(pe):
            pe.wait_ge(consts_in, 32)
            for m in range(LT):
                pe.wait_ge(conv_step, LT * (LTAPS - 1) + m + 1)
                for s in range(2):
                    for b in range(BLOCKS):
                        n = (LT * m + s) * BLOCKS + b
                        if n >= 8:
                            pe.wait_ge(gates_ready, n - 7)
                        pe.matmul(banks[n % 8][:, :], w[:, m, s, :], xc[:, m, b * NB:(b + 1) * NB], start=True, stop=True
                                  ).then_inc(gates_done, 1)
            pe.wait_ge(gates_ready, 4 * BLOCKS)
            pe.wait_ge(sq_ready, LT)
            for b in range(BLOCKS):
                for m in range(LT):
                    ins = pe.matmul(banks[b][:, :], ones[:, :], a2[:, m, b * NB:(b + 1) * NB], start=(m == 0), stop=(m == LT - 1))
                ins.then_inc(sums_done, 1)


def combine_patterns(nc, o_scratch, ident, norm_gain, mix_t):
    TILES_T = S // P
    PATS = len(DILATIONS)
    CW = HEADS * HD
    with ExitStack() as ctx:
        used = []
        ctx.callback(free_semaphores, nc, used)

        def sb(name, shape, dt=F32):
            return ctx.enter_context(nc.sbuf_tensor("cb_" + name, shape, dt))

        def sem(name):
            used.append(nc.alloc_semaphore("cb_" + name))
            return used[-1]

        rows = sb("rows", [P, 2, PATS, ROW])
        low = sb("low", [P, 2, HEADS])
        weight = sb("weight", [P, 2, PATS, HEADS])
        total = sb("total", [P, 2, HEADS, OW])
        o_all = sb("o_all", [P, TILES_T, CW])
        junk = sb("junk", [P, CW])
        ss = sb("ss", [P, TILES_T])
        rstd = sb("rstd", [P, TILES_T])
        o_n = sb("o_n", [P, 4, CW])
        out = sb("out", [P, 2, GROUPS, NB])
        idf = sb("idf", [P, P])
        gain = sb("gain", [P, GROUPS])
        eps = sb("eps", [P, 1])
        banks = [ctx.enter_context(nc.psum_tensor(f"cb_bank{i}", [P, NB], F32)) for i in range(2 * GROUPS)]

        consts_in = sem("consts_in")
        eps_ready = sem("eps_ready")
        loaded = [sem(f"loaded{i}") for i in range(2)]
        step = sem("step")
        low_ready = sem("low_ready")
        weight_ready = sem("weight_ready")
        rms_ready = sem("rms_ready")
        rstd_ready = sem("rstd_ready")
        o_n_ready = sem("o_n_ready")
        turned = sem("turned")
        out_ready = sem("out_ready")
        stored = [sem(f"stored{i}") for i in range(2)]
        STEPS = 12

        block = ctx.enter_context(nc.Block())

        @block.sync
        def _(sp):
            sp.dma_start(idf[:, :], ident).then_inc(consts_in, 16)
            sp.dma_start(gain[:, :], norm_gain).then_inc(consts_in, 16)
            for t in range(TILES_T):
                if t >= 2:
                    sp.wait_ge(step, STEPS * (t - 1))
                sp.dma_start(rows[:, t % 2, :, :], o_scratch[:, t * P:(t + 1) * P, :].rearrange("a p r -> p a r")
                             ).then_inc(loaded[t % 2], 16)
            for b in range(BLOCKS):
                sp.wait_ge(out_ready, GROUPS * (b + 1))
                sp.dma_start(mix_t[5:8, :, b * NB:(b + 1) * NB].rearrange("g p s -> p g s"), out[:, b % 2, :, :]).then_inc(stored[b % 2], 16)
            for p in range(2):
                sp.wait_ge(stored[p], 16 * BLOCKS // 2)

        @block.scalar
        def _(act):
            with act.Fori(0, TILES_T // 2) as i:
                for p in range(2):
                    act.wait_ge(low_ready, 2 * i + (p + 1))
                    act.activation(weight[:, p, :, :], weight[:, p, :, :], ACT.Exp).then_inc(weight_ready, 1)
            act.wait_ge(step, STEPS * TILES_T)
            act.wait_ge(eps_ready, 1)
            act.activation(rstd[:, :], ss[:, :], ACT.Sqrt, bias=eps[:, :], scale=1.0 / CW).then_inc(rms_ready, 1)
            act.wait_ge(consts_in, 32)
            for b in range(BLOCKS):
                if b >= 2:
                    act.wait_ge(stored[b % 2], 16 * (b // 2))
                act.wait_ge(turned, 4 * (b + 1))
                for g in range(GROUPS):
                    act.activation(out[:, b % 2, g, :], banks[GROUPS * (b % 2) + g][:, :], ACT.Copy, scale=gain[:, g:g + 1]
                                   ).then_inc(out_ready, 1)

        @block.vector
        def _(dve):
            dve.memset(eps[:, :], EPS).then_inc(eps_ready, 1)

            def combine(t, p, use):
                def done(ins, count):
                    ins.then_inc(step, 1)
                    dve.wait_ge(step, STEPS * t + count)

                dve.wait_ge(loaded[p], 16 * (use + 1))
                neg = [rows[:, p, a, NEG:NEG + HEADS] for a in range(PATS)]
                done(dve.tensor_tensor(low[:, p, :], neg[0], neg[1], ALU.min), 1)
                done(dve.tensor_tensor(low[:, p, :], low[:, p, :], neg[2], ALU.min), 2)
                done(dve.tensor_tensor(weight[:, p, :, :], low[:, p, :].unsqueeze(1).to_broadcast([P, PATS, HEADS]),
                                       rows[:, p, :, NEG:NEG + HEADS], ALU.subtract), 3)
                dve.sem_inc(low_ready, 1)
                dve.wait_ge(weight_ready, t + 1)
                sums = [rows[:, p, a, 0:NEG].rearrange("p (h d) -> p h d", d=OW) for a in range(PATS)]
                for a in range(PATS):
                    ins = dve.tensor_tensor(sums[a], sums[a], weight[:, p, a, :].unsqueeze(2).to_broadcast([P, HEADS, OW]), ALU.mult)
                    ins.then_inc(step, 1)
                dve.wait_ge(step, STEPS * t + 5)
                done(dve.tensor_tensor(total[:, p, :, :], sums[0], sums[1], ALU.add), 7)
                done(dve.tensor_tensor(total[:, p, :, :], total[:, p, :, :], sums[2], ALU.add), 8)
                done(dve.reciprocal(low[:, p, :].unsqueeze(2), total[:, p, :, HD:OW]), 9)
                o = o_all[:, bass.ds(t, 1), :].rearrange("p o (h d) -> p (o h) d", d=HD)
                done(dve.tensor_tensor(o, total[:, p, :, 0:HD], low[:, p, :].unsqueeze(2).to_broadcast([P, HEADS, HD]), ALU.mult), 10)
                flat = o_all[:, bass.ds(t, 1), :].rearrange("p o d -> p (o d)")
                done(dve.tensor_tensor(junk[:, :], flat, flat, ALU.mult), 11)
                done(dve.tensor_reduce(ss[:, bass.ds(t, 1)], junk[:, :], AX.X, ALU.add), 12)

            with dve.Fori(0, TILES_T // 2) as i:
                combine(2 * i, 0, i)
                combine(2 * i + 1, 1, i)
            dve.wait_ge(rms_ready, 1)
            dve.reciprocal(rstd[:, :], rstd[:, :]).then_inc(rstd_ready, 1)
            dve.wait_ge(rstd_ready, 1)
            for t in range(TILES_T):
                if t >= 4:
                    dve.wait_ge(turned, t - 3)
                dve.tensor_scalar(o_n[:, t % 4, :], o_all[:, t, :], rstd[:, t:t + 1], None, ALU.mult).then_inc(o_n_ready, 1)

        @block.tensor
        def _(pe):
            pe.wait_ge(consts_in, 32)
            for t in range(TILES_T):
                b = t // 4
                pe.wait_ge(o_n_ready, t + 1)
                if b >= 2 and t % 4 == 0:
                    pe.wait_ge(out_ready, GROUPS * (b - 1))
                for g in range(GROUPS):
                    ins = pe.transpose(banks[GROUPS * (b % 2) + g][:, (t % 4) * P:(t % 4 + 1) * P], o_n[:, t % 4, g * P:(g + 1) * P], idf[:, :])
                ins.then_inc(turned, 1)


def shape_constants():

    def bf16_bits(v):
        return (np.ascontiguousarray(v).view(np.uint32) >> 16).astype(np.uint16)

    rot = HD // 4
    inv = (np.float32(500000.0) ** (-np.arange(0, rot, 2, dtype=np.float32) / np.float32(rot))).astype(np.float32)
    angle = np.arange(S, dtype=np.float32)[None, :] * inv[:, None]
    rope = np.zeros((P, 2, S), np.float32)
    rope[:, 0] = 1.0
    rotate = np.zeros((P, P), np.float32)
    for head in range(2):
        lo = slice(head * HD, head * HD + rot // 2)
        hi = slice(head * HD + rot // 2, head * HD + rot)
        rope[lo, 0] = rope[hi, 0] = np.cos(angle)
        rope[lo, 1] = rope[hi, 1] = np.sin(angle)
        for d in range(rot // 2):
            rotate[hi.start + d, lo.start + d] = -1.0
            rotate[lo.start + d, hi.start + d] = 1.0
    q = np.arange(SPAN)[:, None]
    k = np.arange(SPAN)[None, :]
    masks = np.zeros((P, PAIRED, 2 * SPAN), np.float32)
    for j, (pat, r, b) in enumerate(attention_blocks()):
        if j < PAIRED:
            masks[:, j, :SPAN] = np.where((k >= q) & (b > 0), 0.0, -1e30)
            masks[:, j, SPAN:] = np.where(k <= q, 0.0, -1e30)
    ident = np.eye(P, dtype=np.float32)
    head_scales = np.zeros((P, 2), np.float32)
    for head in range(2):
        head_scales[head * HD:(head + 1) * HD, head] = HD ** -0.5
    return {"head_scales": head_scales, "rope": rope, "rotate": rotate, "masks": bf16_bits(masks), "ident": ident,
            "ident_bf": bf16_bits(ident)}
FFN = 2816
PAIRS = FFN // P
OUT_SLABS = KT // 2
HALVES = 2
HALF = S // HALVES
HB = HALF // NB
TAPS = 3


def output_projection(nc, mix_t, x_t, w_slabs, rstd, x2_t):
    with ExitStack() as ctx:
        used = []
        ctx.callback(free_semaphores, nc, used)

        def sb(name, shape, dt=F32):
            return ctx.enter_context(nc.sbuf_tensor("op_" + name, shape, dt))

        def sem(name):
            used.append(nc.alloc_semaphore("op_" + name))
            return used[-1]

        w_raw = sb("w_raw", [P, KT, 2 * P])
        w_hi = sb("w_hi", [P, KT, D], F32R)
        w_lo = sb("w_lo", [P, KT, D], F32R)
        RING = 4
        mix_in = sb("mix_in", [P, RING, NB])
        mix_hi = sb("mix_hi", [P, 2, KT, NB], F32R)
        mix_lo = sb("mix_lo", [P, 2, KT, NB], F32R)
        x = sb("x", [P, 2, KT, NB])
        squares = sb("squares", [P, 2, NB])
        total = sb("total", [P, 2, NB])
        ones = sb("ones", [P, P])
        eps = sb("eps", [P, 1])
        banks = [ctx.enter_context(nc.psum_tensor(f"op_bank{i}", [P, NB], F32)) for i in range(4)]
        sum_bank = ctx.enter_context(nc.psum_tensor("op_sum_bank", [P, NB], F32))

        consts_ready = sem("consts_ready")
        w_loaded = sem("w_loaded")
        w_hi_ready = sem("w_hi_ready")
        w_ready = sem("w_ready")
        mix_loaded = [sem(f"mix_loaded{i}") for i in range(RING)]
        mix_hi_ready = sem("mix_hi_ready")
        mix_ready = sem("mix_ready")
        x_loaded = [sem(f"x_loaded{i}") for i in range(2)]
        product_done = sem("product_done")
        added = sem("added")
        square_ready = sem("square_ready")
        summed = sem("summed")
        sum_done = sem("sum_done")
        std_ready = sem("std_ready")
        rstd_ready = sem("rstd_ready")
        stored = [sem(f"stored{i}") for i in range(2)]

        block = ctx.enter_context(nc.Block())

        def blk(b):
            return slice(b * NB, (b + 1) * NB)

        @block.sync
        def _(sp):
            def load_weights(n):
                if n:
                    sp.wait_ge(w_ready, n)
                sp.dma_start(w_raw[:, :, :], w_slabs[n]).then_inc(w_loaded, 16)

            def load_mix(b):
                for k in range(KT):
                    n = KT * b + k
                    if n >= RING:
                        sp.wait_ge(mix_ready, n - RING + 1)
                    sp.dma_start(mix_in[:, n % RING, :], mix_t[k, :, blk(b)]).then_inc(mix_loaded[n % RING], 16)

            def load_x(b):
                if b >= 2:
                    sp.wait_ge(stored[b % 2], 16 * (b // 2))
                    sp.wait_ge(square_ready, KT * (b - 1))
                sp.dma_start(x[:, b % 2, :, :], x_t[:, :, blk(b)]).then_inc(x_loaded[b % 2], 16)

            load_weights(0)
            load_mix(0)
            for n in range(1, OUT_SLABS):
                load_weights(n)
            load_x(0)
            load_x(1)
            for b in range(BLOCKS):
                if b + 1 < BLOCKS:
                    load_mix(b + 1)
                sp.wait_ge(added, KT * (b + 1))
                sp.dma_start(x2_t[:, :, blk(b)], x[:, b % 2, :, :]).then_inc(stored[b % 2], 16)
                if b + 2 < BLOCKS:
                    load_x(b + 2)
            for p in range(2):
                sp.wait_ge(stored[p], 16 * BLOCKS // 2)

        @block.scalar
        def _(act):
            def weights_high(n):
                act.wait_ge(w_loaded, 16 * (n + 1))
                act.activation(w_hi[:, :, n * 2 * P:(n + 1) * 2 * P], w_raw[:, :, :], ACT.Copy).then_inc(w_hi_ready, 1)

            def high(b):
                if b >= 2:
                    act.wait_ge(product_done, KT * (b - 1))
                for k in range(KT):
                    n = KT * b + k
                    act.wait_ge(mix_loaded[n % RING], 16 * (n // RING + 1))
                    act.activation(mix_hi[:, b % 2, k, :], mix_in[:, n % RING, :], ACT.Copy).then_inc(mix_hi_ready, 1)

            def square(b):
                for k in range(KT):
                    n = KT * b + k
                    act.wait_ge(added, n + 1)
                    if n >= 2:
                        act.wait_ge(summed, n - 1)
                    act.activation(squares[:, n % 2, :], x[:, b % 2, k, :], ACT.Square).then_inc(square_ready, 1)

            def root(b):
                act.wait_ge(sum_done, b + 1)
                act.activation(rstd[:, blk(b)], sum_bank[:, :], ACT.Sqrt, bias=eps[:, :], scale=1.0 / D).then_inc(std_ready, 1)

            weights_high(0)
            high(0)
            for n in range(1, OUT_SLABS):
                weights_high(n)
            act.wait_ge(consts_ready, 2)
            for b in range(BLOCKS):
                if b + 1 < BLOCKS:
                    high(b + 1)
                if b:
                    root(b - 1)
                square(b)
            root(BLOCKS - 1)

        @block.gpsimd
        def _(pool):
            for b in range(BLOCKS):
                for k in range(KT):
                    n = KT * b + k
                    pool.wait_ge(square_ready, n + 1)
                    if k:
                        pool.wait_ge(summed, n)
                        ins = pool.tensor_tensor(total[:, b % 2, :], total[:, b % 2, :], squares[:, n % 2, :], ALU.add)
                    else:
                        if b >= 2:
                            pool.wait_ge(sum_done, b - 1)
                        ins = pool.tensor_copy(total[:, b % 2, :], squares[:, n % 2, :])
                    ins.then_inc(summed, 1)

        @block.vector
        def _(dve):
            dve.memset(ones[:, :], 1.0).then_inc(consts_ready, 1)
            dve.memset(eps[:, :], EPS).then_inc(consts_ready, 1)

            def weights_low(n):
                dve.wait_ge(w_hi_ready, n + 1)
                at = slice(n * 2 * P, (n + 1) * 2 * P)
                dve.tensor_tensor(w_lo[:, :, at], w_raw[:, :, :], w_hi[:, :, at].bitcast(F32), ALU.subtract).then_inc(w_ready, 1)

            def low(b):
                for k in range(KT):
                    n = KT * b + k
                    dve.wait_ge(mix_hi_ready, n + 1)
                    dve.tensor_tensor(mix_lo[:, b % 2, k, :], mix_in[:, n % RING, :], mix_hi[:, b % 2, k, :].bitcast(F32),
                                      ALU.subtract).then_inc(mix_ready, 1)

            def invert(b):
                dve.wait_ge(std_ready, b + 1)
                dve.reciprocal(rstd[:, blk(b)], rstd[:, blk(b)]).then_inc(rstd_ready, 1)

            weights_low(0)
            low(0)
            for n in range(1, OUT_SLABS):
                weights_low(n)
            for b in range(BLOCKS):
                if b + 1 < BLOCKS:
                    low(b + 1)
                dve.wait_ge(x_loaded[b % 2], 16 * (b // 2 + 1))
                for m in range(KT):
                    n = KT * b + m
                    dve.wait_ge(product_done, n + 1)
                    at = x[:, b % 2, m, :]
                    dve.tensor_tensor(at, banks[n % 4][:, :], at, ALU.add).then_inc(added, 1)
                    if b and m == KT // 2:
                        invert(b - 1)
            invert(BLOCKS - 1)
            dve.wait_ge(rstd_ready, BLOCKS)

        @block.tensor
        def _(pe):
            pe.wait_ge(consts_ready, 2)

            def sum_squares(b):
                pe.wait_ge(summed, KT * (b + 1))
                if b:
                    pe.wait_ge(std_ready, b)
                pe.matmul(sum_bank[:, :], ones[:, :], total[:, b % 2, :], start=True, stop=True).then_inc(sum_done, 1)

            for b in range(BLOCKS):
                if b:
                    pe.wait_ge(mix_ready, KT * (b + 1))
                for m in range(KT):
                    n = KT * b + m
                    if b == 0 and m % 2 == 0:
                        pe.wait_ge(w_ready, m // 2 + 1)
                    if n >= 4:
                        pe.wait_ge(added, n - 3)
                    cols = slice(m * P, (m + 1) * P)
                    product(pe, banks[n % 4][:, :],
                            [w_hi[:, k, cols] for k in range(KT)], [w_lo[:, k, cols] for k in range(KT)],
                            [mix_hi[:, b % 2, k, :] for k in range(KT)], [mix_lo[:, b % 2, k, :] for k in range(KT)],
                            mix_ready if n == 0 else None).then_inc(product_done, 1)
                    if b and m == 2:
                        sum_squares(b - 1)
            sum_squares(BLOCKS - 1)


def conv_ffn(nc, x2_t, slabs, w_down, conv, gains, rstd, out_t):
    with ExitStack() as ctx:
        used = []
        ctx.callback(free_semaphores, nc, used)

        def sb(name, shape, dt=F32):
            return ctx.enter_context(nc.sbuf_tensor("ff_" + name, shape, dt))

        def sem(name):
            used.append(nc.alloc_semaphore("ff_" + name))
            return used[-1]

        h_hi = sb("h_hi", [P, KT, HALF], F32R)
        h_lo = sb("h_lo", [P, KT, HALF], F32R)
        x2 = sb("x2", [P, KT, HALF])
        up_raw = sb("up_raw", [P, KT, 2 * P])
        up_hi = sb("up_hi", [P, 2, KT, 2 * P], F32R)
        up_lo = sb("up_lo", [P, 2, KT, 2 * P], F32R)
        dn_raw = sb("dn_raw", [P, D])
        dn_hi = sb("dn_hi", [P, 2, D], F32R)
        dn_lo = sb("dn_lo", [P, 2, D], F32R)
        u = sb("u", [P, 2, TAPS - 1 + HALF])
        y = sb("y", [P, 2, HALF])
        a_hi = sb("a_hi", [P, 2, HALF], F32R)
        a_lo = sb("a_lo", [P, 2, HALF], F32R)
        halo = sb("halo", [P, 2, PAIRS, 2, TAPS - 1])
        conv_all = sb("conv_all", [P, PAIRS, 2, TAPS + 1])
        conv_now = sb("conv_now", [P, 2, 2, TAPS + 1])
        out_rstd = sb("out_rstd", [P, NB])
        squares = sb("squares", [P, 2, NB])
        gain = sb("gain", [P, 2, KT])
        ones = sb("ones", [P, P])
        eps = sb("eps", [P, 1])
        banks = [ctx.enter_context(nc.psum_tensor(f"ff_bank{i}", [P, NB], F32)) for i in range(8)]

        consts_in = sem("consts_in")
        gain_in = sem("gain_in")
        consts_ready = sem("consts_ready")
        halo_zeroed = sem("halo_zeroed")
        h_loaded = [[sem(f"h_loaded{b}{i}") for i in range(2)] for b in range(HB)]
        h_hi_ready = sem("h_hi_ready")
        h_even_ready = sem("h_even_ready")
        h_odd_ready = sem("h_odd_ready")
        x2_loaded = sem("x2_loaded")
        up_loaded = sem("up_loaded")
        up_scaled = sem("up_scaled")
        up_hi_ready = sem("up_hi_ready")
        up_ready = sem("up_ready")
        up_done = sem("up_done")
        moved = sem("moved")
        dn_loaded = sem("dn_loaded")
        dn_hi_ready = sem("dn_hi_ready")
        dn_ready = sem("dn_ready")
        dn_done = sem("dn_done")
        dn_added = sem("dn_added")
        square_ready = sem("square_ready")
        square_used = sem("square_used")
        std_ready = sem("std_ready")
        rstd_ready = sem("rstd_ready")
        halo_in = sem("halo_in")
        halo_out = sem("halo_out")
        conv_w_ready = sem("conv_w_ready")
        taps_ready = sem("taps_ready")
        conv_step = sem("conv_step")
        gelu_ready = sem("gelu_ready")
        gated_ready = sem("gated_ready")
        a_hi_ready = sem("a_hi_ready")
        a_ready = sem("a_ready")
        y_ready = sem("y_ready")
        stored = sem("stored")

        block = ctx.enter_context(nc.Block())
        DOWN = KT * HB
        ALL = HALVES * PAIRS

        def blk(b):
            return slice(b * NB, (b + 1) * NB)

        def in_half(half, b):
            return slice(half * HALF + b * NB, half * HALF + (b + 1) * NB)

        def turns(engine, body, half):
            first = half * PAIRS
            looped = (PAIRS - 2) // 2 - half
            with engine.Fori(0, looped) as i:
                body(2 * i + first, 0)
                body(2 * i + (first + 1), 1)
            for g in range(first + 2 * looped, first + PAIRS - 1):
                body(g, g % 2)

        def exists(g):
            return not isinstance(g, int) or g < ALL

        @block.sync
        def _(sp):
            def load_slab(g, e):
                if not isinstance(g, int) or g > 0:
                    sp.wait_ge(up_ready, g)
                sp.dma_start(up_raw[:, :, :], slabs[e + OUT_SLABS]).then_inc(up_loaded, 16)

            def load_down(g, e):
                if not isinstance(g, int) or g > 0:
                    sp.wait_ge(dn_ready, g)
                sp.dma_start(dn_raw[:, :], w_down[e]).then_inc(dn_loaded, 16)

            def load_h(half, b):
                if half:
                    sp.wait_ge(up_done, 4 * PAIRS - 4 + 2 * (b + 1))
                for i in range(2):
                    ks = slice(i * KT // 2, (i + 1) * KT // 2)
                    sp.dma_start(h_lo[:, ks, blk(b)].bitcast(F32), x2_t[:, ks, in_half(half, b)]).then_inc(h_loaded[b][i], 16)

            def load_x2(half):
                if half:
                    sp.wait_ge(stored, 16 * DOWN // 2)
                sp.dma_start(x2[:, :, :], x2_t[:, :, half * HALF:(half + 1) * HALF]).then_inc(x2_loaded, 16)

            def store(half):
                for m in range(0, DOWN, 2):
                    sp.wait_ge(y_ready, DOWN * half + m + 2)
                    k = m % KT
                    sp.dma_start(out_t[:, k:k + 2, in_half(half, m // KT)], x2[:, k:k + 2, blk(m // KT)]).then_inc(stored, 16)

            load_slab(0, 0)
            sp.dma_start(gain[:, :, :], gains).then_inc(gain_in, 16)
            load_h(0, 0)
            load_slab(1, 1)
            load_h(0, 1)
            sp.dma_start(conv_all[:, :, :, :], conv).then_inc(consts_in, 16)
            load_down(0, 0)
            load_x2(0)
            load_slab(2, 2)
            load_down(1, 1)
            with sp.Fori(0, PAIRS - 3) as i:
                load_slab(i + 3, i + 3)
                load_down(i + 2, i + 2)
            for g in range(PAIRS - 3, PAIRS - 1):
                load_slab(g + 3, g + 3 - PAIRS)
                load_down(g + 2, (g + 2) % PAIRS)
            for b in range(HB):
                load_h(1, b)
            load_slab(PAIRS + 2, 2)
            load_down(PAIRS + 1, 1)
            store(0)
            load_x2(1)
            with sp.Fori(0, PAIRS - 3) as i:
                load_slab(i + (PAIRS + 3), i + 3)
                load_down(i + (PAIRS + 2), i + 2)
            load_down(ALL - 1, PAIRS - 1)
            store(1)
            sp.wait_ge(stored, 16 * DOWN)

        @block.gpsimd
        def _(pool):
            pool.sem_inc(halo_out, 1)
            pool.memset(halo[:, 0], 0.0).then_inc(halo_zeroed, 1)
            pool.wait_ge(gain_in, 16)

            def scale_slab(g):
                pool.wait_ge(up_loaded, 16 * (g + 1))
                pool.tensor_tensor(up_raw[:, :, :], up_raw[:, :, :], gain[:, 0, :].unsqueeze(2).to_broadcast([P, KT, 2 * P]),
                                   ALU.mult).then_inc(up_scaled, 1)

            def low_even(half, b):
                for k in range(0, KT, 2):
                    pool.wait_ge(h_hi_ready, KT * (HB * half + b) + k + 1)
                    at = h_lo[:, k, blk(b)]
                    pool.tensor_tensor(at, at.bitcast(F32), h_hi[:, k, blk(b)].bitcast(F32), ALU.subtract).then_inc(h_even_ready, 1)

            def halo_of(half, e):
                return halo[:, half, bass.ds(e, 1), :, :].rearrange("p o a t -> p (o a) t")

            def take_halo(g, j, half):
                e = g - half * PAIRS
                pool.wait_ge(conv_step, 4 * g + 4)
                pool.wait_ge(halo_out, g + 1)
                pool.tensor_copy(conv_now[:, j, :, :], conv_all[:, bass.ds(e, 1), :, :].rearrange("p o a t -> p (o a) t")).then_inc(conv_w_ready, 1)
                pool.tensor_copy(u[:, :, 0:TAPS - 1], halo_of(half, e)).then_inc(halo_in, 1)

            def save_halo(g, half):
                if half == 0:
                    pool.wait_ge(moved, 4 * g + 8)
                    pool.tensor_copy(halo_of(1, g), u[:, :, HALF:HALF + TAPS - 1]).then_inc(halo_out, 1)
                else:
                    pool.sem_inc(halo_out, 1)

            scale_slab(0)
            low_even(0, 0)
            scale_slab(1)
            low_even(0, 1)
            pool.wait_ge(halo_zeroed, 1)
            pool.wait_ge(consts_in, 16)
            for half in range(HALVES):
                first = half * PAIRS
                take_halo(first, 0, half)
                scale_slab(first + 2)
                save_halo(first, half)

                def body(g, j):
                    take_halo(g + 1, 1 - j, half)
                    if exists(g + 3):
                        scale_slab(g + 3)
                    save_halo(g + 1, half)

                turns(pool, body, half)
                if half + 1 < HALVES:
                    for b in range(HB):
                        low_even(half + 1, b)

        @block.scalar
        def _(act):
            def slab_high(g, p):
                act.wait_ge(up_scaled, g + 1)
                if not isinstance(g, int) or g >= 2:
                    act.wait_ge(up_done, 4 * g - 4)
                act.activation(up_hi[:, p, :, :], up_raw[:, :, :], ACT.Copy).then_inc(up_hi_ready, 1)

            def down_high(g, p):
                act.wait_ge(dn_loaded, 16 * (g + 1))
                if not isinstance(g, int) or g >= 2:
                    act.wait_ge(dn_done, DOWN * g - DOWN)
                act.activation(dn_hi[:, p, :], dn_raw[:, :], ACT.Copy).then_inc(dn_hi_ready, 1)

            def split_h(half, b):
                for k in range(KT):
                    if k % (KT // 2) == 0:
                        act.wait_ge(h_loaded[b][k // (KT // 2)], 16 * (half + 1))
                    act.activation(h_hi[:, k, blk(b)], h_lo[:, k, blk(b)].bitcast(F32), ACT.Copy).then_inc(h_hi_ready, 1)

            def taps(g, j):
                act.wait_ge(moved, 4 * g + 8)
                act.wait_ge(a_ready, g + 1)
                act.wait_ge(conv_w_ready, g + 1)
                for a in (1, 0):
                    act.activation(y[:, a, :], u[:, a, TAPS - 1:], ACT.Identity, bias=conv_now[:, j, a, TAPS:TAPS + 1],
                                   scale=conv_now[:, j, a, TAPS - 1:TAPS]).then_inc(taps_ready, 1)

            def gate(g, p):
                act.wait_ge(conv_step, 4 * g + 8)
                act.activation(y[:, 1, :], y[:, 1, :], ACT.Gelu_apprx_tanh).then_inc(gelu_ready, 1)
                act.wait_ge(gated_ready, g + 1)
                if not isinstance(g, int) or g >= 2:
                    act.wait_ge(dn_done, DOWN * g - DOWN)
                act.activation(a_hi[:, p, :], y[:, 0, :], ACT.Copy).then_inc(a_hi_ready, 1)

            def final_roots(half):
                for b in range(HB):
                    for k in range(KT):
                        n = DOWN * half + KT * b + k
                        act.wait_ge(dn_added, 4 + DOWN * (PAIRS * (half + 1) - 1) + KT * b + k + 1)
                        if n >= 2:
                            act.wait_ge(square_used, n - 1)
                        act.activation(squares[:, n % 2, :], x2[:, k, blk(b)], ACT.Square).then_inc(square_ready, 1)
                    n = DOWN * half + KT * b
                    act.wait_ge(square_used, n + KT)
                    if n:
                        act.wait_ge(y_ready, n)
                    act.activation(out_rstd[:, :], banks[2 + b][:, :], ACT.Sqrt, bias=eps[:, :], scale=1.0 / D).then_inc(std_ready, 1)

            slab_high(0, 0)
            split_h(0, 0)
            slab_high(1, 1)
            split_h(0, 1)
            down_high(0, 0)
            act.wait_ge(consts_ready, 2)
            for half in range(HALVES):
                first = half * PAIRS
                taps(first, 0)
                slab_high(first + 2, 0)
                gate(first, 0)
                down_high(first + 1, 1)

                def body(g, j):
                    taps(g + 1, 1 - j)
                    if exists(g + 3):
                        slab_high(g + 3, 1 - j)
                    gate(g + 1, 1 - j)
                    if exists(g + 2):
                        down_high(g + 2, j)

                turns(act, body, half)
                if half + 1 < HALVES:
                    for b in range(HB):
                        split_h(half + 1, b)
                final_roots(half)

        @block.vector
        def _(dve):
            dve.sem_inc(moved, 4)
            dve.sem_inc(dn_added, 4)
            dve.sem_inc(conv_step, 4)
            dve.sem_inc(a_ready, 1)
            dve.memset(ones[:, :], 1.0).then_inc(consts_ready, 1)
            dve.memset(eps[:, :], EPS).then_inc(consts_ready, 1)

            def slab_low(g, p):
                dve.wait_ge(up_hi_ready, g + 1)
                dve.tensor_tensor(up_lo[:, p, :, :], up_raw[:, :, :], up_hi[:, p, :, :].bitcast(F32),
                                  ALU.subtract).then_inc(up_ready, 1)

            def down_low(g, p):
                dve.wait_ge(dn_hi_ready, g + 1)
                dve.tensor_tensor(dn_lo[:, p, :], dn_raw[:, :], dn_hi[:, p, :].bitcast(F32), ALU.subtract).then_inc(dn_ready, 1)

            def low_odd(half, b):
                for k in range(1, KT, 2):
                    dve.wait_ge(h_hi_ready, KT * (HB * half + b) + k + 1)
                    at = h_lo[:, k, blk(b)]
                    dve.tensor_tensor(at, at.bitcast(F32), h_hi[:, k, blk(b)].bitcast(F32), ALU.subtract).then_inc(h_odd_ready, 1)

            def to_u(g, half):
                dve.wait_ge(conv_step, 4 * g + 4)
                dve.wait_ge(halo_out, g + 1)
                for q in range(4):
                    b, a = q // 2, q % 2
                    dve.wait_ge(up_done, 4 * g + (q + 1))
                    dve.tensor_tensor(u[:, a, TAPS - 1 + b * NB:TAPS - 1 + (b + 1) * NB], banks[q][:, :],
                                      rstd[:, in_half(half, b)], ALU.mult).then_inc(moved, 1)

            def convolve(g, j):
                dve.wait_ge(taps_ready, 2 * g + 2)
                dve.wait_ge(halo_in, g + 1)
                dve.wait_ge(moved, 4 * g + 8)
                for s, (tap, a) in enumerate([(1, 1), (1, 0), (0, 1), (0, 0)]):
                    if tap == 0:
                        dve.wait_ge(conv_step, 4 * g + (4 + s - 1))
                    dve.scalar_tensor_tensor(out=y[:, a, :], in0=u[:, a, tap:tap + HALF], scalar=conv_now[:, j, a, tap:tap + 1],
                                             in1=y[:, a, :], op0=ALU.mult, op1=ALU.add).then_inc(conv_step, 1)

            def gated(g):
                dve.wait_ge(gelu_ready, g + 1)
                dve.wait_ge(conv_step, 4 * g + 8)
                dve.tensor_tensor(y[:, 0, :], y[:, 0, :], y[:, 1, :], ALU.mult).then_inc(gated_ready, 1)

            def act_low(g, p):
                dve.wait_ge(a_hi_ready, g + 1)
                dve.tensor_tensor(a_lo[:, p, :], y[:, 0, :], a_hi[:, p, :].bitcast(F32), ALU.subtract).then_inc(a_ready, 1)

            def add_down(g):
                dve.wait_ge(dn_added, DOWN * g + 4)
                for m in range(DOWN):
                    dve.wait_ge(dn_done, DOWN * g + (m + 1))
                    at = x2[:, m % KT, blk(m // KT)]
                    dve.tensor_tensor(at, banks[4 + m % 4][:, :], at, ALU.add).then_inc(dn_added, 1)

            def normalise(half, b):
                dve.wait_ge(std_ready, half * HB + b + 1)
                dve.reciprocal(out_rstd[:, :], out_rstd[:, :]).then_inc(rstd_ready, 1)
                dve.wait_ge(rstd_ready, half * HB + b + 1)
                for k in range(KT):
                    at = x2[:, k, blk(b)]
                    dve.scalar_tensor_tensor(out=at, in0=at, scalar=gain[:, 1, k:k + 1], in1=out_rstd[:, :],
                                             op0=ALU.mult, op1=ALU.mult).then_inc(y_ready, 1)

            slab_low(0, 0)
            low_odd(0, 0)
            slab_low(1, 1)
            low_odd(0, 1)
            down_low(0, 0)
            for half in range(HALVES):
                first = half * PAIRS
                to_u(first, half)
                convolve(first, 0)
                slab_low(first + 2, 0)
                gated(first)
                act_low(first, 0)
                down_low(first + 1, 1)
                dve.wait_ge(x2_loaded, 16 * (half + 1))

                def body(g, j):
                    to_u(g + 1, half)
                    add_down(g)
                    convolve(g + 1, 1 - j)
                    if exists(g + 3):
                        slab_low(g + 3, 1 - j)
                    gated(g + 1)
                    act_low(g + 1, 1 - j)
                    if exists(g + 2):
                        down_low(g + 2, j)

                turns(dve, body, half)
                if half + 1 < HALVES:
                    for b in range(HB):
                        low_odd(half + 1, b)
                add_down(first + PAIRS - 1)
                if half == 0:
                    dve.wait_ge(gain_in, 16)
                dve.wait_ge(dn_added, 4 + DOWN * PAIRS * (half + 1))
                for b in range(HB):
                    normalise(half, b)

        @block.tensor
        def _(pe):
            pe.wait_ge(consts_ready, 2)

            def up(g, p, half_start=None):
                pe.wait_ge(up_ready, g + 1)
                for q in range(4):
                    b, a = q // 2, q % 2
                    if half_start is not None and a == 0:
                        pe.wait_ge(h_even_ready, KT // 2 * (HB * half_start + b + 1))
                        pe.wait_ge(h_odd_ready, KT // 2 * (HB * half_start + b + 1))
                        if half_start:
                            if b:
                                pe.wait_ge(std_ready, HB * half_start)
                    pe.wait_ge(moved, 4 * g + (q + 1))
                    product(pe, banks[q][:, :],
                            [up_hi[:, p, k, a * P:(a + 1) * P] for k in range(KT)],
                            [up_lo[:, p, k, a * P:(a + 1) * P] for k in range(KT)],
                            [h_hi[:, k, blk(b)] for k in range(KT)],
                            [h_lo[:, k, blk(b)] for k in range(KT)]).then_inc(up_done, 1)

            def down(g, p, last_of=None):
                pe.wait_ge(dn_ready, g + 1)
                pe.wait_ge(a_ready, g + 2)
                if last_of is not None:
                    pe.wait_ge(moved, 4 * g + 8)
                for m in range(DOWN):
                    pe.wait_ge(dn_added, DOWN * g + (m + 1))
                    b, k = m // KT, m % KT
                    oc = slice(k * P, (k + 1) * P)
                    product(pe, banks[4 + m % 4][:, :], [dn_hi[:, p, oc]], [dn_lo[:, p, oc]],
                            [a_hi[:, p, blk(b)]], [a_lo[:, p, blk(b)]]).then_inc(dn_done, 1)
                    if last_of is not None and m >= 3:
                        sum_square(last_of, m - 3)
                if last_of is not None:
                    for m in range(DOWN - 3, DOWN):
                        sum_square(last_of, m)

            def sum_square(half, m):
                k = m % KT
                pe.wait_ge(square_ready, DOWN * half + m + 1)
                pe.matmul(banks[2 + m // KT][:, :], ones[:, :], squares[:, m % 2, :], start=(k == 0),
                          stop=(k == KT - 1)).then_inc(square_used, 1)

            for half in range(HALVES):
                first = half * PAIRS
                up(first, 0, half)

                def body(g, j):
                    up(g + 1, 1 - j)
                    down(g, j)

                turns(pe, body, half)
                down(first + PAIRS - 1, 1, half)




def mixer_constants():
    starts = np.ones((P, NB), np.float32)
    starts[:, ::CH] = 0.0
    j = np.arange(P)[:, None]
    i = np.arange(CH)[None, :]
    return {"starts": starts, "causal": np.ascontiguousarray(np.broadcast_to((i >= j)[:, None, :], (P, 2, CH))).astype(np.uint32)}


def program(nc, t, out_t):
    proj_t = nc.dram_tensor("proj_t", [TILES, P, S], F32, kind="Internal").ap()
    o_scratch = nc.dram_tensor("o_scratch", [len(DILATIONS), S, ROW], F32, kind="Internal").ap()
    mix_t = nc.dram_tensor("mix_t", [KT, P, S], F32, kind="Internal").ap()
    input_projection(nc, t["x_t"], t["norm_mix"], t["w_in"], proj_t)
    dilated_attention(nc, proj_t, t["rope"], t["rotate"], t["masks"].bitcast(BF16), t["ident"], t["ident_bf"].bitcast(BF16), t["head_scales"], o_scratch)
    gated_linear_attention(nc, proj_t, t["gla_w_gate"], t["gla_b_gate"], t["starts"], t["causal"], t["ident"], t["gla_norm"], mix_t)
    recurrent_branch(nc, proj_t, t["lru"], t["lru_w"], mix_t)
    combine_patterns(nc, o_scratch, t["ident"], t["swa_norm"], mix_t)
    x2_t = nc.dram_tensor("x2_t", [P, KT, S], F32, kind="Internal").ap()
    with ExitStack() as ctx:
        rstd = ctx.enter_context(nc.sbuf_tensor("ffn_rstd", [P, S], F32))
        output_projection(nc, mix_t, t["x_t"], t["slabs"], rstd, x2_t)
        conv_ffn(nc, x2_t, t["slabs"], t["w_down"], t["conv"], t["gains"], rstd, out_t)


def pad_heads(w):
    out = np.zeros(w.shape[:-1] + (GP * P,), np.float32)
    for h in range(GH):
        out[..., h * 64:h * 64 + DK] = w[..., h * DK:(h + 1) * DK]
    return out


def kernel(**inputs):
    import concourse.bacc as bacc
    from concourse.bass_utils import run_bass_kernel_spmd as run

    a = {k: np.asarray(v) for k, v in inputs.items()}
    flat = np.ascontiguousarray

    def per_channel(v):
        return flat(v.reshape(-1, P).T)

    arrays = {"x_t": flat(a["x"][0].T.reshape(KT, P, S).transpose(1, 0, 2)), "norm_mix": per_channel(a["norm_mix"][0])}
    sizes = (GH * DK, GH * DK, AW, AW, RANK, LW, LW, HEADS * HD, HEADS * HD, HEADS * HD)
    aq, ak, av, ar, glr, bg, bi, cq, ck, cv = np.split(a["w_in"][0], np.cumsum(sizes)[:-1], axis=1)
    aq = pad_heads(aq)
    aq[:, GLR_ROW:GLR_ROW + RANK] = glr
    w = np.concatenate([aq, pad_heads(ak), av, ar, bg, bi, cq, ck, cv], axis=1)
    arrays["w_in"] = flat(w.reshape(KT, P, TILES, P).transpose(2, 1, 0, 3))
    arrays["gla_w_gate"] = flat(pad_heads(a["gla_w_gate"][0]).reshape(RANK, GP, P))
    arrays["gla_b_gate"] = per_channel(pad_heads(a["gla_b_gate"][0]))
    arrays["gla_norm"] = per_channel(np.tile(a["gla_norm"][0], GH))
    per = [a["lru_conv_w"][0][t] for t in range(LTAPS)] + [a[n][0] for n in ("lru_conv_b", "lru_b_a", "lru_b_x", "lru_lambda", "lru_norm")]
    arrays["lru"] = flat(np.stack(per).reshape(C_NORM + 1, LT, P).transpose(2, 1, 0))
    lru_w = np.zeros((P, LT, 2, P), np.float32)
    bs = a["lru_w_a"].shape[-1]
    for s, name in enumerate(("lru_w_a", "lru_w_x")):
        for n in range(LW // bs):
            at = n * bs % P
            lru_w[at:at + bs, n * bs // P, s, at:at + bs] = a[name][0, n]
    arrays["lru_w"] = lru_w
    arrays["swa_norm"] = per_channel(a["swa_norm"][0])
    w_out_slabs = a["w_out"][0].reshape(KT, P, OUT_SLABS, 2 * P).transpose(2, 1, 0, 3)
    w_up_slabs = a["ffn_w_up"][0].reshape(KT, P, 2, PAIRS, P).transpose(3, 1, 0, 2, 4).reshape(PAIRS, P, KT, 2 * P)
    arrays["slabs"] = np.concatenate([w_out_slabs, w_up_slabs])
    arrays["w_down"] = flat(a["ffn_w_down"][0].reshape(PAIRS, P, D))
    conv = np.concatenate([a["ffn_conv_w"][0], a["ffn_conv_b"]])
    arrays["conv"] = flat(conv.reshape(TAPS + 1, 2, PAIRS, P).transpose(3, 2, 1, 0))
    arrays["gains"] = flat(np.stack([per_channel(a["norm_ffn"][0]), per_channel(a["norm_final"])], axis=1))
    arrays.update(shape_constants())
    arrays.update(mixer_constants())

    nc = bacc.Bacc("TRN2", target_bir_lowering=False, num_devices=1)
    tensors = {k: nc.dram_tensor("in_" + k, v.shape, mybir.dt.from_np(v.dtype), kind="ExternalInput").ap() for k, v in arrays.items()}
    out_t = nc.dram_tensor("out_t", [P, KT, S], F32, kind="ExternalOutput").ap()
    program(nc, tensors, out_t)
    r = run(nc, [{"in_" + k: v for k, v in arrays.items()}], core_ids=[0])
    return flat(r.results[0]["out_t"].transpose(2, 1, 0).reshape(1, S, D))
```

```python
from contextlib import ExitStack

import numpy as np

import concourse.bass as bass
from concourse import mybir

F32 = mybir.dt.float32
F32R = mybir.dt.float32r
BF16 = mybir.dt.bfloat16
ALU = mybir.AluOpType
ACT = mybir.ActivationFunctionType
AX = mybir.AxisListType

P = 128
D = 1024
KT = D // P
S = 2048
NB = 512
BLOCKS = S // NB
EPS = 1e-6

T_AQ, T_AK, T_AV, T_AR, T_BG, T_BI, T_CQ, T_CK, T_CV = 0, 2, 4, 7, 10, 12, 14, 17, 20
TILES = 23
GLR_ROW = 112


def free_semaphores(nc, used):
    nc.clear_and_free_semaphores(used)
    nc.all_engine_barrier()


def product(pe, out, w_hi, w_lo, x_hi, x_lo, x_ready=None):
    n = len(w_hi)
    for k in range(n):
        if x_ready is not None:
            pe.wait_ge(x_ready[k % len(x_ready)], k // len(x_ready) + 1)
        pe.matmul(out, w_hi[k], x_hi[k], start=(k == 0), stop=False)
        pe.matmul(out, w_hi[k], x_lo[k], start=False, stop=False)
        last = pe.matmul(out, w_lo[k], x_hi[k], start=False, stop=(k == n - 1))
    return last


def input_projection(nc, x_t, norm_gain, w_tiles, proj_t):
    with ExitStack() as ctx:
        used = []
        ctx.callback(free_semaphores, nc, used)

        def sb(name, shape, dt=F32):
            return ctx.enter_context(nc.sbuf_tensor("ip_" + name, shape, dt))

        def sem(name):
            used.append(nc.alloc_semaphore("ip_" + name))
            return used[-1]

        x_in = sb("x_in", [P, 2, KT, NB])
        squares = sb("squares", [P, 3, NB])
        total = sb("total", [P, 2, 2, NB])
        x_hi = sb("x_hi", [P, KT, S], F32R)
        x_lo = sb("x_lo", [P, KT, S], F32R)
        w_raw = sb("w_raw", [P, KT, P])
        w_hi = sb("w_hi", [P, 2, KT, P], F32R)
        w_lo = sb("w_lo", [P, 2, KT, P], F32R)
        staged = sb("staged", [P, 2, NB])
        rstd = sb("rstd", [P, S])
        gain = sb("gain", [P, KT])
        ones = sb("ones", [P, P])
        eps = sb("eps", [P, 1])
        banks = [ctx.enter_context(nc.psum_tensor(f"ip_bank{i}", [P, NB], F32)) for i in range(8)]

        gain_in = sem("gain_in")
        x_loaded = [sem(f"x_loaded{i}") for i in range(2)]
        consts_ready = sem("consts_ready")
        hi_ready = sem("hi_ready")
        x_ready = sem("x_ready")
        square_ready = sem("square_ready")
        added = [sem("added_even"), sem("added_odd")]
        x_first_loaded = sem("x_first_loaded")
        sum_done = sem("sum_done")
        std_ready = sem("std_ready")
        rstd_ready = sem("rstd_ready")
        w_loaded = sem("w_loaded")
        w_scaled = sem("w_scaled")
        w_hi_ready = sem("w_hi_ready")
        w_ready = sem("w_ready")
        product_done = sem("product_done")
        bank_free = sem("bank_free")
        stored = [sem(f"stored{i}") for i in range(2)]

        block = ctx.enter_context(nc.Block())
        SUM_BANK = (7, 7, 0, 1)
        FIRST = 2 * BLOCKS
        TURNS = (TILES - 3) // 2

        def blk(b):
            return slice(b * NB, (b + 1) * NB)

        def add_squares(engine, b, odd):
            for k in range(KT // 2):
                n = KT // 2 * b + k
                engine.wait_ge(square_ready, 2 * n + odd + 1)
                at = squares[:, (2 * n + odd) % 3, :]
                if k:
                    engine.wait_ge(added[odd], n)
                    ins = engine.tensor_tensor(total[:, b % 2, odd, :], total[:, b % 2, odd, :], at, ALU.add)
                else:
                    if b >= 2:
                        engine.wait_ge(sum_done, b - 1)
                    ins = engine.tensor_copy(total[:, b % 2, odd, :], at)
                ins.then_inc(added[odd], 1)

        @block.sync
        def _(sp):
            for p in range(2):
                sp.sem_inc(stored[p], 16)

            def load_weights(t):
                if not isinstance(t, int) or t > 0:
                    sp.wait_ge(w_ready, t)
                sp.dma_start(w_raw[:, :, :], w_tiles[t]).then_inc(w_loaded, 16)

            def load_x(b):
                if b >= 2:
                    sp.wait_ge(x_ready, KT * (b - 1))
                    sp.wait_ge(square_ready, KT * (b - 1))
                if b == 0:
                    sp.dma_start(x_in[:, 0, 0:KT // 2, :], x_t[:, 0:KT // 2, blk(0)]).then_inc(x_first_loaded, 16)
                    sp.dma_start(x_in[:, 0, KT // 2:, :], x_t[:, KT // 2:, blk(0)]).then_inc(x_loaded[0], 16)
                else:
                    sp.dma_start(x_in[:, b % 2, :, :], x_t[:, :, blk(b)]).then_inc(x_loaded[b % 2], 16)

            def store_first(n):
                sp.wait_ge(bank_free, 8 + n + 1)
                sp.dma_start(proj_t[n % 2][:, blk(n // 2)], staged[:, n % 2, :]).then_inc(stored[n % 2], 16)

            def store_tile(t):
                for b in range(BLOCKS):
                    sp.wait_ge(bank_free, BLOCKS * t + (8 + b + 1))
                    sp.dma_start(proj_t[t][:, blk(b)], staged[:, b % 2, :]).then_inc(stored[b % 2], 16)

            load_weights(0)
            sp.dma_start(gain[:, :], norm_gain).then_inc(gain_in, 16)
            load_x(0)
            load_weights(1)
            load_x(1)
            load_x(2)
            load_x(3)
            load_weights(2)
            for n in range(FIRST):
                if n == FIRST - 2:
                    load_weights(3)
                store_first(n)
            with sp.Fori(0, TURNS - 1) as i:
                for j in range(2):
                    load_weights(2 * i + (4 + j))
                    store_tile(2 * i + (2 + j))
            load_weights(TILES - 1)
            for t in range(TILES - 3, TILES):
                store_tile(t)
            for p in range(2):
                sp.wait_ge(stored[p], 16 + 16 * BLOCKS // 2 * TILES)

        @block.gpsimd
        def _(pool):
            pool.wait_ge(gain_in, 16)

            def scale_weights(t):
                pool.wait_ge(w_loaded, 16 * (t + 1))
                pool.tensor_tensor(w_raw[:, :, :], w_raw[:, :, :], gain[:, :].unsqueeze(2).to_broadcast([P, KT, P]),
                                   ALU.mult).then_inc(w_scaled, 1)

            scale_weights(0)
            scale_weights(1)
            add_squares(pool, 0, 0)
            add_squares(pool, 1, 0)
            add_squares(pool, 2, 0)
            scale_weights(2)
            add_squares(pool, 3, 0)
            with pool.Fori(0, TURNS) as i:
                for j in range(2):
                    scale_weights(2 * i + (3 + j))

        @block.scalar
        def _(act):
            def weights_high(t, p, multiplied):
                act.wait_ge(w_scaled, t + 1)
                if multiplied is not None:
                    act.wait_ge(product_done, multiplied)
                act.activation(w_hi[:, p, :, :], w_raw[:, :, :], ACT.Copy).then_inc(w_hi_ready, 1)

            def high(b):
                if b == 0:
                    act.wait_ge(x_first_loaded, 16)
                for k in range(KT):
                    if k == (KT // 2 if b == 0 else 0):
                        act.wait_ge(x_loaded[b % 2], 16 * (b // 2 + 1))
                    act.activation(x_hi[:, k, blk(b)], x_in[:, b % 2, k, :], ACT.Copy).then_inc(hi_ready, 1)

            def square(b):
                for k in range(KT):
                    n = KT * b + k
                    if n >= 3:
                        act.wait_ge(added[(n - 3) % 2], (n - 3) // 2 + 1)
                    act.activation(squares[:, n % 3, :], x_in[:, b % 2, k, :], ACT.Square).then_inc(square_ready, 1)

            def root(b):
                act.wait_ge(sum_done, b + 1)
                act.activation(rstd[:, blk(b)], banks[SUM_BANK[b]][:, :], ACT.Sqrt, bias=eps[:, :],
                               scale=1.0 / D).then_inc(std_ready, 1)

            weights_high(0, 0, None)
            high(0)
            weights_high(1, 1, None)
            square(0)
            high(1)
            square(1)
            act.wait_ge(consts_ready, 2)
            high(2)
            high(3)
            square(2)
            root(0)
            square(3)
            root(1)
            root(2)
            weights_high(2, 0, FIRST - 1)
            root(3)
            with act.Fori(0, TURNS) as i:
                weights_high(2 * i + 3, 1, 8 * i + 8)
                weights_high(2 * i + 4, 0, 8 * i + 12)

        @block.vector
        def _(dve):
            dve.sem_inc(bank_free, 8)
            dve.memset(ones[:, :], 1.0).then_inc(consts_ready, 1)
            dve.memset(eps[:, :], EPS).then_inc(consts_ready, 1)

            def weights_low(t, p):
                dve.wait_ge(w_hi_ready, t + 1)
                dve.tensor_tensor(w_lo[:, p, :, :], w_raw[:, :, :], w_hi[:, p, :, :].bitcast(F32),
                                  ALU.subtract).then_inc(w_ready, 1)

            def low(b):
                for k in range(KT):
                    dve.wait_ge(hi_ready, KT * b + k + 1)
                    dve.tensor_tensor(x_lo[:, k, blk(b)], x_in[:, b % 2, k, :], x_hi[:, k, blk(b)].bitcast(F32),
                                      ALU.subtract).then_inc(x_ready, 1)

            def invert(b):
                dve.wait_ge(std_ready, b + 1)
                dve.reciprocal(rstd[:, blk(b)], rstd[:, blk(b)]).then_inc(rstd_ready, 1)
                dve.wait_ge(rstd_ready, b + 1)

            def drain(n, bank, b, use):
                dve.wait_ge(product_done, n + 1)
                dve.wait_ge(stored[bank % 2], 16 * (use + 1))
                dve.tensor_tensor(staged[:, bank % 2, :], banks[bank][:, :], rstd[:, blk(b)], ALU.mult).then_inc(bank_free, 1)

            def drain_tile(t, p):
                for b in range(BLOCKS):
                    drain(BLOCKS * t + b, 4 * p + b, b, 2 * t + b // 2)

            weights_low(0, 0)
            low(0)
            weights_low(1, 1)
            add_squares(dve, 0, 1)
            low(1)
            add_squares(dve, 1, 1)
            low(2)
            low(3)
            for b in range(BLOCKS):
                if b + 2 < BLOCKS:
                    add_squares(dve, b + 2, 1)
                if b == 3:
                    weights_low(2, 0)
                invert(b)
                for n in range(2 * b, 2 * b + 2):
                    drain(n, n, b, n // 2)
            with dve.Fori(0, TURNS) as i:
                weights_low(2 * i + 3, 1)
                drain_tile(2 * i + 2, 0)
                weights_low(2 * i + 4, 0)
                drain_tile(2 * i + 3, 1)
            drain_tile(TILES - 1, 0)

        @block.tensor
        def _(pe):
            pe.wait_ge(consts_ready, 2)

            def project(n, bank, p, b):
                pe.wait_ge(bank_free, n + 1)
                product(pe, banks[bank][:, :],
                        [w_hi[:, p, k, :] for k in range(KT)], [w_lo[:, p, k, :] for k in range(KT)],
                        [x_hi[:, k, blk(b)] for k in range(KT)], [x_lo[:, k, blk(b)] for k in range(KT)],
                        (x_ready,) if isinstance(n, int) and n == 0 else None).then_inc(product_done, 1)

            def sum_squares(b):
                for odd in range(2):
                    pe.wait_ge(added[odd], KT // 2 * (b + 1))
                if b >= 2:
                    pe.wait_ge(bank_free, 8 + b - 1)
                elif b:
                    pe.wait_ge(std_ready, 1)
                for odd in range(2):
                    ins = pe.matmul(banks[SUM_BANK[b]][:, :], ones[:, :], total[:, b % 2, odd, :], start=(odd == 0),
                                    stop=(odd == 1))
                ins.then_inc(sum_done, 1)

            def tile(t, p):
                pe.wait_ge(w_ready, t + 1)
                for b in range(BLOCKS):
                    project(BLOCKS * t + b, 4 * p + b, p, b)

            for n in range(FIRST):
                b, t = n // 2, n % 2
                if b == 0:
                    pe.wait_ge(w_ready, t + 1)
                elif t == 0:
                    pe.wait_ge(x_ready, KT * (b + 1))
                if n == FIRST - 1:
                    pe.wait_ge(std_ready, 2)
                project(n, n, t, b)
                if n in (3, 5, 6, 7):
                    sum_squares({3: 0, 5: 1, 6: 2, 7: 3}[n])
            pe.wait_ge(w_ready, 3)
            for b in range(BLOCKS):
                if b < 2:
                    pe.wait_ge(std_ready, 3 + b)
                project(FIRST + b, b, 0, b)
            with pe.Fori(0, TURNS) as i:
                tile(2 * i + 3, 1)
                tile(2 * i + 4, 0)


HEADS = 6
HD = 64
GROUPS = HEADS // 2
DILATIONS = (1, 4, 16)
SPAN = 128
PAIRED = 32
SINGLE = 16
OW = HD + 1
ROW = HEADS * (OW + 1)
NEG = HEADS * OW


def attention_blocks():
    for pat, dil in enumerate(DILATIONS):
        for r in range(dil):
            for b in range(S // dil // SPAN):
                yield pat, r, b


def dilated_attention(nc, proj_t, rope, rotate, masks, ident, ident_bf, head_scales, o_scratch):
    with ExitStack() as ctx:
        used = []
        ctx.callback(free_semaphores, nc, used)

        def sb(name, shape, dt=F32):
            return ctx.enter_context(nc.sbuf_tensor("at_" + name, shape, dt))

        def sem(name):
            used.append(nc.alloc_semaphore("at_" + name))
            return used[-1]

        qkv = sb("qkv", [P, 3, GROUPS, S])
        cos_sin = sb("cos_sin", [P, 2, S])
        rot_w = sb("rot_w", [P, P])
        mask = sb("mask", [P, PAIRED, 2 * SPAN], BF16)
        idf = sb("idf", [P, P])
        head_scale = sb("head_scale", [P, 2])
        idb = sb("idb", [P, P], BF16)
        rope_c = sb("rope_c", [P, 2, NB])
        rope_s = sb("rope_s", [P, 2, NB])
        q_s = sb("q_s", [P, 2, GROUPS, 2, SPAN])
        k_s = sb("k_s", [P, 2, GROUPS, 2 * SPAN])
        v_s = sb("v_s", [P, 2, GROUPS, SPAN])
        v_tok = sb("v_tok", [P, 2, HEADS, OW])
        probs = sb("probs", [P, GROUPS, 4 * SPAN])
        probs_t = sb("probs_t", [P, GROUPS, 4 * SPAN])
        neg = sb("neg", [P, 2, HEADS])
        o_sb = sb("o_sb", [P, 2, ROW])

        def bank(name):
            return ctx.enter_context(nc.psum_tensor("at_" + name, [P, NB], F32))

        s_bank = [bank(f"s{i}") for i in range(GROUPS)]
        t_bank = [bank(f"t{i}") for i in range(2)]
        o_bank = [bank(f"o{i}") for i in range(2)]
        v_bank = bank("v")

        consts_in = sem("consts_in")
        rope_in = sem("rope_in")
        q_in, k_in, v_in = sem("q_in"), sem("k_in"), sem("v_in")
        rotated = sem("rotated")
        times_cos = sem("times_cos")
        times_sin = sem("times_sin")
        roped = sem("roped")
        staged = sem("staged")
        q_staged = sem("q_staged")
        scores_ready = sem("scores_ready")
        max_ready = sem("max_ready")
        probs_ready = sem("probs_ready")
        pt_done = sem("pt_done")
        pt_even = sem("pt_even")
        pt_odd = sem("pt_odd")
        vt_done = sem("vt_done")
        v_ready = sem("v_ready")
        o_done = sem("o_done")
        o_ready = sem("o_ready")
        stored = [sem(f"stored{i}") for i in range(2)]

        block = ctx.enter_context(nc.Block())
        blocks = list(attention_blocks())

        @block.sync
        def _(sp):
            sp.dma_start(rot_w[:, :], rotate).then_inc(rope_in, 16)
            sp.dma_start(cos_sin[:, :, :], rope).then_inc(rope_in, 16)
            sp.dma_start(head_scale[:, :], head_scales).then_inc(consts_in, 16)
            for a, (t, loaded) in enumerate([(T_CQ, q_in), (T_CK, k_in), (T_CV, v_in)]):
                if a:
                    sp.wait_ge((q_in, k_in)[a - 1], 16)
                sp.dma_start(qkv[:, a, :, :], proj_t[t:t + GROUPS].rearrange("g p s -> p g s")).then_inc(loaded, 16)
            sp.dma_start(idf[:, :], ident).then_inc(consts_in, 16)
            sp.dma_start(idb[:, :], ident_bf).then_inc(consts_in, 16)
            sp.dma_start(mask[:, :, :], masks).then_inc(consts_in, 16)
            for j, (pat, r, b) in enumerate(blocks):
                dil = DILATIONS[pat]
                first = dil * SPAN * b + r
                rows = o_scratch[pat, first:first + dil * (SPAN - 1) + 1:dil, :]
                sp.wait_ge(o_ready, 2 * j + 6)
                sp.dma_start(rows, o_sb[:, j % 2, :]).then_inc(stored[j % 2], 16)
            for p in range(2):
                sp.wait_ge(stored[p], 16 * len(blocks) // 2)

        UNITS = GROUPS * BLOCKS

        def unit_at(i, m):
            return bass.ds(i * (2 * NB) + m // GROUPS * NB, NB)

        def tokens(a, start, dil):
            return qkv[:, a, :, start:start + dil * (SPAN - 1) + 1:dil]

        @block.gpsimd
        def _(pool):
            pool.wait_ge(rope_in, 32)
            for a, loaded in enumerate((q_in, k_in)):
                pool.wait_ge(loaded, 16)
                with pool.Fori(0, BLOCKS // 2) as i:
                    for m in range(2 * GROUPS):
                        pool.wait_ge(roped, UNITS * a + 2 * GROUPS * i + (m + 1))
                        at = unit_at(i, m)
                        pool.tensor_tensor(rope_c[:, m % 2, :], qkv[:, a, m % GROUPS, at], cos_sin[:, 0, at],
                                           ALU.mult).then_inc(times_cos, 1)
            pool.wait_ge(roped, 2 + 2 * UNITS)
            pool.wait_ge(v_in, 16)
            for j, (pat, r, b) in enumerate(blocks):
                dil = DILATIONS[pat]
                first = dil * SPAN * b + r

                if j >= 2:
                    pool.wait_ge(scores_ready, GROUPS * (j - 1))
                    pool.wait_ge(vt_done, j - 1)
                if pat < 2:
                    prev = first - dil * SPAN if b else first
                    pool.tensor_copy(k_s[:, j % 2, :, 0:SPAN], tokens(1, prev, dil)).then_inc(staged, 1)
                    pool.tensor_copy(k_s[:, j % 2, :, SPAN:2 * SPAN], tokens(1, first, dil)).then_inc(staged, 1)
                else:
                    pool.tensor_copy(k_s[:, j % 2, :, 0:SPAN], tokens(1, first, dil)).then_inc(staged, 1)
                pool.tensor_copy(v_s[:, j % 2, :, :], tokens(2, first, dil)).then_inc(staged, 1)

        def staged_after(j, wide):
            return 3 * j + 3 if wide else 2 * j + (2 + PAIRED)

        @block.scalar
        def _(act):
            def neg_at(slot, hh, g):
                return neg[:, slot, 2 * g + hh:2 * g + hh + 1]

            def exps(j, slot, wide, g, fresh):
                width = (2 if wide else 1) * SPAN
                act.wait_ge(max_ready, GROUPS * j + (g + 1))
                if not fresh:
                    act.wait_ge(pt_done, GROUPS * j + (g - 2))
                for hh in range(2):
                    ins = act.activation(probs[:, g, hh * width:(hh + 1) * width], s_bank[g][:, hh * width:(hh + 1) * width],
                                         ACT.Exp, bias=neg_at(slot, hh, g))
                ins.then_inc(probs_ready, 1)

            def turned_odd(j, slot, wide, fresh):
                n = (4 if wide else 2) * SPAN
                act.wait_ge(pt_done, GROUPS * j + 2)
                if not fresh:
                    act.wait_ge(o_done, j)
                act.activation(probs_t[:, 1, 0:n], t_bank[(slot + 1) % 2][:, 0:n], ACT.Copy).then_inc(pt_odd, 1)

            def stage_queries(j):
                pat, r, b = blocks[j]
                dil = DILATIONS[pat]
                for hh in range(2):
                    act.activation(q_s[:, j % 2, :, hh, :], tokens(0, dil * SPAN * b + r, dil), ACT.Copy,
                                   scale=head_scale[:, hh:hh + 1]).then_inc(q_staged, 1)

            def take_values(j):
                act.wait_ge(vt_done, j + 1)
                if j:
                    act.wait_ge(o_done, j)
                act.activation(v_tok[:, j % 2, :, 0:HD], v_bank[:, 0:HEADS * HD].rearrange("p (h d) -> p h d", h=HEADS),
                               ACT.Copy).then_inc(v_ready, 1)

            act.wait_ge(v_ready, 2)
            act.wait_ge(consts_in, 16 * 4)
            act.wait_ge(roped, 2 + 2 * UNITS)
            stage_queries(0)
            stage_queries(1)
            for j in range(len(blocks)):
                wide = j < PAIRED
                if j == PAIRED:
                    turned_odd(j - 1, 1, True, False)
                for g in range(GROUPS):
                    exps(j, j % 2, wide, g, j == 0)
                    if g == 1 and j and j != PAIRED:
                        turned_odd(j - 1, 1 - j % 2, wide, j == 1)
                take_values(j)
                if j + 2 < len(blocks):
                    stage_queries(j + 2)
            turned_odd(PAIRED + SINGLE - 1, 1, False, False)

        @block.vector
        def _(dve):
            dve.sem_inc(o_ready, 4)
            dve.sem_inc(roped, 2)
            dve.sem_inc(times_sin, 2)
            for slot in range(2):
                dve.memset(v_tok[:, slot, :, :], 1.0).then_inc(v_ready, 1)
            dve.wait_ge(rope_in, 32)
            for a in range(2):
                with dve.Fori(0, BLOCKS // 2) as i:
                    for m in range(2 * GROUPS):
                        n = UNITS * a + 2 * GROUPS * i + m
                        at = unit_at(i, m)
                        dve.wait_ge(rotated, n + 1)
                        dve.wait_ge(roped, n + 1)
                        dve.tensor_tensor(rope_s[:, m % 2, :], s_bank[m % 2][:, :], cos_sin[:, 1, at], ALU.mult).then_inc(times_sin, 1)
                        dve.wait_ge(times_sin, n + 3)
                        dve.wait_ge(times_cos, n + 1)
                        dve.tensor_tensor(qkv[:, a, m % GROUPS, at], rope_c[:, m % 2, :], rope_s[:, m % 2, :],
                                          ALU.add).then_inc(roped, 1)

            def maxima(j, slot, wide, g):
                width = (2 if wide else 1) * SPAN
                dve.wait_ge(scores_ready, GROUPS * j + (g + 1))
                dve.tensor_reduce(neg[:, slot, 2 * g:2 * g + 2],
                                  s_bank[g][:, 0:2 * width].rearrange("p (h k) -> p h k", h=2), AX.X, ALU.max,
                                  negate=True).then_inc(max_ready, 1)

            def turned_even(j, slot, wide, g, fresh):
                n = (4 if wide else 2) * SPAN
                dve.wait_ge(pt_done, GROUPS * j + (g + 1))
                if not fresh:
                    dve.wait_ge(o_done, j)
                dve.tensor_copy(probs_t[:, g, 0:n], t_bank[(slot + g) % 2][:, 0:n]).then_inc(pt_even, 1)

            def take_sums(j, slot, uses):
                if uses is not None:
                    dve.wait_ge(stored[slot], uses)
                dve.wait_ge(o_done, j + 1)
                dve.tensor_copy(o_sb[:, slot, 0:NEG], o_bank[slot][:, 0:NEG]).then_inc(o_ready, 1)
                dve.wait_ge(max_ready, GROUPS * (j + 1))
                dve.tensor_copy(o_sb[:, slot, NEG:ROW], neg[:, slot, :]).then_inc(o_ready, 1)

            def start(j, slot, wide):
                for g in range(GROUPS):
                    if g == 0 and j:
                        dve.wait_ge(o_ready, 2 * j + 2)
                    maxima(j, slot, wide, g)

            def body(j, slot, wide, uses, last_fresh=False):
                if not last_fresh:
                    dve.wait_ge(o_ready, 2 * j + 2)
                maxima(j, slot, wide, 0)
                turned_even(j - 1, 1 - slot, wide, 0, last_fresh)
                maxima(j, slot, wide, 1)
                turned_even(j - 1, 1 - slot, wide, 2, last_fresh)
                maxima(j, slot, wide, 2)
                take_sums(j - 1, 1 - slot, uses)

            def finish(j, slot, wide):
                turned_even(j, slot, wide, 0, False)
                turned_even(j, slot, wide, 2, False)
                take_sums(j, slot, 16 * (j // 2))

            dve.wait_ge(v_ready, 2)
            start(0, 0, True)
            body(1, 1, True, None, True)
            body(2, 0, True, None)
            body(3, 1, True, 16)
            with dve.Fori(0, PAIRED // 2 - 2) as i:
                body(2 * i + 4, 0, True, 16 * (i + 1))
                body(2 * i + 5, 1, True, 16 * (i + 2))
            finish(PAIRED - 1, 1, True)
            start(PAIRED, 0, False)
            body(PAIRED + 1, 1, False, 16 * (PAIRED // 2))
            with dve.Fori(0, SINGLE // 2 - 1) as i:
                body(2 * i + (PAIRED + 2), 0, False, 16 * (i + PAIRED // 2))
                body(2 * i + (PAIRED + 3), 1, False, 16 * (i + (PAIRED // 2 + 1)))
            finish(PAIRED + SINGLE - 1, 1, False)

        @block.tensor
        def _(pe):
            pe.wait_ge(rope_in, 32)
            for a, loaded in enumerate((q_in, k_in)):
                pe.wait_ge(loaded, 16)
                with pe.Fori(0, BLOCKS // 2) as i:
                    for m in range(2 * GROUPS):
                        pe.wait_ge(times_sin, UNITS * a + 2 * GROUPS * i + (m + 1))
                        pe.matmul(s_bank[m % 2][:, :], rot_w[:, :], qkv[:, a, m % GROUPS, unit_at(i, m)],
                                  start=True, stop=True).then_inc(rotated, 1)
            pe.wait_ge(consts_in, 16 * 4)
            pe.wait_ge(times_sin, 2 + 2 * UNITS)

            def turn_v(j, slot, wide):
                pe.wait_ge(v_ready, j + 2)
                for g in range(GROUPS):
                    ins = pe.transpose(v_bank[:, g * SPAN:(g + 1) * SPAN], v_s[:, slot, g, :], idf[:, :])
                ins.then_inc(vt_done, 1)

            def scores(j, slot, wide, g, fresh):
                width = (2 if wide else 1) * SPAN
                if g == 0:
                    pe.wait_ge(staged, staged_after(j, wide))
                    pe.wait_ge(q_staged, 2 * j + 2)
                if not fresh:
                    pe.wait_ge(probs_ready, GROUPS * j + (g - 2))
                if wide:
                    at = mask[:, bass.ds(j, 1), :] if not isinstance(j, int) else mask[:, j:j + 1, :]
                else:
                    at = mask[:, 1:2, SPAN:2 * SPAN]
                for hh in range(2):
                    pe.matmul(s_bank[g][:, hh * width:(hh + 1) * width], idb[:, :], at.rearrange("p o k -> p (o k)"),
                              start=(hh == 0), stop=False, skip_group_check=True)
                for hh in range(2):
                    ins = pe.matmul(s_bank[g][:, hh * width:(hh + 1) * width], q_s[:, slot, g, hh, :],
                                    k_s[:, slot, g, 0:width], start=False, stop=(hh == 1), skip_group_check=True)
                ins.then_inc(scores_ready, 1)

            def turn_probs(j, slot, wide, g, fresh):
                pe.wait_ge(probs_ready, GROUPS * j + (g + 1))
                if g == 2:
                    pe.wait_ge(pt_even, 2 * j + 1)
                elif not fresh:
                    pe.wait_ge(pt_odd, j) if g == 0 else pe.wait_ge(pt_even, 2 * j)
                for c in range(4 if wide else 2):
                    ins = pe.transpose(t_bank[(slot + g) % 2][:, c * SPAN:(c + 1) * SPAN],
                                       probs[:, g, c * SPAN:(c + 1) * SPAN], idf[:, :])
                ins.then_inc(pt_done, 1)

            def sums(j, slot, wide, g):
                if g == 1:
                    pe.wait_ge(pt_odd, j + 1)
                else:
                    pe.wait_ge(pt_even, 2 * j + (1 if g == 0 else 2))
                if g == 0:
                    pe.wait_ge(v_ready, j + 3)
                    pe.wait_ge(o_ready, 2 * j + 1)
                for hh in range(2):
                    h = 2 * g + hh
                    out = o_bank[slot][:, h * OW:(h + 1) * OW]
                    if wide:
                        pe.matmul(out, probs_t[:, g, 2 * hh * SPAN:(2 * hh + 1) * SPAN], v_tok[:, 1 - slot, h, :], start=True, stop=False)
                        ins = pe.matmul(out, probs_t[:, g, (2 * hh + 1) * SPAN:(2 * hh + 2) * SPAN], v_tok[:, slot, h, :], start=False, stop=True)
                    else:
                        ins = pe.matmul(out, probs_t[:, g, hh * SPAN:(hh + 1) * SPAN], v_tok[:, slot, h, :], start=True, stop=True)
                if g == GROUPS - 1:
                    ins.then_inc(o_done, 1)

            def body(j, slot, wide, last_fresh=False):
                scores(j, slot, wide, 0, False)
                turn_probs(j - 1, 1 - slot, wide, 0, last_fresh)
                scores(j, slot, wide, 1, False)
                turn_probs(j - 1, 1 - slot, wide, 1, last_fresh)
                sums(j - 1, 1 - slot, wide, 0)
                turn_probs(j - 1, 1 - slot, wide, 2, last_fresh)
                scores(j, slot, wide, 2, False)
                sums(j - 1, 1 - slot, wide, 1)
                turn_v(j, slot, wide)
                sums(j - 1, 1 - slot, wide, 2)

            def start(j, slot, wide, fresh):
                for g in range(GROUPS):
                    scores(j, slot, wide, g, fresh)
                turn_v(j, slot, wide)

            def finish(j, slot, wide):
                for g in range(GROUPS):
                    turn_probs(j, slot, wide, g, False)
                    if g:
                        sums(j, slot, wide, g - 1)
                sums(j, slot, wide, GROUPS - 1)

            start(0, 0, True, True)
            body(1, 1, True, True)
            with pe.Fori(0, PAIRED // 2 - 1) as i:
                body(2 * i + 2, 0, True)
                body(2 * i + 3, 1, True)
            finish(PAIRED - 1, 1, True)
            start(PAIRED, 0, False, False)
            body(PAIRED + 1, 1, False)
            with pe.Fori(0, SINGLE // 2 - 1) as i:
                body(2 * i + (PAIRED + 2), 0, False)
                body(2 * i + (PAIRED + 3), 1, False)
            finish(PAIRED + SINGLE - 1, 1, False)
GH = 4
DK = 48
DV = 96
GP = GH // 2
CH = 128
CHUNKS = NB // CH
RANK = 16
TEMP = 16.0
LIMIT = 80.0 * TEMP
AW = GH * DV


def gated_linear_attention(nc, proj_t, gate_w, gate_b, chunk_starts, causal, ident, norm_gain, mix_t):
    with ExitStack() as ctx:
        used = []
        ctx.callback(free_semaphores, nc, used)

        def sb(name, shape, dt=F32):
            return ctx.enter_context(nc.sbuf_tensor("gl_" + name, shape, dt))

        def sem(name):
            used.append(nc.alloc_semaphore("gl_" + name))
            return used[-1]

        q_in = sb("q_in", [P, 2, GP, NB])
        k_in = sb("k_in", [P, 2, GP, NB])
        v_in = sb("v_in", [P, 2, 3, NB])
        low_rank = sb("low_rank", [RANK, 2, NB])
        w_gate = sb("w_gate", [RANK, GP, P])
        b_gate = sb("b_gate", [P, GP])
        starts = sb("starts", [P, NB])
        keep = sb("keep", [P, 2, CH], mybir.dt.uint32)
        idf = sb("idf", [P, P])
        gain = sb("gain", [P, 3])
        eps = sb("eps", [P, 1])
        z = sb("z", [P, GP, NB])
        z_abs = sb("z_abs", [P, GP, NB])
        log_g = sb("log_g", [P, GP, NB])
        cum = sb("cum", [P, GP, NB])
        to_mid = sb("to_mid", [P, GP, NB])
        to_end = sb("to_end", [P, GP, NB])
        to_border = sb("to_border", [P, GP, NB])
        e_mid = sb("e_mid", [P, GP, NB])
        e_mid_inv = sb("e_mid_inv", [P, GP, NB])
        e_cum = sb("e_cum", [P, 2, GP, NB])
        q_mid = sb("q_mid", [P, 2, GP, NB])
        k_mid = sb("k_mid", [P, 2, GP, NB])
        q_start = sb("q_start", [P, 2, GP, NB])
        k_end = sb("k_end", [P, 2, GP, NB])
        qk_border = sb("qk_border", [P, 2, GP, NB])
        v_tok = sb("v_tok", [P, 2, AW])
        k_tok = sb("k_tok", [P, 2, GP, P])
        scores = sb("scores", [P, 2, GH, CH])
        state = sb("state", [P, 2, GP, DV])
        o_all = sb("o_all", [P, S // CH, AW])
        square = sb("square", [P, 2, AW * CHUNKS])
        ss = sb("ss", [P, S // CH * GH])
        rstd = sb("rstd", [P, S // CH * GH])
        o_n = sb("o_n", [P, CHUNKS, AW])
        gate_r = sb("gate_r", [P, 3, S])

        def bank(name):
            return ctx.enter_context(nc.psum_tensor("gl_bank_" + name, [P, NB], F32))

        z_bank, v_bank, k_bank, st_bank = bank("z"), bank("v"), bank("k"), bank("st")
        s_bank = [bank(f"s{i}") for i in range(2)]
        o_bank = [bank(f"o{i}") for i in range(2)]

        consts_in = sem("consts_in")
        zeroed = sem("zeroed")
        loaded = [sem(f"loaded{i}") for i in range(2)]
        low_rank_loaded = [sem(f"low_rank_loaded{i}") for i in range(2)]
        r_loaded = sem("r_loaded")
        z_ready = sem("z_ready")
        z_copied = sem("z_copied")
        z_abs_ready = sem("z_abs_ready")
        act_step = sem("act_step")
        dve_step = sem("dve_step")
        exps_ready = sem("exps_ready")
        factors_ready = sem("factors_ready")
        turned = sem("turned")
        tok_ready = sem("tok_ready")
        scores_done = sem("scores_done")
        scores_ready = sem("scores_ready")
        update_done = sem("update_done")
        state_ready = sem("state_ready")
        o_done = sem("o_done")
        o_ready = sem("o_ready")
        silu_ready = sem("silu_ready")
        gated_ready = sem("gated_ready")
        square_ready = sem("square_ready")
        ss_ready = sem("ss_ready")
        rms_ready = sem("rms_ready")
        rstd_ready = sem("rstd_ready")
        o_n_ready = sem("o_n_ready")
        o_turned = sem("o_turned")
        out_ready = sem("out_ready")
        stored = sem("stored")

        block = ctx.enter_context(nc.Block())
        PRE = 8
        LOADS = 3

        def col(chunk, lo=0, hi=CH):
            return slice(chunk * CH + lo, chunk * CH + hi)

        @block.sync
        def _(sp):
            def load(n, p):
                at = bass.ds(n * NB, NB)
                sp.dma_start(low_rank[:, p, :], proj_t[T_AQ, GLR_ROW:GLR_ROW + RANK, at]).then_inc(low_rank_loaded[p], 16)
                sp.dma_start(q_in[:, p, :, :], proj_t[T_AQ:T_AQ + 2, :, at].rearrange("g p s -> p g s")).then_inc(loaded[p], 16)
                sp.dma_start(k_in[:, p, :, :], proj_t[T_AK:T_AK + 2, :, at].rearrange("g p s -> p g s")).then_inc(loaded[p], 16)
                sp.dma_start(v_in[:, p, :, :], proj_t[T_AV:T_AV + 3, :, at].rearrange("g p s -> p g s")).then_inc(loaded[p], 16)

            for dst, src in ((w_gate[:, :, :], gate_w), (b_gate[:, :], gate_b), (starts[:, :], chunk_starts),
                             (keep[:, :, :], causal), (idf[:, :], ident), (gain[:, :], norm_gain)):
                sp.dma_start(dst, src).then_inc(consts_in, 16)

            load(0, 0)
            sp.wait_ge(loaded[0], 16 * LOADS)
            load(1, 1)
            sp.dma_start(gate_r[:, :, :], proj_t[T_AR:T_AR + 3].rearrange("g p s -> p g s")).then_inc(r_loaded, 16)
            for n in range(2, BLOCKS):
                sp.wait_ge(factors_ready, n - 1)
                sp.wait_ge(turned, CHUNKS * (n - 1))
                load(n, n % 2)
            for n in range(BLOCKS):
                sp.wait_ge(out_ready, 3 * (n + 1))
                sp.dma_start(mix_t[0:3, :, n * NB:(n + 1) * NB].rearrange("g p s -> p g s"), gate_r[:, :, n * NB:(n + 1) * NB]
                             ).then_inc(stored, 16)
            sp.wait_ge(stored, 16 * BLOCKS)

        @block.tensor
        def _(pe):
            pe.wait_ge(consts_in, 16 * 6)

            def gate(n, p):
                pe.wait_ge(low_rank_loaded[p], 16 * (n // 2 + 1))
                for m in range(GP):
                    u = GP * n + m
                    if u:
                        pe.wait_ge(z_copied, u)
                    pe.matmul(z_bank[:, :], w_gate[:, m, :], low_rank[:, p, :], start=True, stop=True).then_inc(z_ready, 1)

            def turn(c, chunk, p):
                if c:
                    pe.wait_ge(tok_ready, c)
                for g in range(3):
                    pe.transpose(v_bank[:, g * P:(g + 1) * P], v_in[:, p, g, col(chunk)], idf[:, :])
                for m in range(GP):
                    ins = pe.transpose(k_bank[:, m * P:(m + 1) * P], k_end[:, p, m, col(chunk)], idf[:, :])
                ins.then_inc(turned, 1)

            def inner(c, chunk, p):
                if c:
                    pe.wait_ge(scores_ready, c)
                for h in range(GH):
                    m, b = h // 2, h % 2
                    rows = slice(64 * b, 64 * b + DK)
                    at = m * CH
                    pe.matmul(s_bank[b][0:64, at:at + 64], k_mid[rows, p, m, col(chunk, 0, 64)], q_mid[rows, p, m, col(chunk, 0, 64)],
                              start=True, stop=True)
                    pe.matmul(s_bank[b][64:128, at + 64:at + 128], k_mid[rows, p, m, col(chunk, 64)], q_mid[rows, p, m, col(chunk, 64)],
                              start=True, stop=True)
                    ins = pe.matmul(s_bank[b][0:64, at + 64:at + 128], qk_border[rows, p, m, col(chunk, 0, 64)],
                                    qk_border[rows, p, m, col(chunk, 64)], start=True, stop=True)
                ins.then_inc(scores_done, 1)

            def update(c):
                pe.wait_ge(tok_ready, c + 1)
                if c:
                    pe.wait_ge(state_ready, c)
                for h in range(GH):
                    m, b = h // 2, h % 2
                    ins = pe.matmul(st_bank[64 * b:64 * b + 64, m * DV:(m + 1) * DV], k_tok[:, c % 2, m, 64 * b:64 * b + 64],
                                    v_tok[:, c % 2, h * DV:(h + 1) * DV], start=True, stop=True)
                ins.then_inc(update_done, 1)

            def output(c, chunk, p):
                pe.wait_ge(scores_ready, c + 1)
                if c:
                    pe.wait_ge(o_ready, c)
                    pe.wait_ge(state_ready, c)
                for m in range(GP):
                    for b in range(2):
                        h = 2 * m + b
                        out = o_bank[b][:, m * DV:(m + 1) * DV]
                        pe.matmul(out, scores[:, c % 2, h, :], v_tok[:, c % 2, h * DV:(h + 1) * DV], start=True, stop=False)
                        ins = pe.matmul(out, q_start[64 * b:64 * b + DK, p, m, col(chunk)], state[64 * b:64 * b + DK, c % 2, m, :],
                                        start=False, stop=True)
                ins.then_inc(o_done, 1)

            pe.wait_ge(zeroed, 3)
            gate(0, 0)
            pe.wait_ge(loaded[0], 16 * LOADS)
            for n in range(BLOCKS):
                pe.wait_ge(factors_ready, n + 1)
                for chunk in range(CHUNKS):
                    c = CHUNKS * n + chunk
                    turn(c, chunk, n % 2)
                    inner(c, chunk, n % 2)
                    if chunk == 0 and n + 1 < BLOCKS:
                        gate(n + 1, (n + 1) % 2)
                    update(c)
                    output(c, chunk, n % 2)

            for n in range(BLOCKS):
                for t in range(CHUNKS):
                    pe.wait_ge(o_n_ready, CHUNKS * n + t + 1)
                    for g in range(3):
                        if t == 0 and n:
                            pe.wait_ge(out_ready, 3 * (n - 1) + g + 1)
                        ins = pe.transpose([v_bank, k_bank, st_bank][g][:, t * CH:(t + 1) * CH], o_n[:, t, g * P:(g + 1) * P], idf[:, :])
                    ins.then_inc(o_turned, 1)

        @block.scalar
        def _(act):
            act.wait_ge(consts_in, 16 * 6)

            def gate(n):
                for m in range(GP):
                    u = GP * n + m
                    act.wait_ge(z_ready, u + 1)
                    if n:
                        act.wait_ge(dve_step, PRE * (n - 1) + 1)
                    act.activation(z[:, m, :], z_bank[:, :], ACT.Identity, bias=b_gate[:, m:m + 1]).then_inc(z_copied, 1)
                act.wait_ge(z_copied, GP * (n + 1))
                act.activation(z_abs[:, :, :], z[:, :, :], ACT.Abs).then_inc(z_abs_ready, 1)
                act.wait_ge(z_abs_ready, n + 1)
                act.activation(z_abs[:, :, :], z_abs[:, :, :], ACT.Exp, scale=-1.0).then_inc(act_step, 1)
                act.wait_ge(act_step, 2 * n + 1)
                act.activation(z_abs[:, :, :], z_abs[:, :, :], ACT.Ln, bias=1.0).then_inc(act_step, 1)

            def exps(n):
                if n:
                    act.wait_ge(factors_ready, n)
                if n >= 2:
                    act.wait_ge(state_ready, CHUNKS * (n - 1))
                act.wait_ge(dve_step, PRE * n + 3)
                act.activation(e_cum[:, n % 2, :, :], cum[:, :, :], ACT.Exp, scale=1.0 / TEMP).then_inc(exps_ready, 1)
                act.wait_ge(dve_step, PRE * n + 5)
                act.activation(e_mid[:, :, :], to_mid[:, :, :], ACT.Exp, scale=1.0 / TEMP).then_inc(exps_ready, 1)
                act.activation(e_mid_inv[:, :, :], to_mid[:, :, :], ACT.Exp, scale=-1.0 / TEMP).then_inc(exps_ready, 1)
                act.wait_ge(dve_step, PRE * n + 8)
                act.activation(to_end[:, :, :], to_end[:, :, :], ACT.Exp, scale=1.0 / TEMP).then_inc(exps_ready, 1)
                act.activation(to_border[:, :, :], to_border[:, :, :], ACT.Exp, scale=1.0 / TEMP).then_inc(exps_ready, 1)

            def tokens(c):
                act.wait_ge(turned, c + 1)
                if c >= 2:
                    act.wait_ge(o_done, c - 1)
                act.activation(v_tok[:, c % 2, :], v_bank[:, 0:AW], ACT.Copy)
                act.activation(k_tok[:, c % 2, :, :], k_bank[:, 0:GP * P].rearrange("p (m k) -> p m k", m=GP), ACT.Copy
                               ).then_inc(tok_ready, 1)

            def output(c):
                act.wait_ge(o_done, c + 1)
                for b in range(2):
                    ins = act.activation(o_all[:, c, :].rearrange("p (m b v) -> p m b v", m=GP, b=2)[:, :, b, :],
                                         o_bank[b][:, 0:GP * DV].rearrange("p (m v) -> p m v", m=GP), ACT.Copy)
                ins.then_inc(o_ready, 1)

            gate(0)
            exps(0)
            for n in range(BLOCKS):
                for chunk in range(CHUNKS):
                    c = CHUNKS * n + chunk
                    tokens(c)
                    if chunk == 0 and n + 1 < BLOCKS:
                        gate(n + 1)
                    output(c)
                    if chunk == CHUNKS - 2 and n + 1 < BLOCKS:
                        exps(n + 1)
                if n == 0:
                    act.wait_ge(r_loaded, 16)
                    for g in range(3):
                        act.activation(gate_r[:, g, :], gate_r[:, g, :], ACT.Silu).then_inc(silu_ready, 1)
            act.wait_ge(ss_ready, S // CH // 4)
            act.activation(rstd[:, :], ss[:, :], ACT.Sqrt, bias=eps[:, :], scale=1.0 / DV).then_inc(rms_ready, 1)

        @block.gpsimd
        def _(pool):
            def square_outputs(n):
                if n >= 2:
                    pool.wait_ge(ss_ready, n - 1)
                for half in range(2):
                    at = slice(half * AW * CHUNKS // 2, (half + 1) * AW * CHUNKS // 2)
                    pool.wait_ge(o_ready, CHUNKS * n + CHUNKS // 2 * (half + 1))
                    two = o_all[:, CHUNKS * n + CHUNKS // 2 * half:CHUNKS * n + CHUNKS // 2 * (half + 1), :].rearrange("p c v -> p (c v)")
                    ins = pool.tensor_tensor(square[:, n % 2, at], two, two, ALU.mult)
                ins.then_inc(square_ready, 1)

            pool.wait_ge(consts_in, 16 * 6)
            square_outputs(0)
            pool.wait_ge(silu_ready, 3)
            for g in range(3):
                pool.tensor_scalar(gate_r[:, g, :], gate_r[:, g, :], gain[:, g:g + 1], None, ALU.mult).then_inc(gated_ready, 1)
            for n in range(1, BLOCKS):
                square_outputs(n)

        @block.vector
        def _(dve):
            dve.memset(scores[:, :, :, :], 0.0).then_inc(zeroed, 1)
            dve.memset(state[:, 0, :, :], 0.0).then_inc(zeroed, 1)
            dve.memset(eps[:, :], EPS).then_inc(zeroed, 1)
            dve.wait_ge(zeroed, 3)
            dve.wait_ge(consts_in, 16 * 6)

            def halves(x):
                return x[:, :, :].rearrange("p m (c j) -> p (m c) j", j=64)

            def chunked(x):
                return x[:, :, :].rearrange("p m (c j) -> p (m c) j", j=CH)

            def decays(n):
                dve.wait_ge(act_step, 2 * n + 2)
                if n:
                    dve.wait_ge(exps_ready, 5 * n)
                    dve.wait_ge(dve_step, PRE * n)
                dve.scalar_tensor_tensor(out=log_g[:, :, :], in0=z[:, :, :], scalar=0.0, in1=z_abs[:, :, :], op0=ALU.min,
                                         op1=ALU.subtract).then_inc(dve_step, 1)
                dve.wait_ge(dve_step, PRE * n + 1)
                for m in range(GP):
                    dve.tensor_tensor_scan(cum[:, m, :], starts[:, :], log_g[:, m, :], 0.0, ALU.mult, ALU.add).then_inc(dve_step, 1)
                dve.wait_ge(dve_step, PRE * n + 3)
                mid = halves(cum)[:, :, 31:32].to_broadcast([P, GP * NB // 64, 64])
                dve.tensor_tensor(halves(to_mid), halves(cum), mid, ALU.subtract).then_inc(dve_step, 1)
                dve.wait_ge(dve_step, PRE * n + 4)
                dve.tensor_scalar(to_mid[:, :, :], to_mid[:, :, :], LIMIT, -LIMIT, ALU.min, ALU.max).then_inc(dve_step, 1)
                if n:
                    dve.wait_ge(factors_ready, n)
                end = chunked(cum)[:, :, CH - 1:CH].to_broadcast([P, GP * CHUNKS, CH])
                dve.tensor_tensor(chunked(to_end), end, chunked(cum), ALU.subtract).then_inc(dve_step, 1)
                border = chunked(cum)[:, :, 63:64].to_broadcast([P, GP * CHUNKS, 64])
                dve.tensor_tensor(chunked(to_border)[:, :, 0:64], border, chunked(cum)[:, :, 0:64], ALU.subtract).then_inc(dve_step, 1)
                dve.tensor_tensor(chunked(to_border)[:, :, 64:CH], chunked(cum)[:, :, 64:CH], border, ALU.subtract).then_inc(dve_step, 1)

            def factors(n, p):
                if n >= 2:
                    dve.wait_ge(o_done, CHUNKS * (n - 1))
                dve.wait_ge(loaded[p], 16 * LOADS * (n // 2 + 1))
                q, k = q_in[:, p, :, :], k_in[:, p, :, :]
                scale = DK ** -0.5

                def scaled(out, x, e):
                    return dve.scalar_tensor_tensor(out=out, in0=x, scalar=scale, in1=e, op0=ALU.mult, op1=ALU.mult)

                dve.wait_ge(exps_ready, 5 * n + 1)
                scaled(q_start[:, p, :, :], q, e_cum[:, p, :, :])
                dve.wait_ge(exps_ready, 5 * n + 2)
                scaled(q_mid[:, p, :, :], q, e_mid[:, :, :])
                dve.wait_ge(exps_ready, 5 * n + 3)
                dve.tensor_tensor(k_mid[:, p, :, :], k, e_mid_inv[:, :, :], ALU.mult)
                dve.wait_ge(exps_ready, 5 * n + 4)
                dve.tensor_tensor(k_end[:, p, :, :], k, to_end[:, :, :], ALU.mult)
                dve.wait_ge(exps_ready, 5 * n + 5)
                kc = k.rearrange("p m (c j) -> p (m c) j", j=CH)
                qc = q.rearrange("p m (c j) -> p (m c) j", j=CH)
                dve.tensor_tensor(chunked(qk_border[:, p, :, :])[:, :, 0:64], kc[:, :, 0:64], chunked(to_border)[:, :, 0:64], ALU.mult)
                scaled(chunked(qk_border[:, p, :, :])[:, :, 64:CH], qc[:, :, 64:CH], chunked(to_border)[:, :, 64:CH]).then_inc(factors_ready, 1)

            def mask(c):
                dve.wait_ge(scores_done, c + 1)
                if c >= 2:
                    dve.wait_ge(o_done, c - 1)
                for b in range(2):
                    sc = scores[:, c % 2, :, :].rearrange("p (m b) i -> p m b i", b=2)[:, :, b, :]
                    ps = s_bank[b][:, 0:GP * CH].rearrange("p (m i) -> p m i", m=GP)
                    dve.copy_predicated(sc[0:64], keep[0:64, :, :], ps[0:64])
                    ins = dve.copy_predicated(sc[64:128, :, 64:CH], keep[64:128, :, 64:CH], ps[64:128, :, 64:CH])
                ins.then_inc(scores_ready, 1)

            def advance(c, chunk, p):
                dve.wait_ge(update_done, c + 1)
                if c:
                    dve.wait_ge(state_ready, c)
                    dve.wait_ge(o_done, c)
                for m in range(GP):
                    ins = dve.scalar_tensor_tensor(out=state[:, (c + 1) % 2, m, :], in0=state[:, c % 2, m, :],
                                                   scalar=e_cum[:, p, m, (chunk + 1) * CH - 1:(chunk + 1) * CH],
                                                   in1=st_bank[:, m * DV:(m + 1) * DV], op0=ALU.mult, op1=ALU.add)
                ins.then_inc(state_ready, 1)

            def sum_squares(n):
                dve.wait_ge(square_ready, n + 1)
                dve.tensor_reduce(ss[:, CHUNKS * GH * n:CHUNKS * GH * (n + 1)], square[:, n % 2, :].rearrange("p (h v) -> p h v", v=DV),
                                  AX.X, ALU.add).then_inc(ss_ready, 1)

            decays(0)
            factors(0, 0)
            for n in range(BLOCKS):
                for chunk in range(CHUNKS):
                    c = CHUNKS * n + chunk
                    mask(c)
                    if chunk == CHUNKS - 1 and n + 1 < BLOCKS:
                        factors(n + 1, (n + 1) % 2)
                    advance(c, chunk, n % 2)
                    if chunk == CHUNKS - 3 and n + 1 < BLOCKS:
                        decays(n + 1)
                    if chunk == 0 and n:
                        sum_squares(n - 1)
            sum_squares(BLOCKS - 1)
            dve.wait_ge(rms_ready, 1)
            dve.reciprocal(rstd[:, :], rstd[:, :]).then_inc(rstd_ready, 1)
            dve.wait_ge(rstd_ready, 1)
            dve.wait_ge(gated_ready, 3)

            def scale_outputs(n):
                for t in range(CHUNKS):
                    c = CHUNKS * n + t
                    if n:
                        dve.wait_ge(o_turned, CHUNKS * (n - 1) + t + 1)
                    dve.tensor_tensor(o_n[:, t, :].rearrange("p (h v) -> p h v", v=DV), o_all[:, c, :].rearrange("p (h v) -> p h v", v=DV),
                                      rstd[:, GH * c:GH * (c + 1)].unsqueeze(2).to_broadcast([P, GH, DV]), ALU.mult).then_inc(o_n_ready, 1)

            def gate_outputs(n):
                dve.wait_ge(o_turned, CHUNKS * (n + 1))
                for g in range(3):
                    at = gate_r[:, g, n * NB:(n + 1) * NB]
                    dve.tensor_tensor(at, [v_bank, k_bank, st_bank][g][:, :], at, ALU.mult).then_inc(out_ready, 1)

            scale_outputs(0)
            for n in range(1, BLOCKS):
                scale_outputs(n)
                gate_outputs(n - 1)
            gate_outputs(BLOCKS - 1)


LW = 256
LT = LW // P
LTAPS = 4
C_TAP, C_BIAS, C_BA, C_BX, C_LAM, C_NORM = 0, 4, 5, 6, 7, 8


def recurrent_and_patterns(nc, proj_t, consts, gate_w, o_scratch, ident, swa_gain, mix_t):
    TURNS = S // (2 * P)
    PATS = len(DILATIONS)
    CW = HEADS * HD
    with ExitStack() as ctx:
        used = []
        ctx.callback(free_semaphores, nc, used)

        def sb(name, shape, dt=F32):
            return ctx.enter_context(nc.sbuf_tensor(name, shape, dt))

        def sem(name):
            used.append(nc.alloc_semaphore(name))
            return used[-1]

        x_in = sb("lr_x_in", [P, LT, LTAPS - 1 + S])
        gate = sb("lr_gate", [P, LT, S])
        xc = sb("lr_xc", [P, LT, S])
        r = sb("lr_r", [P, LT, S])
        i_x = sb("lr_i_x", [P, LT, S])
        root = sb("lr_root", [P, LT, S])
        a2 = sb("lr_a2", [P, LT, S])
        lr_rstd = sb("lr_rstd", [P, S])
        c = sb("lr_c", [P, LT, C_NORM + 1])
        w = sb("lr_w", [P, LT, 2, P])
        sp8 = sb("lr_sp8", [P, LT, 4])
        ones = sb("lr_ones", [P, P])
        eps = sb("lr_eps", [P, 1])
        lr_banks = [ctx.enter_context(nc.psum_tensor(f"lr_bank{i}", [P, NB], F32)) for i in range(2)]

        rows = sb("cb_rows", [P, 2, PATS, 2, ROW])
        neg = sb("cb_neg", [P, PATS, S // P, HEADS])
        low = sb("cb_low", [P, S // P, HEADS])
        weight = sb("cb_weight", [P, PATS, S // P, HEADS])
        total = sb("cb_total", [P, 2, HEADS, OW])
        inverse = sb("cb_inverse", [P, 2, HEADS, 1])
        o_all = sb("cb_o_all", [P, S // P, CW])
        o_squares = sb("cb_squares", [P, 2, 2, CW])
        ss = sb("cb_ss", [P, S // P])
        cb_rstd = sb("cb_rstd", [P, S // P])
        o_n = sb("cb_o_n", [P, 4, CW])
        out = sb("cb_out", [P, 2, GROUPS, NB])
        idf = sb("cb_idf", [P, P])
        gain = sb("cb_gain", [P, GROUPS])
        cb_banks = [ctx.enter_context(nc.psum_tensor(f"cb_bank{i}", [P, NB], F32)) for i in range(2 * GROUPS)]

        lr_consts_in = sem("lr_consts_in")
        x_loaded = [sem(f"lr_x_loaded{m}") for m in range(LT)]
        gate_loaded = sem("lr_gate_loaded")
        zeroed = sem("lr_zeroed")
        small = sem("lr_small")
        small_act = sem("lr_small_act")
        last_tap_ready = sem("lr_last_tap_ready")
        conv_step = sem("lr_conv_step")
        gates_done = sem("lr_gates_done")
        gates_ready = sem("lr_gates_ready")
        tanh_ready = sem("lr_tanh_ready")
        a_ready = sem("lr_a_ready")
        a2_ready = sem("lr_a2_ready")
        power_ready = sem("lr_power_ready")
        root_ready = sem("lr_root_ready")
        ix_ready = sem("lr_ix_ready")
        u_ready = sem("lr_u_ready")
        h_ready = sem("lr_h_ready")
        gelu_ready = sem("lr_gelu_ready")
        hg_ready = sem("lr_hg_ready")
        sq_ready = sem("lr_sq_ready")
        sums_done = sem("lr_sums_done")
        lr_std_ready = sem("lr_std_ready")
        lr_rstd_ready = sem("lr_rstd_ready")
        lr_out_ready = sem("lr_out_ready")
        lr_stored = sem("lr_stored")

        cb_consts_in = sem("cb_consts_in")
        neg_in = sem("cb_neg_in")
        loaded = [sem(f"cb_loaded{i}") for i in range(2)]
        prepared = sem("cb_prepared")
        weight_ready = sem("cb_weight_ready")
        weighted = sem("cb_weighted")
        step = sem("cb_step")
        squared = sem("cb_squared")
        summed = sem("cb_summed")
        cb_std_ready = sem("cb_std_ready")
        cb_rstd_ready = sem("cb_rstd_ready")
        o_n_ready = sem("cb_o_n_ready")
        turned = sem("cb_turned")
        cb_out_ready = sem("cb_out_ready")
        cb_stored = [sem(f"cb_stored{i}") for i in range(2)]
        FIRST_SHARED = 2
        STEPS = 5

        block = ctx.enter_context(nc.Block())

        def blk(b):
            return slice(b * NB, (b + 1) * NB)

        def weighted_after(i, to_come):
            return 2 * (i + 1) + max(0, i + 1 - FIRST_SHARED) - to_come

        def sums_of(i, a):
            return rows[:, i % 2, a, :, 0:NEG].rearrange("p t (h d) -> p t h d", d=OW)

        def weight_of(i, a):
            return weight[:, a, 2 * i:2 * i + 2, :].unsqueeze(3).to_broadcast([P, 2, HEADS, OW])

        @block.sync
        def _(sp):
            sp.dma_start(c[:, :, :], consts).then_inc(lr_consts_in, 16)
            sp.dma_start(w[:, :, :, :], gate_w).then_inc(lr_consts_in, 16)
            for m in range(LT):
                sp.dma_start(x_in[:, m, LTAPS - 1:], proj_t[T_BI + m]).then_inc(x_loaded[m], 16)
            sp.wait_ge(x_loaded[0], 16)
            for a in range(PATS):
                sp.dma_start(neg[:, a, :, :], o_scratch[a].rearrange("(t p) r -> p t r", p=P)[:, :, NEG:ROW]).then_inc(neg_in, 16)

            def load_rows(i):
                if i >= 2:
                    sp.wait_ge(step, STEPS * (i - 1))
                for a in range(PATS):
                    at = o_scratch[a, 2 * P * i:2 * P * (i + 1), :].rearrange("(t p) r -> p t r", p=P)
                    sp.dma_start(rows[:, i % 2, a, :, :], at).then_inc(loaded[i % 2], 16)

            load_rows(0)
            load_rows(1)
            sp.dma_start(gate[:, :, :], proj_t[T_BG:T_BG + LT].rearrange("g p s -> p g s")).then_inc(gate_loaded, 16)
            sp.dma_start(idf[:, :], ident).then_inc(cb_consts_in, 16)
            sp.dma_start(gain[:, :], swa_gain).then_inc(cb_consts_in, 16)
            for i in range(2, TURNS):
                load_rows(i)

            def lr_store(b):
                sp.wait_ge(lr_out_ready, LT * (b + 1))
                sp.dma_start(mix_t[3:5, :, blk(b)].rearrange("g p s -> p g s"), i_x[:, :, blk(b)]).then_inc(lr_stored, 16)

            def cb_store(b):
                sp.wait_ge(cb_out_ready, GROUPS * (b + 1))
                sp.dma_start(mix_t[5:8, :, blk(b)].rearrange("g p s -> p g s"), out[:, b % 2, :, :]).then_inc(cb_stored[b % 2], 16)

            lr_store(0)
            lr_store(1)
            lr_store(2)
            cb_store(0)
            lr_store(3)
            for b in range(1, BLOCKS):
                cb_store(b)
            sp.wait_ge(lr_stored, 16 * BLOCKS)
            for p in range(2):
                sp.wait_ge(cb_stored[p], 16 * BLOCKS // 2)

        @block.vector
        def _(dve):
            dve.memset(x_in[:, :, 0:LTAPS - 1], 0.0).then_inc(zeroed, 1)
            dve.memset(ones[:, :], 1.0).then_inc(zeroed, 1)
            dve.memset(eps[:, :], EPS).then_inc(zeroed, 1)
            dve.wait_ge(zeroed, 3)

            def log_weights():
                dve.wait_ge(neg_in, 16 * PATS)
                dve.tensor_tensor(low[:, :, :], neg[:, 0, :, :], neg[:, 1, :, :], ALU.min).then_inc(prepared, 1)
                dve.wait_ge(prepared, 1)
                dve.tensor_tensor(low[:, :, :], low[:, :, :], neg[:, 2, :, :], ALU.min).then_inc(prepared, 1)
                dve.wait_ge(prepared, 2)
                for a in range(PATS):
                    dve.tensor_tensor(weight[:, a, :, :], low[:, :, :], neg[:, a, :, :], ALU.subtract).then_inc(prepared, 1)

            def turn(i):
                def done(ins, count):
                    ins.then_inc(step, 1)
                    dve.wait_ge(step, STEPS * i + count)

                dve.wait_ge(loaded[i % 2], 16 * PATS * (i // 2 + 1))
                dve.wait_ge(weight_ready, 1)
                sums = [sums_of(i, a) for a in range(PATS)]
                if i < FIRST_SHARED:
                    done(dve.tensor_tensor(sums[0], sums[0], weight_of(i, 0), ALU.mult), 1)
                else:
                    dve.sem_inc(step, 1)
                dve.wait_ge(weighted, weighted_after(i, 1))
                done(dve.tensor_tensor(total[:, :, :, :], sums[0], sums[1], ALU.add), 2)
                dve.wait_ge(weighted, weighted_after(i, 0))
                done(dve.tensor_tensor(total[:, :, :, :], total[:, :, :, :], sums[2], ALU.add), 3)
                done(dve.reciprocal(inverse[:, :, :, :], total[:, :, :, HD:OW]), 4)
                o = o_all[:, 2 * i:2 * i + 2, :]
                done(dve.tensor_tensor(o.rearrange("p t (h d) -> p t h d", d=HD), total[:, :, :, 0:HD],
                                       inverse[:, :, :, :].to_broadcast([P, 2, HEADS, HD]), ALU.mult), 5)
                if i:
                    sum_squares(i - 1)

            def sum_squares(i):
                dve.wait_ge(squared, i + 1)
                dve.tensor_reduce(ss[:, 2 * i:2 * i + 2], o_squares[:, i % 2, :, :], AX.X, ALU.add).then_inc(summed, 1)

            def conv(m):
                dve.wait_ge(last_tap_ready, m + 1)
                dve.wait_ge(x_loaded[m], 16)
                for t in range(LTAPS - 1):
                    if t:
                        dve.wait_ge(conv_step, (LTAPS - 1) * m + t)
                    dve.scalar_tensor_tensor(out=xc[:, m, :], in0=x_in[:, m, t:t + S], scalar=c[:, m, t:t + 1], in1=xc[:, m, :],
                                             op0=ALU.mult, op1=ALU.add).then_inc(conv_step, 1)

            def softplus():
                dve.wait_ge(small_act, 3)
                dve.tensor_scalar(sp8[:, :, 2:3], c[:, :, C_LAM:C_LAM + 1], -1.0, 0.0, ALU.mult, ALU.max).then_inc(small, 1)
                dve.wait_ge(small, 1)
                dve.tensor_tensor(sp8[:, :, 1:2], sp8[:, :, 1:2], sp8[:, :, 2:3], ALU.add).then_inc(small, 1)
                dve.wait_ge(small, 2)
                dve.tensor_scalar(sp8[:, :, 2:3], sp8[:, :, 1:2], 8.0, None, ALU.mult).then_inc(small, 1)
                dve.tensor_scalar(sp8[:, :, 3:4], sp8[:, :, 1:2], -8.0, None, ALU.mult).then_inc(small, 1)

            def power(m):
                dve.wait_ge(a2_ready, m + 1)
                dve.wait_ge(tanh_ready, m + 1)
                dve.scalar_tensor_tensor(out=root[:, m, :], in0=a2[:, m, :], scalar=1.0, in1=root[:, m, :], op0=ALU.add,
                                         op1=ALU.mult).then_inc(power_ready, 1)

            def recurrence(m):
                dve.wait_ge(root_ready, m + 1)
                dve.wait_ge(ix_ready, m + 1)
                dve.tensor_tensor(root[:, m, :], root[:, m, :], i_x[:, m, :], ALU.mult).then_inc(u_ready, 1)
                dve.wait_ge(u_ready, m + 1)
                dve.tensor_tensor_scan(xc[:, m, :], r[:, m, :], root[:, m, :], 0.0, ALU.mult, ALU.add).then_inc(h_ready, 1)
                dve.wait_ge(h_ready, m + 1)
                dve.wait_ge(gelu_ready, m + 1)
                dve.tensor_tensor(xc[:, m, :], xc[:, m, :], gate[:, m, :], ALU.mult).then_inc(hg_ready, 1)

            def lr_normalise(b):
                dve.wait_ge(lr_std_ready, b + 1)
                dve.reciprocal(lr_rstd[:, blk(b)], lr_rstd[:, blk(b)]).then_inc(lr_rstd_ready, 1)
                dve.wait_ge(lr_rstd_ready, b + 1)
                for m in range(LT):
                    dve.scalar_tensor_tensor(out=i_x[:, m, blk(b)], in0=xc[:, m, blk(b)], scalar=c[:, m, C_NORM:C_NORM + 1],
                                             in1=lr_rstd[:, blk(b)], op0=ALU.mult, op1=ALU.mult).then_inc(lr_out_ready, 1)

            dve.wait_ge(lr_consts_in, 32)
            conv(0)
            log_weights()
            conv(1)
            softplus()
            turn(0)
            turn(1)
            power(0)
            turn(2)
            power(1)
            turn(3)
            recurrence(0)
            turn(4)
            recurrence(1)
            turn(5)
            lr_normalise(0)
            lr_normalise(1)
            turn(6)
            turn(7)
            sum_squares(TURNS - 1)
            dve.wait_ge(cb_std_ready, 1)
            dve.reciprocal(cb_rstd[:, :], cb_rstd[:, :]).then_inc(cb_rstd_ready, 1)
            dve.wait_ge(cb_rstd_ready, 1)
            for t in range(S // P):
                if t >= 4:
                    dve.wait_ge(turned, t - 3)
                dve.tensor_scalar(o_n[:, t % 4, :], o_all[:, t, :], cb_rstd[:, t:t + 1], None, ALU.mult).then_inc(o_n_ready, 1)
                if t == 3:
                    lr_normalise(2)
                if t == 7:
                    lr_normalise(3)

        @block.gpsimd
        def _(pool):
            def weigh(i):
                pool.wait_ge(loaded[i % 2], 16 * PATS * (i // 2 + 1))
                for a in range(1 if i < FIRST_SHARED else 0, PATS):
                    pool.tensor_tensor(sums_of(i, a), sums_of(i, a), weight_of(i, a), ALU.mult).then_inc(weighted, 1)

            def gated_input(m):
                pool.wait_ge(gates_ready, 2 * BLOCKS * (m + 1))
                pool.tensor_tensor(i_x[:, m, :], i_x[:, m, :], xc[:, m, :], ALU.mult).then_inc(ix_ready, 1)

            def square(i):
                pool.wait_ge(step, STEPS * (i + 1))
                if i >= 2:
                    pool.wait_ge(summed, i - 1)
                o = o_all[:, 2 * i:2 * i + 2, :]
                pool.tensor_tensor(o_squares[:, i % 2, :, :], o, o, ALU.mult).then_inc(squared, 1)

            pool.wait_ge(weight_ready, 1)
            weigh(0)
            for i in range(1, TURNS):
                weigh(i)
                square(i - 1)
                if 1 <= i <= LT:
                    gated_input(i - 1)
            square(TURNS - 1)

        @block.scalar
        def _(act):
            act.wait_ge(lr_consts_in, 32)
            for m in range(LT):
                act.wait_ge(x_loaded[m], 16)
                act.activation(xc[:, m, :], x_in[:, m, LTAPS - 1:], ACT.Identity, bias=c[:, m, C_BIAS:C_BIAS + 1],
                               scale=c[:, m, LTAPS - 1:LTAPS]).then_inc(last_tap_ready, 1)
            act.activation(sp8[:, :, 0:1], c[:, :, C_LAM:C_LAM + 1], ACT.Abs).then_inc(small_act, 1)
            act.wait_ge(small_act, 1)
            act.activation(sp8[:, :, 0:1], sp8[:, :, 0:1], ACT.Exp, scale=-1.0).then_inc(small_act, 1)
            act.wait_ge(small_act, 2)
            act.activation(sp8[:, :, 1:2], sp8[:, :, 0:1], ACT.Ln, bias=1.0).then_inc(small_act, 1)
            act.wait_ge(prepared, 2 + PATS)
            act.activation(weight[:, :, :, :], weight[:, :, :, :], ACT.Exp).then_inc(weight_ready, 1)
            for m in range(LT):
                for s, (dst, bias) in enumerate(((r, C_BA), (i_x, C_BX))):
                    for b in range(BLOCKS):
                        n = (LT * m + s) * BLOCKS + b
                        act.wait_ge(gates_done, n + 1)
                        act.activation(dst[:, m, blk(b)], lr_banks[n % 2][:, :], ACT.Sigmoid,
                                       bias=c[:, m, bias:bias + 1]).then_inc(gates_ready, 1)
            act.wait_ge(small, 4)
            act.wait_ge(gates_ready, 4 * BLOCKS)
            for m in range(LT):
                act.activation(root[:, m, :], r[:, m, :], ACT.Tanh, scale=sp8[:, m, 2:3]).then_inc(tanh_ready, 1)
            for m in range(LT):
                act.wait_ge(tanh_ready, m + 1)
                act.activation(r[:, m, :], r[:, m, :], ACT.Exp, scale=sp8[:, m, 3:4]).then_inc(a_ready, 1)
                act.wait_ge(a_ready, m + 1)
                act.activation(a2[:, m, :], r[:, m, :], ACT.Square).then_inc(a2_ready, 1)
            act.wait_ge(gate_loaded, 16)
            for m in range(LT):
                act.activation(gate[:, m, :], gate[:, m, :], ACT.Gelu_apprx_tanh).then_inc(gelu_ready, 1)
            for m in range(LT):
                act.wait_ge(power_ready, m + 1)
                act.activation(root[:, m, :], root[:, m, :], ACT.Sqrt).then_inc(root_ready, 1)
            for m in range(LT):
                act.wait_ge(hg_ready, m + 1)
                act.activation(a2[:, m, :], xc[:, m, :], ACT.Square).then_inc(sq_ready, 1)
            for b in range(BLOCKS):
                act.wait_ge(sums_done, b + 1)
                act.activation(lr_rstd[:, blk(b)], lr_banks[b % 2][:, :], ACT.Sqrt, bias=eps[:, :], scale=1.0 / LW).then_inc(lr_std_ready, 1)
            act.wait_ge(summed, TURNS)
            act.activation(cb_rstd[:, :], ss[:, :], ACT.Sqrt, bias=eps[:, :], scale=1.0 / CW).then_inc(cb_std_ready, 1)
            act.wait_ge(cb_consts_in, 32)
            for b in range(BLOCKS):
                if b >= 2:
                    act.wait_ge(cb_stored[b % 2], 16 * (b // 2))
                act.wait_ge(turned, 4 * (b + 1))
                for g in range(GROUPS):
                    act.activation(out[:, b % 2, g, :], cb_banks[GROUPS * (b % 2) + g][:, :], ACT.Copy, scale=gain[:, g:g + 1]
                                   ).then_inc(cb_out_ready, 1)

        @block.tensor
        def _(pe):
            pe.wait_ge(lr_consts_in, 32)
            for m in range(LT):
                pe.wait_ge(conv_step, (LTAPS - 1) * (m + 1))
                for s in range(2):
                    for b in range(BLOCKS):
                        n = (LT * m + s) * BLOCKS + b
                        if n >= 2:
                            pe.wait_ge(gates_ready, n - 1)
                        pe.matmul(lr_banks[n % 2][:, :], w[:, m, s, :], xc[:, m, blk(b)], start=True, stop=True
                                  ).then_inc(gates_done, 1)
            pe.wait_ge(gates_ready, 4 * BLOCKS)
            pe.wait_ge(sq_ready, LT)
            for b in range(BLOCKS):
                if b >= 2:
                    pe.wait_ge(lr_std_ready, b - 1)
                for m in range(LT):
                    ins = pe.matmul(lr_banks[b % 2][:, :], ones[:, :], a2[:, m, blk(b)], start=(m == 0), stop=(m == LT - 1))
                ins.then_inc(sums_done, 1)
            pe.wait_ge(cb_consts_in, 32)
            for t in range(S // P):
                b = t // 4
                pe.wait_ge(o_n_ready, t + 1)
                if b >= 2 and t % 4 == 0:
                    pe.wait_ge(cb_out_ready, GROUPS * (b - 1))
                for g in range(GROUPS):
                    ins = pe.transpose(cb_banks[GROUPS * (b % 2) + g][:, (t % 4) * P:(t % 4 + 1) * P], o_n[:, t % 4, g * P:(g + 1) * P], idf[:, :])
                ins.then_inc(turned, 1)




def shape_constants():

    def bf16_bits(v):
        return (np.ascontiguousarray(v).view(np.uint32) >> 16).astype(np.uint16)

    rot = HD // 4
    inv = (np.float32(500000.0) ** (-np.arange(0, rot, 2, dtype=np.float32) / np.float32(rot))).astype(np.float32)
    angle = np.arange(S, dtype=np.float32)[None, :] * inv[:, None]
    rope = np.zeros((P, 2, S), np.float32)
    rope[:, 0] = 1.0
    rotate = np.zeros((P, P), np.float32)
    for head in range(2):
        lo = slice(head * HD, head * HD + rot // 2)
        hi = slice(head * HD + rot // 2, head * HD + rot)
        rope[lo, 0] = rope[hi, 0] = np.cos(angle)
        rope[lo, 1] = rope[hi, 1] = np.sin(angle)
        for d in range(rot // 2):
            rotate[hi.start + d, lo.start + d] = -1.0
            rotate[lo.start + d, hi.start + d] = 1.0
    q = np.arange(SPAN)[:, None]
    k = np.arange(SPAN)[None, :]
    masks = np.zeros((P, PAIRED, 2 * SPAN), np.float32)
    for j, (pat, r, b) in enumerate(attention_blocks()):
        if j < PAIRED:
            masks[:, j, :SPAN] = np.where((k >= q) & (b > 0), 0.0, -1e30)
            masks[:, j, SPAN:] = np.where(k <= q, 0.0, -1e30)
    ident = np.eye(P, dtype=np.float32)
    head_scales = np.zeros((P, 2), np.float32)
    for head in range(2):
        head_scales[head * HD:(head + 1) * HD, head] = HD ** -0.5
    return {"head_scales": head_scales, "rope": rope, "rotate": rotate, "masks": bf16_bits(masks), "ident": ident,
            "ident_bf": bf16_bits(ident)}
FFN = 2816
PAIRS = FFN // P
OUT_SLABS = KT // 2
HALVES = 2
HALF = S // HALVES
HB = HALF // NB
TAPS = 3


def output_projection(nc, mix_t, x_t, w_slabs, rstd, x2_t):
    with ExitStack() as ctx:
        used = []
        ctx.callback(free_semaphores, nc, used)

        def sb(name, shape, dt=F32):
            return ctx.enter_context(nc.sbuf_tensor("op_" + name, shape, dt))

        def sem(name):
            used.append(nc.alloc_semaphore("op_" + name))
            return used[-1]

        w_raw = sb("w_raw", [P, 2, KT, 2 * P])
        w_hi = sb("w_hi", [P, KT, D], F32R)
        w_lo = sb("w_lo", [P, KT, D], F32R)
        RING = 4
        mix_in = sb("mix_in", [P, RING, NB])
        mix_hi = sb("mix_hi", [P, 2, KT, NB], F32R)
        mix_lo = sb("mix_lo", [P, 2, KT, NB], F32R)
        x = sb("x", [P, 2, KT, NB])
        squares = sb("squares", [P, 2, NB])
        total = sb("total", [P, 2, NB])
        ones = sb("ones", [P, P])
        eps = sb("eps", [P, 1])
        banks = [ctx.enter_context(nc.psum_tensor(f"op_bank{i}", [P, NB], F32)) for i in range(4)]
        sum_bank = ctx.enter_context(nc.psum_tensor("op_sum_bank", [P, NB], F32))

        consts_ready = sem("consts_ready")
        w_loaded = [sem(f"w_loaded{i}") for i in range(2)]
        w_hi_ready = sem("w_hi_ready")
        w_ready = sem("w_ready")
        mix_loaded = [sem(f"mix_loaded{i}") for i in range(RING)]
        mix_hi_ready = sem("mix_hi_ready")
        mix_ready = sem("mix_ready")
        x_loaded = [sem(f"x_loaded{i}") for i in range(2)]
        product_done = sem("product_done")
        added = sem("added")
        square_ready = sem("square_ready")
        summed = sem("summed")
        sum_done = sem("sum_done")
        std_ready = sem("std_ready")
        rstd_ready = sem("rstd_ready")
        stored = [sem(f"stored{i}") for i in range(2)]

        block = ctx.enter_context(nc.Block())

        def blk(b):
            return slice(b * NB, (b + 1) * NB)

        @block.sync
        def _(sp):
            def load_weights(n):
                if n >= 2:
                    sp.wait_ge(w_ready, n - 1)
                sp.dma_start(w_raw[:, n % 2, :, :], w_slabs[n]).then_inc(w_loaded[n % 2], 16)

            def load_mix(b):
                for k in range(KT):
                    n = KT * b + k
                    if n == RING:
                        load_weights(1)
                    if n >= RING:
                        sp.wait_ge(mix_ready, n - RING + 1)
                    sp.dma_start(mix_in[:, n % RING, :], mix_t[k, :, blk(b)]).then_inc(mix_loaded[n % RING], 16)

            def load_x(b):
                if b >= 2:
                    sp.wait_ge(stored[b % 2], 16 * (b // 2))
                    sp.wait_ge(square_ready, KT * (b - 1))
                sp.dma_start(x[:, b % 2, :, :], x_t[:, :, blk(b)]).then_inc(x_loaded[b % 2], 16)

            load_weights(0)
            load_mix(0)
            load_weights(2)
            load_x(0)
            load_weights(3)
            load_x(1)
            for b in range(BLOCKS):
                if b + 1 < BLOCKS:
                    load_mix(b + 1)
                sp.wait_ge(added, KT * (b + 1))
                sp.dma_start(x2_t[:, :, blk(b)], x[:, b % 2, :, :]).then_inc(stored[b % 2], 16)
                if b + 2 < BLOCKS:
                    load_x(b + 2)
            for p in range(2):
                sp.wait_ge(stored[p], 16 * BLOCKS // 2)

        @block.scalar
        def _(act):
            def weights_high(n):
                act.wait_ge(w_loaded[n % 2], 16 * (n // 2 + 1))
                act.activation(w_hi[:, :, n * 2 * P:(n + 1) * 2 * P], w_raw[:, n % 2, :, :], ACT.Copy).then_inc(w_hi_ready, 1)

            def high(b):
                if b >= 2:
                    act.wait_ge(product_done, KT * (b - 1))
                for k in range(KT):
                    n = KT * b + k
                    act.wait_ge(mix_loaded[n % RING], 16 * (n // RING + 1))
                    act.activation(mix_hi[:, b % 2, k, :], mix_in[:, n % RING, :], ACT.Copy).then_inc(mix_hi_ready, 1)

            def square(b):
                for k in range(KT):
                    n = KT * b + k
                    act.wait_ge(added, n + 1)
                    if n >= 2:
                        act.wait_ge(summed, n - 1)
                    act.activation(squares[:, n % 2, :], x[:, b % 2, k, :], ACT.Square).then_inc(square_ready, 1)

            def root(b):
                act.wait_ge(sum_done, b + 1)
                act.activation(rstd[:, blk(b)], sum_bank[:, :], ACT.Sqrt, bias=eps[:, :], scale=1.0 / D).then_inc(std_ready, 1)

            weights_high(0)
            high(0)
            for n in range(1, OUT_SLABS):
                weights_high(n)
            act.wait_ge(consts_ready, 2)
            for b in range(BLOCKS):
                if b + 1 < BLOCKS:
                    high(b + 1)
                if b:
                    root(b - 1)
                square(b)
            root(BLOCKS - 1)

        @block.gpsimd
        def _(pool):
            for b in range(BLOCKS):
                for k in range(KT):
                    n = KT * b + k
                    pool.wait_ge(square_ready, n + 1)
                    if k:
                        pool.wait_ge(summed, n)
                        ins = pool.tensor_tensor(total[:, b % 2, :], total[:, b % 2, :], squares[:, n % 2, :], ALU.add)
                    else:
                        if b >= 2:
                            pool.wait_ge(sum_done, b - 1)
                        ins = pool.tensor_copy(total[:, b % 2, :], squares[:, n % 2, :])
                    ins.then_inc(summed, 1)

        @block.vector
        def _(dve):
            dve.memset(ones[:, :], 1.0).then_inc(consts_ready, 1)
            dve.memset(eps[:, :], EPS).then_inc(consts_ready, 1)

            def weights_low(n):
                dve.wait_ge(w_hi_ready, n + 1)
                at = slice(n * 2 * P, (n + 1) * 2 * P)
                dve.tensor_tensor(w_lo[:, :, at], w_raw[:, n % 2, :, :], w_hi[:, :, at].bitcast(F32), ALU.subtract).then_inc(w_ready, 1)

            def low(b, k):
                n = KT * b + k
                dve.wait_ge(mix_hi_ready, n + 1)
                dve.tensor_tensor(mix_lo[:, b % 2, k, :], mix_in[:, n % RING, :], mix_hi[:, b % 2, k, :].bitcast(F32),
                                  ALU.subtract).then_inc(mix_ready, 1)

            def invert(b):
                dve.wait_ge(std_ready, b + 1)
                dve.reciprocal(rstd[:, blk(b)], rstd[:, blk(b)]).then_inc(rstd_ready, 1)

            weights_low(0)
            for k in range(KT):
                low(0, k)
            for n in range(1, OUT_SLABS):
                weights_low(n)
            for b in range(BLOCKS):
                dve.wait_ge(x_loaded[b % 2], 16 * (b // 2 + 1))
                for m in range(KT):
                    n = KT * b + m
                    if b + 1 < BLOCKS:
                        low(b + 1, m)
                    dve.wait_ge(product_done, n + 1)
                    at = x[:, b % 2, m, :]
                    dve.tensor_tensor(at, banks[n % 4][:, :], at, ALU.add).then_inc(added, 1)
                    if b and m == KT // 2:
                        invert(b - 1)
            invert(BLOCKS - 1)
            dve.wait_ge(rstd_ready, BLOCKS)

        @block.tensor
        def _(pe):
            pe.wait_ge(consts_ready, 2)

            def sum_squares(b):
                pe.wait_ge(summed, KT * (b + 1))
                if b:
                    pe.wait_ge(std_ready, b)
                pe.matmul(sum_bank[:, :], ones[:, :], total[:, b % 2, :], start=True, stop=True).then_inc(sum_done, 1)

            for b in range(BLOCKS):
                if b:
                    pe.wait_ge(mix_ready, KT * (b + 1))
                for m in range(KT):
                    n = KT * b + m
                    if b == 0 and m % 2 == 0:
                        pe.wait_ge(w_ready, m // 2 + 1)
                    if n >= 4:
                        pe.wait_ge(added, n - 3)
                    cols = slice(m * P, (m + 1) * P)
                    product(pe, banks[n % 4][:, :],
                            [w_hi[:, k, cols] for k in range(KT)], [w_lo[:, k, cols] for k in range(KT)],
                            [mix_hi[:, b % 2, k, :] for k in range(KT)], [mix_lo[:, b % 2, k, :] for k in range(KT)],
                            (mix_ready,) if n == 0 else None).then_inc(product_done, 1)
                    if b and m == 2:
                        sum_squares(b - 1)
            sum_squares(BLOCKS - 1)


def conv_ffn(nc, x2_t, slabs, w_down, conv, gains, rstd, out_t):
    with ExitStack() as ctx:
        used = []
        ctx.callback(free_semaphores, nc, used)

        def sb(name, shape, dt=F32):
            return ctx.enter_context(nc.sbuf_tensor("ff_" + name, shape, dt))

        def sem(name):
            used.append(nc.alloc_semaphore("ff_" + name))
            return used[-1]

        h_hi = sb("h_hi", [P, KT, HALF], F32R)
        h_lo = sb("h_lo", [P, KT, HALF], F32R)
        x2 = sb("x2", [P, KT, HALF])
        up_raw = sb("up_raw", [P, KT, 2 * P])
        up_hi = sb("up_hi", [P, 2, KT, 2 * P], F32R)
        up_lo = sb("up_lo", [P, 2, KT, 2 * P], F32R)
        dn_raw = sb("dn_raw", [P, D])
        dn_hi = sb("dn_hi", [P, 2, D], F32R)
        dn_lo = sb("dn_lo", [P, 2, D], F32R)
        u = sb("u", [P, 2, TAPS - 1 + HALF])
        y = sb("y", [P, 2, HALF])
        a_hi = sb("a_hi", [P, 2, HALF], F32R)
        a_lo = sb("a_lo", [P, 2, HALF], F32R)
        halo = sb("halo", [P, 2, PAIRS, 2, TAPS - 1])
        conv_all = sb("conv_all", [P, PAIRS, 2, TAPS + 1])
        conv_now = sb("conv_now", [P, 2, 2, TAPS + 1])
        out_rstd = sb("out_rstd", [P, NB])
        squares = sb("squares", [P, 2, NB])
        gain = sb("gain", [P, 2, KT])
        ones = sb("ones", [P, P])
        eps = sb("eps", [P, 1])
        banks = [ctx.enter_context(nc.psum_tensor(f"ff_bank{i}", [P, NB], F32)) for i in range(8)]

        consts_in = sem("consts_in")
        gain_in = sem("gain_in")
        consts_ready = sem("consts_ready")
        halo_zeroed = sem("halo_zeroed")
        h_loaded = [[sem(f"h_loaded{b}{i}") for i in range(2)] for b in range(HB)]
        h_hi_ready = sem("h_hi_ready")
        h_even_ready = sem("h_even_ready")
        h_odd_ready = sem("h_odd_ready")
        x2_loaded = sem("x2_loaded")
        up_loaded = sem("up_loaded")
        up_scaled = sem("up_scaled")
        up_hi_ready = sem("up_hi_ready")
        up_ready = sem("up_ready")
        up_done = sem("up_done")
        moved = sem("moved")
        dn_loaded = sem("dn_loaded")
        dn_hi_ready = sem("dn_hi_ready")
        dn_ready = sem("dn_ready")
        dn_done = sem("dn_done")
        dn_added = sem("dn_added")
        square_ready = sem("square_ready")
        square_used = sem("square_used")
        std_ready = sem("std_ready")
        rstd_ready = sem("rstd_ready")
        halo_in = sem("halo_in")
        halo_out = sem("halo_out")
        conv_w_ready = sem("conv_w_ready")
        taps_ready = sem("taps_ready")
        conv_step = sem("conv_step")
        gelu_ready = sem("gelu_ready")
        gated_ready = sem("gated_ready")
        a_hi_ready = sem("a_hi_ready")
        a_ready = sem("a_ready")
        y_ready = sem("y_ready")
        stored = sem("stored")

        block = ctx.enter_context(nc.Block())
        DOWN = KT * HB
        ALL = HALVES * PAIRS

        def blk(b):
            return slice(b * NB, (b + 1) * NB)

        def in_half(half, b):
            return slice(half * HALF + b * NB, half * HALF + (b + 1) * NB)

        def turns(engine, body, half):
            first = half * PAIRS
            looped = (PAIRS - 2) // 2 - half
            with engine.Fori(0, looped) as i:
                body(2 * i + first, 0)
                body(2 * i + (first + 1), 1)
            for g in range(first + 2 * looped, first + PAIRS - 1):
                body(g, g % 2)

        def exists(g):
            return not isinstance(g, int) or g < ALL

        @block.sync
        def _(sp):
            def load_slab(g, e):
                if not isinstance(g, int) or g > 0:
                    sp.wait_ge(up_ready, g)
                sp.dma_start(up_raw[:, :, :], slabs[e + OUT_SLABS]).then_inc(up_loaded, 16)

            def load_down(g, e):
                if not isinstance(g, int) or g > 0:
                    sp.wait_ge(dn_ready, g)
                sp.dma_start(dn_raw[:, :], w_down[e]).then_inc(dn_loaded, 16)

            def load_h(half, b):
                if half:
                    sp.wait_ge(up_done, 4 * PAIRS - 4 + 2 * (b + 1))
                for i in range(2):
                    ks = slice(i * KT // 2, (i + 1) * KT // 2)
                    sp.dma_start(h_lo[:, ks, blk(b)].bitcast(F32), x2_t[:, ks, in_half(half, b)]).then_inc(h_loaded[b][i], 16)

            def load_x2(half):
                if half:
                    sp.wait_ge(stored, 16 * DOWN // 2)
                sp.dma_start(x2[:, :, :], x2_t[:, :, half * HALF:(half + 1) * HALF]).then_inc(x2_loaded, 16)

            def store(half):
                for m in range(0, DOWN, 2):
                    sp.wait_ge(y_ready, DOWN * half + m + 2)
                    k = m % KT
                    sp.dma_start(out_t[:, k:k + 2, in_half(half, m // KT)], x2[:, k:k + 2, blk(m // KT)]).then_inc(stored, 16)

            load_slab(0, 0)
            sp.dma_start(gain[:, :, :], gains).then_inc(gain_in, 16)
            load_h(0, 0)
            load_slab(1, 1)
            load_h(0, 1)
            sp.dma_start(conv_all[:, :, :, :], conv).then_inc(consts_in, 16)
            load_down(0, 0)
            load_x2(0)
            load_slab(2, 2)
            load_down(1, 1)
            with sp.Fori(0, PAIRS - 3) as i:
                load_slab(i + 3, i + 3)
                load_down(i + 2, i + 2)
            for g in range(PAIRS - 3, PAIRS - 1):
                load_slab(g + 3, g + 3 - PAIRS)
                load_down(g + 2, (g + 2) % PAIRS)
            for b in range(HB):
                load_h(1, b)
            load_slab(PAIRS + 2, 2)
            load_down(PAIRS + 1, 1)
            store(0)
            load_x2(1)
            with sp.Fori(0, PAIRS - 3) as i:
                load_slab(i + (PAIRS + 3), i + 3)
                load_down(i + (PAIRS + 2), i + 2)
            load_down(ALL - 1, PAIRS - 1)
            store(1)
            sp.wait_ge(stored, 16 * DOWN)

        @block.gpsimd
        def _(pool):
            pool.sem_inc(halo_out, 1)
            pool.memset(halo[:, 0], 0.0).then_inc(halo_zeroed, 1)
            pool.wait_ge(gain_in, 16)

            def scale_slab(g):
                pool.wait_ge(up_loaded, 16 * (g + 1))
                pool.tensor_tensor(up_raw[:, :, :], up_raw[:, :, :], gain[:, 0, :].unsqueeze(2).to_broadcast([P, KT, 2 * P]),
                                   ALU.mult).then_inc(up_scaled, 1)

            def low_even(half, b):
                for k in range(0, KT, 2):
                    pool.wait_ge(h_hi_ready, KT * (HB * half + b) + k + 1)
                    at = h_lo[:, k, blk(b)]
                    pool.tensor_tensor(at, at.bitcast(F32), h_hi[:, k, blk(b)].bitcast(F32), ALU.subtract).then_inc(h_even_ready, 1)

            def halo_of(half, e):
                return halo[:, half, bass.ds(e, 1), :, :].rearrange("p o a t -> p (o a) t")

            def take_halo(g, j, half):
                e = g - half * PAIRS
                pool.wait_ge(conv_step, 4 * g + 4)
                pool.wait_ge(halo_out, g + 1)
                pool.tensor_copy(conv_now[:, j, :, :], conv_all[:, bass.ds(e, 1), :, :].rearrange("p o a t -> p (o a) t")).then_inc(conv_w_ready, 1)
                pool.tensor_copy(u[:, :, 0:TAPS - 1], halo_of(half, e)).then_inc(halo_in, 1)

            def save_halo(g, half):
                if half == 0:
                    pool.wait_ge(moved, 4 * g + 8)
                    pool.tensor_copy(halo_of(1, g), u[:, :, HALF:HALF + TAPS - 1]).then_inc(halo_out, 1)
                else:
                    pool.sem_inc(halo_out, 1)

            scale_slab(0)
            low_even(0, 0)
            scale_slab(1)
            low_even(0, 1)
            pool.wait_ge(halo_zeroed, 1)
            pool.wait_ge(consts_in, 16)
            for half in range(HALVES):
                first = half * PAIRS
                take_halo(first, 0, half)
                scale_slab(first + 2)
                save_halo(first, half)

                def body(g, j):
                    take_halo(g + 1, 1 - j, half)
                    if exists(g + 3):
                        scale_slab(g + 3)
                    save_halo(g + 1, half)

                turns(pool, body, half)
                if half + 1 < HALVES:
                    for b in range(HB):
                        low_even(half + 1, b)

        @block.scalar
        def _(act):
            def slab_high(g, p):
                act.wait_ge(up_scaled, g + 1)
                if not isinstance(g, int) or g >= 2:
                    act.wait_ge(up_done, 4 * g - 4)
                act.activation(up_hi[:, p, :, :], up_raw[:, :, :], ACT.Copy).then_inc(up_hi_ready, 1)

            def down_high(g, p):
                act.wait_ge(dn_loaded, 16 * (g + 1))
                if not isinstance(g, int) or g >= 2:
                    act.wait_ge(dn_done, DOWN * g - DOWN)
                act.activation(dn_hi[:, p, :], dn_raw[:, :], ACT.Copy).then_inc(dn_hi_ready, 1)

            def split_h(half, b):
                for k in range(KT):
                    if k % (KT // 2) == 0:
                        act.wait_ge(h_loaded[b][k // (KT // 2)], 16 * (half + 1))
                    act.activation(h_hi[:, k, blk(b)], h_lo[:, k, blk(b)].bitcast(F32), ACT.Copy).then_inc(h_hi_ready, 1)

            def taps(g, j):
                act.wait_ge(moved, 4 * g + 8)
                act.wait_ge(a_ready, g + 1)
                act.wait_ge(conv_w_ready, g + 1)
                for a in (1, 0):
                    act.activation(y[:, a, :], u[:, a, TAPS - 1:], ACT.Identity, bias=conv_now[:, j, a, TAPS:TAPS + 1],
                                   scale=conv_now[:, j, a, TAPS - 1:TAPS]).then_inc(taps_ready, 1)

            def gate(g, p):
                act.wait_ge(conv_step, 4 * g + 8)
                act.activation(y[:, 1, :], y[:, 1, :], ACT.Gelu_apprx_tanh).then_inc(gelu_ready, 1)
                act.wait_ge(gated_ready, g + 1)
                if not isinstance(g, int) or g >= 2:
                    act.wait_ge(dn_done, DOWN * g - DOWN)
                act.activation(a_hi[:, p, :], y[:, 0, :], ACT.Copy).then_inc(a_hi_ready, 1)

            def final_roots(half):
                for b in range(HB):
                    for k in range(KT):
                        n = DOWN * half + KT * b + k
                        act.wait_ge(dn_added, 4 + DOWN * (PAIRS * (half + 1) - 1) + KT * b + k + 1)
                        if n >= 2:
                            act.wait_ge(square_used, n - 1)
                        act.activation(squares[:, n % 2, :], x2[:, k, blk(b)], ACT.Square).then_inc(square_ready, 1)
                    n = DOWN * half + KT * b
                    act.wait_ge(square_used, n + KT)
                    if n:
                        act.wait_ge(y_ready, n)
                    act.activation(out_rstd[:, :], banks[2 + b][:, :], ACT.Sqrt, bias=eps[:, :], scale=1.0 / D).then_inc(std_ready, 1)

            slab_high(0, 0)
            split_h(0, 0)
            slab_high(1, 1)
            split_h(0, 1)
            down_high(0, 0)
            act.wait_ge(consts_ready, 2)
            for half in range(HALVES):
                first = half * PAIRS
                taps(first, 0)
                slab_high(first + 2, 0)
                gate(first, 0)
                down_high(first + 1, 1)

                def body(g, j):
                    taps(g + 1, 1 - j)
                    if exists(g + 3):
                        slab_high(g + 3, 1 - j)
                    gate(g + 1, 1 - j)
                    if exists(g + 2):
                        down_high(g + 2, j)

                turns(act, body, half)
                if half + 1 < HALVES:
                    for b in range(HB):
                        split_h(half + 1, b)
                final_roots(half)

        @block.vector
        def _(dve):
            dve.sem_inc(moved, 4)
            dve.sem_inc(dn_added, 4)
            dve.sem_inc(conv_step, 4)
            dve.sem_inc(a_ready, 1)
            dve.memset(ones[:, :], 1.0).then_inc(consts_ready, 1)
            dve.memset(eps[:, :], EPS).then_inc(consts_ready, 1)

            def slab_low(g, p):
                dve.wait_ge(up_hi_ready, g + 1)
                dve.tensor_tensor(up_lo[:, p, :, :], up_raw[:, :, :], up_hi[:, p, :, :].bitcast(F32),
                                  ALU.subtract).then_inc(up_ready, 1)

            def down_low(g, p):
                dve.wait_ge(dn_hi_ready, g + 1)
                dve.tensor_tensor(dn_lo[:, p, :], dn_raw[:, :], dn_hi[:, p, :].bitcast(F32), ALU.subtract).then_inc(dn_ready, 1)

            def low_odd(half, b):
                for k in range(1, KT, 2):
                    dve.wait_ge(h_hi_ready, KT * (HB * half + b) + k + 1)
                    at = h_lo[:, k, blk(b)]
                    dve.tensor_tensor(at, at.bitcast(F32), h_hi[:, k, blk(b)].bitcast(F32), ALU.subtract).then_inc(h_odd_ready, 1)

            def to_u(g, half):
                dve.wait_ge(conv_step, 4 * g + 4)
                dve.wait_ge(halo_out, g + 1)
                for q in range(4):
                    b, a = q // 2, q % 2
                    dve.wait_ge(up_done, 4 * g + (q + 1))
                    dve.tensor_tensor(u[:, a, TAPS - 1 + b * NB:TAPS - 1 + (b + 1) * NB], banks[q][:, :],
                                      rstd[:, in_half(half, b)], ALU.mult).then_inc(moved, 1)

            def convolve(g, j):
                dve.wait_ge(taps_ready, 2 * g + 2)
                dve.wait_ge(halo_in, g + 1)
                dve.wait_ge(moved, 4 * g + 8)
                for s, (tap, a) in enumerate([(1, 1), (1, 0), (0, 1), (0, 0)]):
                    if tap == 0:
                        dve.wait_ge(conv_step, 4 * g + (4 + s - 1))
                    dve.scalar_tensor_tensor(out=y[:, a, :], in0=u[:, a, tap:tap + HALF], scalar=conv_now[:, j, a, tap:tap + 1],
                                             in1=y[:, a, :], op0=ALU.mult, op1=ALU.add).then_inc(conv_step, 1)

            def gated(g):
                dve.wait_ge(gelu_ready, g + 1)
                dve.wait_ge(conv_step, 4 * g + 8)
                dve.tensor_tensor(y[:, 0, :], y[:, 0, :], y[:, 1, :], ALU.mult).then_inc(gated_ready, 1)

            def act_low(g, p):
                dve.wait_ge(a_hi_ready, g + 1)
                dve.tensor_tensor(a_lo[:, p, :], y[:, 0, :], a_hi[:, p, :].bitcast(F32), ALU.subtract).then_inc(a_ready, 1)

            def add_down(g, first=0, last=DOWN):
                dve.wait_ge(dn_added, DOWN * g + 4)
                for m in range(first, last):
                    dve.wait_ge(dn_done, DOWN * g + (m + 1))
                    at = x2[:, m % KT, blk(m // KT)]
                    dve.tensor_tensor(at, banks[4 + m % 4][:, :], at, ALU.add).then_inc(dn_added, 1)

            def normalise(half, b):
                dve.wait_ge(std_ready, half * HB + b + 1)
                dve.reciprocal(out_rstd[:, :], out_rstd[:, :]).then_inc(rstd_ready, 1)
                dve.wait_ge(rstd_ready, half * HB + b + 1)
                for k in range(KT):
                    at = x2[:, k, blk(b)]
                    dve.scalar_tensor_tensor(out=at, in0=at, scalar=gain[:, 1, k:k + 1], in1=out_rstd[:, :],
                                             op0=ALU.mult, op1=ALU.mult).then_inc(y_ready, 1)

            slab_low(0, 0)
            low_odd(0, 0)
            slab_low(1, 1)
            low_odd(0, 1)
            down_low(0, 0)
            for half in range(HALVES):
                first = half * PAIRS
                to_u(first, half)
                convolve(first, 0)
                slab_low(first + 2, 0)
                gated(first)
                act_low(first, 0)
                down_low(first + 1, 1)
                dve.wait_ge(x2_loaded, 16 * (half + 1))

                def body(g, j):
                    to_u(g + 1, half)
                    if isinstance(g, int) and g == first + PAIRS - 2:
                        convolve(g + 1, 1 - j)
                        add_down(g, 0, 4)
                        gated(g + 1)
                        add_down(g, 4, 8)
                        act_low(g + 1, 1 - j)
                        add_down(g, 8, DOWN)
                        if exists(g + 3):
                            slab_low(g + 3, 1 - j)
                        if exists(g + 2):
                            down_low(g + 2, j)
                        return
                    add_down(g)
                    convolve(g + 1, 1 - j)
                    if exists(g + 3):
                        slab_low(g + 3, 1 - j)
                    gated(g + 1)
                    act_low(g + 1, 1 - j)
                    if exists(g + 2):
                        down_low(g + 2, j)

                turns(dve, body, half)
                if half + 1 < HALVES:
                    for b in range(HB):
                        low_odd(half + 1, b)
                add_down(first + PAIRS - 1)
                if half == 0:
                    dve.wait_ge(gain_in, 16)
                dve.wait_ge(dn_added, 4 + DOWN * PAIRS * (half + 1))
                for b in range(HB):
                    normalise(half, b)

        @block.tensor
        def _(pe):
            pe.wait_ge(consts_ready, 2)

            def up(g, p, half_start=None):
                pe.wait_ge(up_ready, g + 1)
                for q in range(4):
                    b, a = q // 2, q % 2
                    k_ready = None
                    if half_start == 0 and q == 0:
                        k_ready = (h_even_ready, h_odd_ready)
                    elif half_start is not None and a == 0:
                        pe.wait_ge(h_even_ready, KT // 2 * (HB * half_start + b + 1))
                        pe.wait_ge(h_odd_ready, KT // 2 * (HB * half_start + b + 1))
                        if half_start:
                            if b:
                                pe.wait_ge(std_ready, HB * half_start)
                    pe.wait_ge(moved, 4 * g + (q + 1))
                    product(pe, banks[q][:, :],
                            [up_hi[:, p, k, a * P:(a + 1) * P] for k in range(KT)],
                            [up_lo[:, p, k, a * P:(a + 1) * P] for k in range(KT)],
                            [h_hi[:, k, blk(b)] for k in range(KT)],
                            [h_lo[:, k, blk(b)] for k in range(KT)], k_ready).then_inc(up_done, 1)

            def down(g, p, last_of=None):
                pe.wait_ge(dn_ready, g + 1)
                pe.wait_ge(a_ready, g + 2)
                if last_of is not None:
                    pe.wait_ge(moved, 4 * g + 8)
                lag = 10 if last_of == 0 else 3
                for m in range(DOWN):
                    pe.wait_ge(dn_added, DOWN * g + (m + 1))
                    b, k = m // KT, m % KT
                    oc = slice(k * P, (k + 1) * P)
                    product(pe, banks[4 + m % 4][:, :], [dn_hi[:, p, oc]], [dn_lo[:, p, oc]],
                            [a_hi[:, p, blk(b)]], [a_lo[:, p, blk(b)]]).then_inc(dn_done, 1)
                    if last_of is not None and m >= lag:
                        sum_square(last_of, m - lag)
                if last_of is not None:
                    for m in range(DOWN - lag, DOWN):
                        sum_square(last_of, m)

            def sum_square(half, m):
                k = m % KT
                pe.wait_ge(square_ready, DOWN * half + m + 1)
                pe.matmul(banks[2 + m // KT][:, :], ones[:, :], squares[:, m % 2, :], start=(k == 0),
                          stop=(k == KT - 1)).then_inc(square_used, 1)

            for half in range(HALVES):
                first = half * PAIRS
                up(first, 0, half)

                def body(g, j):
                    up(g + 1, 1 - j)
                    down(g, j)

                turns(pe, body, half)
                down(first + PAIRS - 1, 1, half)




def mixer_constants():
    starts = np.ones((P, NB), np.float32)
    starts[:, ::CH] = 0.0
    j = np.arange(P)[:, None]
    i = np.arange(CH)[None, :]
    return {"starts": starts, "causal": np.ascontiguousarray(np.broadcast_to((i >= j)[:, None, :], (P, 2, CH))).astype(np.uint32)}


def program(nc, t, out_t):
    proj_t = nc.dram_tensor("proj_t", [TILES, P, S], F32, kind="Internal").ap()
    o_scratch = nc.dram_tensor("o_scratch", [len(DILATIONS), S, ROW], F32, kind="Internal").ap()
    mix_t = nc.dram_tensor("mix_t", [KT, P, S], F32, kind="Internal").ap()
    input_projection(nc, t["x_t"], t["norm_mix"], t["w_in"], proj_t)
    dilated_attention(nc, proj_t, t["rope"], t["rotate"], t["masks"].bitcast(BF16), t["ident"], t["ident_bf"].bitcast(BF16), t["head_scales"], o_scratch)
    gated_linear_attention(nc, proj_t, t["gla_w_gate"], t["gla_b_gate"], t["starts"], t["causal"], t["ident"], t["gla_norm"], mix_t)
    recurrent_and_patterns(nc, proj_t, t["lru"], t["lru_w"], o_scratch, t["ident"], t["swa_norm"], mix_t)
    x2_t = nc.dram_tensor("x2_t", [P, KT, S], F32, kind="Internal").ap()
    with ExitStack() as ctx:
        rstd = ctx.enter_context(nc.sbuf_tensor("ffn_rstd", [P, S], F32))
        output_projection(nc, mix_t, t["x_t"], t["slabs"], rstd, x2_t)
        conv_ffn(nc, x2_t, t["slabs"], t["w_down"], t["conv"], t["gains"], rstd, out_t)


def pad_heads(w):
    out = np.zeros(w.shape[:-1] + (GP * P,), np.float32)
    for h in range(GH):
        out[..., h * 64:h * 64 + DK] = w[..., h * DK:(h + 1) * DK]
    return out


def kernel(**inputs):
    import concourse.bacc as bacc
    from concourse.bass_utils import run_bass_kernel_spmd as run

    a = {k: np.asarray(v) for k, v in inputs.items()}
    flat = np.ascontiguousarray

    def per_channel(v):
        return flat(v.reshape(-1, P).T)

    arrays = {"x_t": flat(a["x"][0].T.reshape(KT, P, S).transpose(1, 0, 2)), "norm_mix": per_channel(a["norm_mix"][0])}
    sizes = (GH * DK, GH * DK, AW, AW, RANK, LW, LW, HEADS * HD, HEADS * HD, HEADS * HD)
    aq, ak, av, ar, glr, bg, bi, cq, ck, cv = np.split(a["w_in"][0], np.cumsum(sizes)[:-1], axis=1)
    aq = pad_heads(aq)
    aq[:, GLR_ROW:GLR_ROW + RANK] = glr
    w = np.concatenate([aq, pad_heads(ak), av, ar, bg, bi, cq, ck, cv], axis=1)
    arrays["w_in"] = flat(w.reshape(KT, P, TILES, P).transpose(2, 1, 0, 3))
    arrays["gla_w_gate"] = flat(pad_heads(a["gla_w_gate"][0]).reshape(RANK, GP, P))
    arrays["gla_b_gate"] = per_channel(pad_heads(a["gla_b_gate"][0]))
    arrays["gla_norm"] = per_channel(np.tile(a["gla_norm"][0], GH))
    per = [a["lru_conv_w"][0][t] for t in range(LTAPS)] + [a[n][0] for n in ("lru_conv_b", "lru_b_a", "lru_b_x", "lru_lambda", "lru_norm")]
    arrays["lru"] = flat(np.stack(per).reshape(C_NORM + 1, LT, P).transpose(2, 1, 0))
    lru_w = np.zeros((P, LT, 2, P), np.float32)
    bs = a["lru_w_a"].shape[-1]
    for s, name in enumerate(("lru_w_a", "lru_w_x")):
        for n in range(LW // bs):
            at = n * bs % P
            lru_w[at:at + bs, n * bs // P, s, at:at + bs] = a[name][0, n]
    arrays["lru_w"] = lru_w
    arrays["swa_norm"] = per_channel(a["swa_norm"][0])
    w_out_slabs = a["w_out"][0].reshape(KT, P, OUT_SLABS, 2 * P).transpose(2, 1, 0, 3)
    w_up_slabs = a["ffn_w_up"][0].reshape(KT, P, 2, PAIRS, P).transpose(3, 1, 0, 2, 4).reshape(PAIRS, P, KT, 2 * P)
    arrays["slabs"] = np.concatenate([w_out_slabs, w_up_slabs])
    arrays["w_down"] = flat(a["ffn_w_down"][0].reshape(PAIRS, P, D))
    conv = np.concatenate([a["ffn_conv_w"][0], a["ffn_conv_b"]])
    arrays["conv"] = flat(conv.reshape(TAPS + 1, 2, PAIRS, P).transpose(3, 2, 1, 0))
    arrays["gains"] = flat(np.stack([per_channel(a["norm_ffn"][0]), per_channel(a["norm_final"])], axis=1))
    arrays.update(shape_constants())
    arrays.update(mixer_constants())

    nc = bacc.Bacc("TRN2", target_bir_lowering=False, num_devices=1)
    tensors = {k: nc.dram_tensor("in_" + k, v.shape, mybir.dt.from_np(v.dtype), kind="ExternalInput").ap() for k, v in arrays.items()}
    out_t = nc.dram_tensor("out_t", [P, KT, S], F32, kind="ExternalOutput").ap()
    program(nc, tensors, out_t)
    r = run(nc, [{"in_" + k: v for k, v in arrays.items()}], core_ids=[0])
    return flat(r.results[0]["out_t"].transpose(2, 1, 0).reshape(1, S, D))
```
